# Optimizing a Trainium2 kernel written in Bass

```python
import math
import jax, jax.numpy as jnp
from jax import lax
import numpy as np

D_MODEL = 1024
BATCH = 1
SEQ = 256
DEPTH = 2

N_META = 16
MIX_WIDTH = D_MODEL
DIFF_WIDTH = MIX_WIDTH // 2
FOX_WIDTH = MIX_WIDTH - DIFF_WIDTH
DIFF_QK_DIM = 64
DIFF_V_DIM = 2 * DIFF_QK_DIM
DIFF_HEADS = DIFF_WIDTH // DIFF_V_DIM
FOX_HEAD_DIM = 64
FOX_HEADS = FOX_WIDTH // FOX_HEAD_DIM
ROPE_THETA = 10000.0
Q_BLOCK = 128
NORM_EPS = 1e-6
SPLITS = (DIFF_HEADS * 2 * DIFF_QK_DIM, DIFF_HEADS * 2 * DIFF_QK_DIM, DIFF_WIDTH, DIFF_WIDTH,
          FOX_WIDTH, FOX_WIDTH, FOX_WIDTH, FOX_WIDTH, FOX_HEADS)
PROJ_WIDTH = sum(SPLITS)


def rms_norm(x, g):
    xf = x.astype(jnp.float32)
    y = xf * lax.rsqrt(jnp.mean(xf * xf, axis=-1, keepdims=True) + NORM_EPS)
    return (y * g.astype(jnp.float32)).astype(x.dtype)

def rope(t, pos):
    half = t.shape[-1] // 2
    inv = ROPE_THETA ** (-jnp.arange(half, dtype=jnp.float32) / half)
    ang = pos.astype(jnp.float32)[:, None] * inv[None, :]
    cos, sin = jnp.cos(ang), jnp.sin(ang)
    tf = t.astype(jnp.float32)
    t1, t2 = tf[..., :half], tf[..., half:]
    return jnp.concatenate([t1 * cos - t2 * sin, t2 * cos + t1 * sin], axis=-1).astype(t.dtype)

def sweep_query_blocks(block_fn, q_parts, pos):
    meta_out = block_fn(tuple(q[:, :, :N_META] for q in q_parts), pos[:N_META])

    def to_blocks(q):
        b, h, _, d = q.shape
        return jnp.moveaxis(q[:, :, N_META:].reshape(b, h, -1, Q_BLOCK, d), 2, 0)

    blocks = tuple(to_blocks(q) for q in q_parts)
    pos_blocks = pos[N_META:].reshape(-1, Q_BLOCK)
    outs = lax.map(lambda a: block_fn(a[0], a[1]), (blocks, pos_blocks))
    nb, b, h, t, dv = outs.shape
    real = jnp.moveaxis(outs, 0, 2).reshape(b, h, nb * t, dv)
    return jnp.concatenate([meta_out, real], axis=2)

def hybrid_layer(h, pos, norm_g, w_in, b_forget, lam_q1, lam_k1, lam_q2, lam_k2,
                 subln_g, w_out, lambda_init):
    bsz, length, _ = h.shape
    u = rms_norm(h, norm_g)
    proj = jnp.einsum('bld,dp->blp', u, w_in)
    split_points = np.cumsum(SPLITS)[:-1].tolist()
    dq, dk, dv, dz, fq, fk, fv, fz, f_logit = jnp.split(proj, split_points, axis=-1)

    def diff_qk(t):
        t = t.reshape(bsz, length, DIFF_HEADS, 2, DIFF_QK_DIM).transpose(3, 0, 2, 1, 4)
        return rope(t[0], pos), rope(t[1], pos)

    q1, q2 = diff_qk(dq)
    k1, k2 = diff_qk(dk)
    v_a = dv.reshape(bsz, length, DIFF_HEADS, DIFF_V_DIM).transpose(0, 2, 1, 3)
    lam = (jnp.exp(jnp.sum(lam_q1.astype(jnp.float32) * lam_k1.astype(jnp.float32)))
           - jnp.exp(jnp.sum(lam_q2.astype(jnp.float32) * lam_k2.astype(jnp.float32)))
           + lambda_init)
    d_scale = DIFF_QK_DIM ** -0.5

    def diff_block(qs, qpos):
        qa, qc = qs
        mask = pos[None, :] <= qpos[:, None]

        def probs(q, k):
            s = jnp.einsum('bhqd,bhkd->bhqk', q, k).astype(jnp.float32) * d_scale
            return jax.nn.softmax(jnp.where(mask, s, -jnp.inf), axis=-1)

        p = probs(qa, k1) - lam * probs(qc, k2)
        return jnp.einsum('bhqk,bhkd->bhqd', p.astype(v_a.dtype), v_a)

    o_a = sweep_query_blocks(diff_block, (q1, q2), pos)
    o_a = rms_norm(o_a, subln_g.reshape(DIFF_HEADS, 1, DIFF_V_DIM)) * (1.0 - lambda_init)
    o_a = o_a.transpose(0, 2, 1, 3).reshape(bsz, length, DIFF_WIDTH)

    def fox_heads(t):
        return t.reshape(bsz, length, FOX_HEADS, FOX_HEAD_DIM).transpose(0, 2, 1, 3)

    q_f, k_f, v_f = fox_heads(fq), fox_heads(fk), fox_heads(fv)
    log_f = jax.nn.log_sigmoid(f_logit.astype(jnp.float32) + b_forget.astype(jnp.float32))
    cum = jnp.cumsum(log_f, axis=1).transpose(0, 2, 1)
    f_scale = FOX_HEAD_DIM ** -0.5

    def fox_block(qs, qpos):
        q, c_q = qs
        mask = pos[None, :] <= qpos[:, None]
        s = (jnp.einsum('bhqd,bhkd->bhqk', q, k_f).astype(jnp.float32) * f_scale
             + c_q - cum[:, :, None, :])
        p = jax.nn.softmax(jnp.where(mask, s, -jnp.inf), axis=-1)
        return jnp.einsum('bhqk,bhkd->bhqd', p.astype(v_f.dtype), v_f)

    o_b = sweep_query_blocks(fox_block, (q_f, cum[..., None]), pos)
    o_b = o_b.transpose(0, 2, 1, 3).reshape(bsz, length, FOX_WIDTH)

    mixed = jnp.concatenate([o_a * jax.nn.silu(dz), o_b * jax.nn.silu(fz)], axis=-1)
    return h + jnp.einsum('blm,md->bld', mixed, w_out)

def first_inputs(seed: int = 0) -> dict:
    key = jax.random.key(seed)
    ks = jax.random.split(key, 14)
    f32 = jnp.float32
    x = jax.random.normal(ks[0], (BATCH, SEQ, D_MODEL), f32)
    meta_tokens = jax.random.normal(ks[1], (N_META, D_MODEL), f32)
    norm_g = 1.0 + 0.02 * jax.random.normal(ks[2], (DEPTH, D_MODEL), f32)
    w_in = jax.random.normal(ks[3], (DEPTH, D_MODEL, PROJ_WIDTH), f32) * D_MODEL ** -0.5
    b_forget = (jnp.linspace(1.0, 6.0, FOX_HEADS, dtype=f32)[None, :]
                + 0.1 * jax.random.normal(ks[4], (DEPTH, FOX_HEADS), f32))
    lam_q1 = 0.1 * jax.random.normal(ks[5], (DEPTH, DIFF_QK_DIM), f32)
    lam_k1 = 0.1 * jax.random.normal(ks[6], (DEPTH, DIFF_QK_DIM), f32)
    lam_q2 = 0.1 * jax.random.normal(ks[7], (DEPTH, DIFF_QK_DIM), f32)
    lam_k2 = 0.1 * jax.random.normal(ks[8], (DEPTH, DIFF_QK_DIM), f32)
    subln_g = 1.0 + 0.02 * jax.random.normal(ks[9], (DEPTH, DIFF_WIDTH), f32)
    w_out = jax.random.normal(ks[10], (DEPTH, MIX_WIDTH, D_MODEL), f32) * MIX_WIDTH ** -0.5
    final_g = 1.0 + 0.02 * jax.random.normal(ks[11], (D_MODEL,), f32)
    return {'x': x, 'meta_tokens': meta_tokens, 'norm_g': norm_g, 'w_in': w_in,
            'b_forget': b_forget, 'lam_q1': lam_q1, 'lam_k1': lam_k1, 'lam_q2': lam_q2,
            'lam_k2': lam_k2, 'subln_g': subln_g, 'w_out': w_out, 'final_g': final_g}

def first_block(x, meta_tokens, norm_g, w_in, b_forget, lam_q1, lam_k1, lam_q2, lam_k2,
              subln_g, w_out, final_g):
    bsz, _, dm = x.shape
    meta = jnp.broadcast_to(meta_tokens.astype(x.dtype)[None], (bsz, N_META, dm))
    h = jnp.concatenate([meta, x], axis=1)
    pos = jnp.arange(h.shape[1], dtype=jnp.int32)
    for layer in range(DEPTH):
        lambda_init = 0.8 - 0.6 * math.exp(-0.3 * layer)
        h = hybrid_layer(h, pos, norm_g[layer], w_in[layer], b_forget[layer],
                         lam_q1[layer], lam_k1[layer], lam_q2[layer], lam_k2[layer],
                         subln_g[layer], w_out[layer], lambda_init)
    return rms_norm(h, final_g)[:, N_META:]


CHUNK = 64
D_POOL = D_MODEL // 4
POOL_WINDOWS = (2, 4, 8, 16)
N_POOL_GROUPS = len(POOL_WINDOWS)
POOL_GROUP = D_POOL // N_POOL_GROUPS
D_GMLP = 3 * D_MODEL // 8
GMLP_HEADS = 4
GMLP_HEAD_DIM = D_GMLP // GMLP_HEADS
GMLP_BLOCK = 128
D_CONV = D_MODEL - D_POOL - D_GMLP
CONV_WIDTH = 31
D_MIX = D_POOL + D_GMLP + D_CONV
D_IN = D_POOL + 2 * D_GMLP + 2 * D_CONV
D_FF = 2816
N_EXPERTS = 8
TOP_K = 2
D_FF_EXPERT = 3584
N_DENSE = (DEPTH + 1) // 2
N_MOE = DEPTH // 2
EPS = 1e-6


def rms_norm_2(x, g):
    xf = x.astype(jnp.float32)
    y = xf * lax.rsqrt(jnp.mean(xf * xf, axis=-1, keepdims=True) + EPS)
    return (y * g.astype(jnp.float32)).astype(x.dtype)

def layer_norm(x, g, b):
    xf = x.astype(jnp.float32)
    mu = jnp.mean(xf, axis=-1, keepdims=True)
    var = jnp.mean(jnp.square(xf - mu), axis=-1, keepdims=True)
    y = (xf - mu) * lax.rsqrt(var + EPS)
    return (y * g.astype(jnp.float32) + b.astype(jnp.float32)).astype(x.dtype)

def pool_mixer(a, w, scale):
    B, S, _ = a.shape
    af = a.astype(jnp.float32)
    csum = jnp.cumsum(af, axis=1)
    t = jnp.arange(1, S + 1, dtype=jnp.float32)
    outs = []
    for gi, win in enumerate(POOL_WINDOWS):
        sl = slice(gi * POOL_GROUP, (gi + 1) * POOL_GROUP)
        c = csum[..., sl]
        c_prev = jnp.pad(c[:, :-win], ((0, 0), (win, 0), (0, 0)))
        mean = (c - c_prev) / jnp.minimum(t, float(win))[None, :, None]
        outs.append(mean - af[..., sl])
    y = jnp.stack(outs, axis=2).astype(a.dtype)
    y = jnp.einsum('bsgc,gcd->bsgd', y, w).reshape(B, S, D_POOL)
    return y * scale

def gmlp_mixer(u, v, g, ws, b):
    B, S, _ = u.shape
    v = rms_norm_2(v, g)
    n_blk = S // GMLP_BLOCK
    vb = v.reshape(B, n_blk, GMLP_BLOCK, GMLP_HEADS, GMLP_HEAD_DIM)
    ci = jnp.arange(GMLP_BLOCK) // CHUNK
    mask = ci[:, None] >= ci[None, :]
    ws_m = jnp.where(mask[None], ws, jnp.zeros_like(ws))
    z = jnp.einsum('hij,bnjhc->bnihc', ws_m, vb) + b.T[None, None, :, :, None]
    return u * z.reshape(B, S, D_GMLP)

def conv_module(val, gate, w_dw, b_dw, ln_g, ln_b, w_pw, b_pw):
    h = val * jax.nn.sigmoid(gate)
    h = lax.conv_general_dilated(
        h, w_dw[:, None, :], window_strides=(1,),
        padding=((CONV_WIDTH - 1, 0),),
        dimension_numbers=('NWC', 'WIO', 'NWC'),
        feature_group_count=D_CONV) + b_dw
    h = jax.nn.silu(layer_norm(h, ln_g, ln_b))
    return h @ w_pw + b_pw

def swiglu(h, wg, wu, wd):
    return (jax.nn.silu(h @ wg) * (h @ wu)) @ wd

def moe_swiglu(h, router, wg, wu, wd):
    B, S, D = h.shape
    t = h.reshape(B * S, D)
    logits = t.astype(jnp.float32) @ router.astype(jnp.float32)
    top_v, top_i = lax.top_k(logits, TOP_K)
    top_w = jax.nn.softmax(top_v, axis=-1)
    gates = jnp.sum(jax.nn.one_hot(top_i, N_EXPERTS, dtype=jnp.float32)
                    * top_w[..., None], axis=1)
    out = jnp.zeros_like(t)
    for e in range(N_EXPERTS):
        out = out + gates[:, e:e + 1].astype(t.dtype) * swiglu(t, wg[e], wu[e], wd[e])
    return out.reshape(B, S, D)

def second_inputs(seed: int = 0) -> dict:
    key = jax.random.key(seed)
    k = jax.random.split(key, 26)
    f32 = jnp.float32
    nrm = lambda kk, shape, s: jax.random.normal(kk, shape, f32) * s
    return {
        "x": nrm(k[0], (BATCH, SEQ, D_MODEL), 1.0),
        "norm1_g": 1.0 + nrm(k[1], (DEPTH, D_MODEL), 0.05),
        "w_in": nrm(k[2], (DEPTH, D_MODEL, D_IN), D_MODEL ** -0.5),
        "pool_w": nrm(k[3], (DEPTH, N_POOL_GROUPS, POOL_GROUP, POOL_GROUP), POOL_GROUP ** -0.5),
        "pool_scale": 1.0 + nrm(k[4], (DEPTH, D_POOL), 0.1),
        "gm_norm_g": 1.0 + nrm(k[5], (DEPTH, D_GMLP), 0.05),
        "gm_ws": nrm(k[6], (DEPTH, GMLP_HEADS, GMLP_BLOCK, GMLP_BLOCK), 0.5 * GMLP_BLOCK ** -0.5),
        "gm_b": 1.0 + nrm(k[7], (DEPTH, GMLP_HEADS, GMLP_BLOCK), 0.1),
        "conv_dw_w": nrm(k[8], (DEPTH, CONV_WIDTH, D_CONV), CONV_WIDTH ** -0.5),
        "conv_dw_b": nrm(k[9], (DEPTH, D_CONV), 0.02),
        "conv_ln_g": 1.0 + nrm(k[10], (DEPTH, D_CONV), 0.05),
        "conv_ln_b": nrm(k[11], (DEPTH, D_CONV), 0.02),
        "conv_pw_w": nrm(k[12], (DEPTH, D_CONV, D_CONV), D_CONV ** -0.5),
        "conv_pw_b": nrm(k[13], (DEPTH, D_CONV), 0.02),
        "w_out": nrm(k[14], (DEPTH, D_MIX, D_MODEL), D_MIX ** -0.5),
        "norm2_g": 1.0 + nrm(k[15], (DEPTH, D_MODEL), 0.05),
        "ffn_wg": nrm(k[16], (N_DENSE, D_MODEL, D_FF), D_MODEL ** -0.5),
        "ffn_wu": nrm(k[17], (N_DENSE, D_MODEL, D_FF), D_MODEL ** -0.5),
        "ffn_wd": nrm(k[18], (N_DENSE, D_FF, D_MODEL), D_FF ** -0.5),
        "moe_router": nrm(k[19], (N_MOE, D_MODEL, N_EXPERTS), D_MODEL ** -0.5),
        "moe_wg": nrm(k[20], (N_MOE, N_EXPERTS, D_MODEL, D_FF_EXPERT), D_MODEL ** -0.5),
        "moe_wu": nrm(k[21], (N_MOE, N_EXPERTS, D_MODEL, D_FF_EXPERT), D_MODEL ** -0.5),
        "moe_wd": nrm(k[22], (N_MOE, N_EXPERTS, D_FF_EXPERT, D_MODEL), D_FF_EXPERT ** -0.5),
        "final_g": 1.0 + nrm(k[23], (D_MODEL,), 0.05),
    }

def second_block(x, norm1_g, w_in, pool_w, pool_scale, gm_norm_g, gm_ws, gm_b,
              conv_dw_w, conv_dw_b, conv_ln_g, conv_ln_b, conv_pw_w, conv_pw_b,
              w_out, norm2_g, ffn_wg, ffn_wu, ffn_wd,
              moe_router, moe_wg, moe_wu, moe_wd, final_g):
    splits = [D_POOL, D_POOL + D_GMLP, D_POOL + 2 * D_GMLP,
              D_POOL + 2 * D_GMLP + D_CONV]
    for l in range(DEPTH):
        h = rms_norm_2(x, norm1_g[l])
        p = h @ w_in[l]
        a, u, v, cv, cg = jnp.split(p, splits, axis=-1)
        ya = pool_mixer(a, pool_w[l], pool_scale[l])
        yb = gmlp_mixer(u, v, gm_norm_g[l], gm_ws[l], gm_b[l])
        yc = conv_module(cv, cg, conv_dw_w[l], conv_dw_b[l], conv_ln_g[l],
                         conv_ln_b[l], conv_pw_w[l], conv_pw_b[l])
        x = x + jnp.concatenate([ya, yb, yc], axis=-1) @ w_out[l]
        h = rms_norm_2(x, norm2_g[l])
        if l % 2 == 0:
            j = l // 2
            x = x + swiglu(h, ffn_wg[j], ffn_wu[j], ffn_wd[j])
        else:
            j = l // 2
            x = x + moe_swiglu(h, moe_router[j], moe_wg[j], moe_wu[j], moe_wd[j])
    return rms_norm_2(x, final_g)


def setup_inputs(seed=0):
    out = dict(first_inputs(seed))
    for name, value in second_inputs(seed + 1).items():
        if name != "x":
            out[name + "_2"] = value
    return out


def reference(
    x, meta_tokens, norm_g, w_in, b_forget, lam_q1, lam_k1, lam_q2, lam_k2, subln_g, w_out,
    final_g, norm1_g_2, w_in_2, pool_w_2, pool_scale_2, gm_norm_g_2, gm_ws_2, gm_b_2,
    conv_dw_w_2, conv_dw_b_2, conv_ln_g_2, conv_ln_b_2, conv_pw_w_2, conv_pw_b_2, w_out_2,
    norm2_g_2, ffn_wg_2, ffn_wu_2, ffn_wd_2, moe_router_2, moe_wg_2, moe_wu_2, moe_wd_2,
    final_g_2,
):
    x = first_block(
        x, meta_tokens, norm_g, w_in, b_forget, lam_q1, lam_k1, lam_q2, lam_k2, subln_g, w_out,
        final_g,
    )
    return second_block(
        x, norm1_g_2, w_in_2, pool_w_2, pool_scale_2, gm_norm_g_2, gm_ws_2, gm_b_2, conv_dw_w_2,
        conv_dw_b_2, conv_ln_g_2, conv_ln_b_2, conv_pw_w_2, conv_pw_b_2, w_out_2, norm2_g_2,
        ffn_wg_2, ffn_wu_2, ffn_wd_2, moe_router_2, moe_wg_2, moe_wu_2, moe_wd_2, final_g_2,
    )


_drawn_inputs = setup_inputs


def setup_inputs(seed=0):
    import zlib

    import numpy as np

    out = dict(_drawn_inputs(seed))
    spreads = {}
    factors = {'subln_g': 2.887, 'conv_ln_b_2': 3.626, 'conv_pw_b_2': 2.805}
    for name, (base, spread) in spreads.items():
        noise = np.random.default_rng([zlib.crc32(name.encode()), seed]).standard_normal(out[name].shape)
        drawn = base * np.exp(spread * noise) if base else spread * noise
        out[name] = __import__('jax').numpy.asarray(drawn.astype(out[name].dtype))
    for name, factor in factors.items():
        out[name] = (out[name] * factor).astype(out[name].dtype)
    return out
```

```python
from contextlib import ExitStack

import numpy as np

import concourse.bass as bass
from concourse import mybir

F32 = mybir.dt.float32
F32R = mybir.dt.float32r
U32 = mybir.dt.uint32
I32 = mybir.dt.int32
ACT = mybir.ActivationFunctionType
ALU = mybir.AluOpType
AXX = mybir.AxisListType.X

P = 128
D = 1024
KD = D // P
META, SEQ = 16, 256
LEN = META + SEQ
LAYERS = 2
EPS = 1e-6
LAMBDA_INIT = [0.8 - 0.6 * float(np.exp(-0.3 * layer)) for layer in range(LAYERS)]

DIFF_HEADS, FOX_HEADS, HEAD = 4, 8, 64
Z_T, LOGIT_T, QK_T, V_T = 0, 8, 9, 25
PROJ_T = 33
TURN_LAG = 2
MIX_ORDER = (4, 5, 6, 7, 0, 1, 2, 3)
ATT_TAIL = 6
SCALE = HEAD ** -0.5
ROPE_THETA = 10000.0
MIXW = 1024
QKN, VN, ZN = 16, 8, 8
ROPED = 8
MAPS = 2 * DIFF_HEADS + FOX_HEADS
HEADS = DIFF_HEADS + FOX_HEADS
QTILES = [(0, META, 0, META), (META, P, META, META + P), (META + P, P, 2 * META + P, LEN)]
MAPW = 2 * META + P + LEN
KEYS1 = LEN - META
NEG = 3.0e38

U1_TILES = [2] * 4 + [1] + [2] * 12 + [2] + [1] * 6
U1 = len(U1_TILES)
LOGIT_U, PROJ_U = 4, 17
UNITC = 2048
RAW, RING = 6, 3
POOL_T, GM_HEADS, GM_DIM, CONV_T, TAPS = 2, 4, 96, 3, 31
MIX_T = POOL_T + GM_HEADS + CONV_T
MIX_SPLITS = POOL_T + GM_HEADS // 2 + CONV_T
GM_CHUNK = 64
PW_U = 8
ACT_TAKES = CONV_T + POOL_T + GM_HEADS
TAP_STEP = 12
N_PAR, PAR2, CONST2 = 7, 11, 3
LEAD = 4
TOP_K = 2
FAR = 1000.0
U2 = [(KD, 256)] * 4 + [(KD, 192)] * 4 + [(CONV_T, CONV_T * P)] + [(MIX_T, P)] * KD
FF_T = 22
FF_HALF = FF_T // 2
UF = [(KD, 256)] * FF_T + [(FF_HALF, P)] * (2 * KD)
EXPERTS, CHUNKS, CHUNK = 8, 7, 512
UM = 6 * CHUNKS
UNIT_MIX = [LAYERS * U1, LAYERS * U1 + len(U2) + len(UF)]
UNIT_FF = UNIT_MIX[0] + len(U2)
UNIT_MOE = UNIT_MIX[1] + len(U2)
assert UNIT_MOE % RAW == 0 and U1 % RAW == 0 and UM % RAW == 0 and RAW % RING == 0
POOL_WINDOWS = (2, 4, 8, 16)
PADC = TAPS - 1
PADP = max(POOL_WINDOWS)
SPLIT_OUTPUTS = {0: 0, 1: 1, 3: 2, 4: 3, 5: 4}


def expert_units():
    order = []
    for c in range(CHUNKS):
        order += [("gate", c, 0), ("gate", c, 1), ("up", c, 0), ("up", c, 1)]
        if c:
            order += [("down", c - 1, 0), ("down", c - 1, 1)]
    return order + [("down", CHUNKS - 1, 0), ("down", CHUNKS - 1, 1)]


EXPERT_UNITS = expert_units()


def unit_columns(n):
    if n < LAYERS * U1:
        return KD * P * U1_TILES[n % U1]
    for base in UNIT_MIX:
        if base <= n < base + len(U2):
            k, w = U2[n - base]
            return k * w
    if UNIT_FF <= n < UNIT_FF + len(UF):
        k, w = UF[n - UNIT_FF]
        return k * w
    return UNITC


def build_program(nc, io):
    ctx = ExitStack()
    with ctx:
        def sb(name, shape, dt=F32, scope=ctx):
            return scope.enter_context(nc.sbuf_tensor(name, shape, dt))

        semaphores = {}

        def sem(name):
            semaphores[name] = ctx.enter_context(nc.semaphore(name))
            return semaphores[name]

        bank = [ctx.enter_context(nc.psum_tensor(f"bank{i}", [P, 512], F32)) for i in range(8)]
        raw = sb("raw", [P, RAW, UNITC])
        whi = sb("whi", [P, RING, UNITC], F32R)
        wlo = sb("wlo", [P, RING, UNITC], F32R)
        uhi = sb("uhi", [P, KD, LEN], F32R)
        ulo = sb("ulo", [P, KD, LEN], F32R)
        sq = sb("sq", [P, 2, LEN])
        ut = sb("ut", [P, 2, LEN])
        sd = sb("sd", [P, LEN])
        rstd = sb("rstd", [P, LEN])
        zs = sb("zs", [P, KD, LEN])
        xT = zs[:, :, 0:SEQ]
        ident = sb("ident", [P, P])
        mean_d = sb("mean_d", [P, P])
        mean_h = sb("mean_h", [P, P])
        mean_c = sb("mean_c", [P, P])
        ones = sb("ones", [P, P])
        eps = sb("eps", [P, 1])
        one = sb("one", [P, 1])
        gains = sb("gains", [P, 8, KD])

        first = ExitStack()
        hT = sb("hT", [P, KD, LEN], scope=first)
        qk = sb("qk", [P, QKN, LEN], scope=first)
        qraw = sb("qraw", [P, 2, LEN], scope=first)
        rc = sb("rc", [P, 2, LEN], scope=first)
        rsn = sb("rsn", [P, LEN], scope=first)
        vt = sb("vt", [P, 2, LEN], scope=first)
        v0 = sb("v0", [META, VN, P], scope=first)
        v12 = sb("v12", [P, VN, 2, P], scope=first)
        cum = sb("cum", [FOX_HEADS, LEN], scope=first)
        ncum = sb("ncum", [FOX_HEADS, LEN], scope=first)
        sm = sb("sm", [P, 2, MAPW], scope=first)
        ex = sb("ex", [P, 4, MAPW], scope=first)
        held = sb("held", [P, 4], scope=first)
        nmax = sb("nmax", [P, 4, 3], scope=first)
        sums = sb("sums", [P, 4, 3], scope=first)
        rsum = sb("rsum", [P, 4, 3], scope=first)
        rlam = sb("rlam", [P, 2, 3], scope=first)
        pd = sb("pd", [P, MAPW], scope=first)
        pr = sb("pr", [P, 2, MAPW], scope=first)
        pt0 = sb("pt0", [META, 2, LEN], scope=first)
        pt1 = sb("pt1", [P, 2, KEYS1 + P], scope=first)
        rope = sb("rope", [P, 4, LEN], scope=first)
        rot = sb("rot", [P, P], scope=first)
        mask = sb("mask", [P, LEN], scope=first)
        bforget = sb("bforget", [FOX_HEADS, LAYERS], scope=first)
        subln = sb("subln", [P, LAYERS, DIFF_HEADS], scope=first)
        subg = sb("subg", [P, LAYERS, DIFF_HEADS], scope=first)
        lamv = ex[:, 0:2, 0:256].rearrange("p l (v d) -> p l v d", v=4)
        lamp = sb("lamp", [P, LAYERS, 2], scope=first)
        lame = sb("lame", [P, LAYERS, 2], scope=first)
        lamd = sb("lamd", [P, LAYERS], scope=first)
        lam = sb("lam", [P, LAYERS], scope=first)
        h_in = qk[:, 0:KD, :]
        xb, ab, lf = (ex[0:FOX_HEADS, i, 0:LEN] for i in range(3))
        le, ll = sm[0:FOX_HEADS, 0, 0:LEN], sm[0:FOX_HEADS, 1, 0:LEN]
        osb = qk[:, 4:8, :]
        msb = qk[:, 0:4, :]
        sqo, mx32 = qraw, rc
        first.close()

        second = ExitStack()
        wsT = sb("wsT", [P, LAYERS, GM_HEADS, P], scope=second)
        gmb = sb("gmb", [P, LAYERS, GM_HEADS, SEQ], scope=second)
        gmg = sb("gmg", [P, LAYERS, GM_HEADS * GM_DIM], scope=second)
        poolw = sb("poolw", [P, LAYERS, POOL_T, 64], scope=second)
        pools = sb("pools", [P, LAYERS, POOL_T], scope=second)
        poolr = sb("poolr", [P, POOL_T, SEQ], scope=second)
        convw = sb("convw", [P, LAYERS, CONV_T, TAPS], scope=second)
        convp = sb("convp", [P, LAYERS, 4, CONV_T], scope=second)
        router = sb("router", [P, KD, EXPERTS], scope=second)
        lt = sb("lt", [P, P], scope=second)
        iota = sb("iota", [P, P], scope=second)
        mixer = ExitStack()
        sig = sb("sig", [P, 2, SEQ], scope=mixer)
        hpad = sb("hpad", [P, CONV_T, PADC + SEQ], scope=mixer)
        cacc = sb("cacc", [P, CONV_T, SEQ], scope=mixer)
        csq = sb("csq", [P, CONV_T, SEQ], scope=mixer)
        crs = sb("crs", [P, 2, SEQ], scope=mixer)
        chi = sb("chi", [P, CONV_T, SEQ], F32R, scope=mixer)
        clo = sb("clo", [P, CONV_T, SEQ], F32R, scope=mixer)
        pa = sb("pa", [P, POOL_T, SEQ], scope=mixer)
        pc = sb("pc", [P, POOL_T, PADP + SEQ], scope=mixer)
        py = sb("py", [P, POOL_T, SEQ], scope=mixer)
        gu = sb("gu", [P, GM_HEADS, SEQ], scope=mixer)
        gv = sb("gv", [P, 2, GM_HEADS * GM_DIM], scope=mixer)
        gss = sb("gss", [P, 4, 2], scope=mixer)
        gz = sb("gz", [P, GM_HEADS, SEQ], scope=mixer)
        gvj = gz[:].rearrange("p h t -> p (h t)")[:, 0:2 * GM_HEADS * GM_DIM].rearrange("p (a c) -> p a c", a=2)
        mhi = sb("mhi", [P, MIX_T, SEQ], F32R, scope=mixer)
        mlo = sb("mlo", [P, MIX_T, SEQ], F32R, scope=mixer)
        mixer.close()
        ffn = ExitStack()
        fs = sb("fs", [P, 2, SEQ], scope=ffn)
        fa = sb("fa", [P, 2, SEQ], scope=ffn)
        fhi = sb("fhi", [P, FF_T, SEQ], F32R, scope=ffn)
        flo = sb("flo", [P, FF_T, SEQ], F32R, scope=ffn)
        ffn.close()
        moe = ExitStack()
        un = sb("un", [P, KD, SEQ], scope=moe)
        nhi = sb("nhi", [P, 2, D], F32R, scope=moe)
        nlo = sb("nlo", [P, 2, D], F32R, scope=moe)
        hthi = sb("hthi", [P, KD, P], F32R, scope=moe)
        htlo = sb("htlo", [P, KD, P], F32R, scope=moe)
        gsa = sb("gsa", [P, 4, CHUNK], scope=moe)
        gs, ga = gsa[:, 0:2, :], gsa[:, 2:4, :]
        outn = gsa[:].rearrange("p (t h) c -> p t (h c)", t=2)
        athi = sb("athi", [P, 4, P], F32R, scope=moe)
        atlo = sb("atlo", [P, 4, P], F32R, scope=moe)
        yt = sb("yt", [P, D], scope=moe)
        pick = sb("pick", [P, 2, P], F32R, scope=moe)
        gpick = sb("gpick", [P, 2, P], scope=moe)
        gpickT = sb("gpickT", [P, 2, P], scope=moe)
        lg = sb("lg", [P, 2, EXPERTS], scope=moe)
        top = sb("top", [P, 2, 8], scope=moe)
        topi = sb("topi", [P, 2, 8], U32, scope=moe)
        topf = sb("topf", [P, 2, 8], scope=moe)
        tw = sb("tw", [P, 4, 2], scope=moe)
        oh = sb("oh", [P, 2, 2, EXPERTS], scope=moe)
        chosen = sb("chosen", [P, 2, EXPERTS], scope=moe)
        big = sb("big", [P, 2, EXPERTS], scope=moe)
        rank = sb("rank", [P, 2, 2 * EXPERTS + 1], scope=moe)
        gate = sb("gate", [P, 2, 2 * EXPERTS], scope=moe)
        cnt = sb("cnt", [P, 1], scope=moe)
        cnti = sb("cnti", [P, 1], I32, scope=moe)
        moe.close()
        second.close()

        raw_landed = [sem(f"raw_landed{i}") for i in range(RAW)]
        hi_ready, lo_ready = sem("hi_ready"), sem("lo_ready")
        unit_done = sem("unit_done")
        in_landed, par_landed = sem("in_landed"), sem("par_landed")
        lam_landed, par2_landed = sem("lam_landed"), sem("par2_landed")
        const_ready, sums_ready, const2_ready = sem("const_ready"), sem("sums_ready"), sem("const2_ready")
        x_ready, xs_ready = sem("x_ready"), sem("xs_ready")
        sq_ready, ms_step, sd_ready, rstd_ready = sem("sq_ready"), sem("ms_step"), sem("sd_ready"), sem("rstd_ready")
        u_ready, uhi_ready, ulo_ready = sem("u_ready"), sem("uhi_ready"), sem("ulo_ready")
        lam_step, lam_exp, lam_ready = sem("lam_step"), sem("lam_exp"), sem("lam_ready")
        proj_taken = sem("proj_taken")
        rot_done, rot_taken, rc_ready, roped = sem("rot_done"), sem("rot_taken"), sem("rc_ready"), sem("roped")
        vt_done, v_ready = sem("vt_done"), sem("v_ready")
        logit_step, lf_ready, cum_ready = sem("logit_step"), sem("lf_ready"), sem("cum_ready")
        s_done, masked, exp_done = sem("s_done"), sem("masked"), sem("exp_done")
        rsum_ready, rlam_ready, pd_ready = sem("rsum_ready"), sem("rlam_ready"), sem("pd_ready")
        diff_p, fox_p = sem("diff_p"), sem("fox_p")
        t_done, pt0_ready, pt1_ready, pv_done = sem("t_done"), sem("pt0_ready"), sem("pt1_ready"), sem("pv_done")
        diff_taken, fox_mixed = sem("diff_taken"), sem("fox_mixed")
        msq_done, msq_taken = sem("msq_done"), sem("msq_taken")
        subsd_ready, subrs_ready, sub_ready = sem("subsd_ready"), sem("subrs_ready"), sem("sub_ready")
        diff_mixed, mixhi_ready, mixlo_ready = sem("diff_mixed"), sem("mixhi_ready"), sem("mixlo_ready")
        act_taken, cv_taken = sem("act_taken"), sem("cv_taken")
        vsq_ready, vsd_ready, vrs_ready, vn_ready = sem("vsq_ready"), sem("vsd_ready"), sem("vrs_ready"), sem("vn_ready")
        z_done, zb_ready, gm_ready = sem("z_done"), sem("zb_ready"), sem("gm_ready")
        scan_ready, pool_step, pool_ready, pool_done = sem("scan_ready"), sem("pool_step"), sem("pool_ready"), sem("pool_done")
        tap_done, conv_ready, mean_done, centred = sem("tap_done"), sem("conv_ready"), sem("mean_done"), sem("centred")
        csq_ready, var_done, csd_ready, crs_ready = sem("csq_ready"), sem("var_done"), sem("csd_ready"), sem("crs_ready")
        cn_ready, cs_ready, chi_ready, clo_ready = sem("cn_ready"), sem("cs_ready"), sem("chi_ready"), sem("clo_ready")
        mhi_ready, mlo_ready = sem("mhi_ready"), sem("mlo_ready")
        fs_ready, fa_ready, fhi_ready, flo_ready = sem("fs_ready"), sem("fa_ready"), sem("fhi_ready"), sem("flo_ready")
        un_ready, lg_done, route_step = sem("un_ready"), sem("lg_done"), sem("route_step")
        tw_diff, tw_exp, chosen_ready = sem("tw_diff"), sem("tw_exp"), sem("chosen_ready")
        rank_done, route_ready, count_ready = sem("rank_done"), sem("route_ready"), sem("count_ready")
        nt_done, nhi_ready, nlo_ready = sem("nt_done"), sem("nhi_ready"), sem("nlo_ready")
        pick_ready, gpick_ready = sem("pick_ready"), sem("gpick_ready")
        gpickT_done, gpickT_ready = sem("gpickT_done"), sem("gpickT_ready")
        gather_done, hthi_ready, htlo_ready = sem("gather_done"), sem("hthi_ready"), sem("htlo_ready")
        silu_ready, a_ready = sem("silu_ready"), sem("a_ready")
        at_done, athi_ready, atlo_ready = sem("at_done"), sem("athi_ready"), sem("atlo_ready")
        rank_zero, yt_ready = sem("rank_zero"), sem("yt_ready")
        scat_done, scat_taken, last_done, last_taken = sem("scat_done"), sem("scat_taken"), sem("last_done"), sem("last_taken")
        result_ready, ot_done, ot_ready, stored = sem("result_ready"), sem("ot_done"), sem("ot_ready"), sem("stored")

        block = ctx.enter_context(nc.Block())

        def load_unit(sp, n, turn=0, per=0, source=None, columns=None):
            c = columns or unit_columns(n)
            if n >= RAW:
                sp.wait_ge(lo_ready, turn * per + (n - RAW + 1))
            if source is None:
                source = io["w"][n, :, 0:c]
            sp.dma_start(raw[:, n % RAW, 0:c], source).then_inc(raw_landed[n % RAW], 16)

        def split_hi(act, n, turn=0, per=0, columns=None):
            c = columns or unit_columns(n)
            act.wait_ge(raw_landed[n % RAW], turn * (16 * (per // RAW)) + 16 * (n // RAW + 1))
            if n >= RING:
                act.wait_ge(unit_done, turn * per + (n - RING + 1))
            act.activation(whi[:, n % RING, 0:c], raw[:, n % RAW, 0:c], ACT.Copy).then_inc(hi_ready, 1)

        def split_lo(dve, n, turn=0, per=0, columns=None):
            c = columns or unit_columns(n)
            dve.wait_ge(hi_ready, turn * per + (n + 1))
            dve.tensor_tensor(wlo[:, n % RING, 0:c], raw[:, n % RAW, 0:c], whi[:, n % RING, 0:c].bitcast(F32),
                              ALU.subtract).then_inc(lo_ready, 1)

        def unit_views(n, k):
            c = unit_columns(n)
            return [t[:, n % RING, 0:c].rearrange("p (k c) -> p k c", k=k) for t in (whi, wlo)]

        def three_pass(pe, out, s_hi, s_lo, m_hi, m_lo, start, stop):
            pe.matmul(out, s_hi, m_hi, start=start, stop=False)
            pe.matmul(out, s_hi, m_lo, start=False, stop=False)
            return pe.matmul(out, s_lo, m_hi, start=False, stop=stop)

        def proj_place(i):
            if i < LOGIT_T:
                return i // 2, i % 2
            return (LOGIT_U, 0) if i == LOGIT_T else (LOGIT_U + 1 + (i - QK_T) // 2, (i - QK_T) % 2)

        def out_tiles(j):
            d = 0 if j == PROJ_U else 2 + (j - PROJ_U - 1)
            return range(d, d + U1_TILES[j])

        def head_at(m):
            if 0 <= m < 2 * DIFF_HEADS:
                return m // 2 if m % 2 else None
            return m - DIFF_HEADS if 2 * DIFF_HEADS <= m < MAPS else None

        @block.sync
        def _(sp):
            sp.dma_start(h_in, io["hT"]).then_inc(in_landed, 16)
            load_unit(sp, 0)
            load_unit(sp, 1)
            for dst, name in ((gains, "gains"), (rope, "rope"), (rot, "rot"), (mask, "mask"), (ident, "ident"),
                              (bforget, "bforget"), (subln, "subln")):
                sp.dma_start(dst[:], io[name]).then_inc(par_landed, 16)
            sp.dma_start(lamv, io["lamv"]).then_inc(lam_landed, 16)
            for n in range(2, RAW):
                load_unit(sp, n)
            with sp.Fori(0, LAYERS) as l:
                for j in range(RAW, U1 + RAW):
                    c = unit_columns(j) if j < U1 else max(unit_columns(j), unit_columns(UNIT_MIX[0] + j - U1))
                    src = io["w"][bass.ds(l * U1 + j, 1), :, 0:c].rearrange("a p c -> (a p) c")
                    load_unit(sp, j, l, U1, src, c)
            for n in range(UNIT_MIX[0] + RAW, UNIT_FF):
                load_unit(sp, n)
            for first_n, count in ((UNIT_FF, FF_T), (UNIT_FF + FF_T, 2 * KD)):
                for n in range(first_n, first_n + LEAD):
                    load_unit(sp, n)
                n = first_n + LEAD
                with sp.Fori(0, (count - LEAD) // RAW) as t:
                    for j in range(RAW):
                        src = io["w"][bass.ds(t * RAW + (n + j), 1), :, 0:unit_columns(n + j)].rearrange("a p c -> (a p) c")
                        load_unit(sp, n + j, t, RAW, src)
            for n in range(UNIT_MIX[1], UNIT_MOE):
                load_unit(sp, n)
            for j in range(2):
                load_unit(sp, UNIT_MOE + j, source=io["wm"][0, j])

            def expert(it):
                for j in range(2, UM + 2):
                    e = it % EXPERTS if j < UM else (it + 1) % EXPERTS
                    src = io["wm"][bass.ds(e, 1), j % UM].rearrange("a p c -> (a p) c")
                    load_unit(sp, UNIT_MOE + j, it, UM, src)

            with sp.Fori(0, EXPERTS) as it:
                expert(it)
            sp.wait_ge(count_ready, 1)
            fullest = sp.value_load(cnti[0:1, 0:1], min_val=0, max_val=SEQ)
            with sp.If(fullest > P):
                with sp.Fori(EXPERTS, 2 * EXPERTS) as it:
                    expert(it)
            for tt in range(2):
                sp.wait_ge(ot_ready, 2 * tt + 2)
                sp.dma_start(io["out"][0, tt * P:(tt + 1) * P, :], outn[:, tt, :]).then_inc(stored, 16)
            sp.wait_ge(stored, 32)

        @block.tensor
        def _(pe):
            def norm_sums(q, n):
                for k in range(KD):
                    pe.wait_ge(sq_ready, q * KD + (k + 1))
                    pe.matmul(bank[7][:, 0:n], mean_d[:], sq[:, k % 2, 0:n], start=(k == 0), stop=(k == KD - 1)).then_inc(ms_step, 1)

            def project(l, i):
                u, s = proj_place(i)
                hi, lo = unit_views(u, KD)
                if s == 0:
                    pe.wait_ge(lo_ready, l * U1 + (u + 1))
                if i >= 4:
                    pe.wait_ge(proj_taken, l * PROJ_T + (i - 3))
                cols = slice(s * P, (s + 1) * P)
                for k in range(KD):
                    if i == 0:
                        pe.wait_ge(ulo_ready, l * KD + (k + 1))
                    mm = three_pass(pe, bank[i % 4][:, 0:LEN], hi[:, k, cols], lo[:, k, cols],
                                    uhi[:, k, :], ulo[:, k, :], k == 0, k == KD - 1)
                if s == U1_TILES[u] - 1:
                    mm.then_inc(unit_done, 1)

            def turn(l, i):
                if QK_T <= i < QK_T + ROPED:
                    r = i - QK_T
                    pe.wait_ge(proj_taken, l * PROJ_T + (i + 1))
                    if r >= 2:
                        pe.wait_ge(rot_taken, l * ROPED + (r - 1))
                    pe.matmul(bank[4 + r % 2][:, 0:LEN], rot[:], qraw[:, r % 2, :], start=True, stop=True).then_inc(rot_done, 1)
                if i >= V_T:
                    v = i - V_T
                    pe.wait_ge(proj_taken, l * PROJ_T + (i + 1))
                    if v >= 2:
                        pe.wait_ge(v_ready, l * VN + (v - 1))
                    b = bank[6 + v % 2]
                    pe.transpose(b[0:META, 0:P], vt[:, v % 2, 0:META], ident[:])
                    pe.transpose(b[:, P:2 * P], vt[:, v % 2, META:META + P], ident[:])
                    pe.transpose(b[:, 2 * P:3 * P], vt[:, v % 2, META + P:LEN], ident[:]).then_inc(vt_done, 1)

            def scores(l, m):
                if m >= 3:
                    pe.wait_ge(masked, l * MAPS + (m - 2))
                fox = m >= 2 * DIFF_HEADS
                if fox:
                    f = m - 2 * DIFF_HEADS
                    tq, tk, part = 8 + f // 2, 12 + f // 2, HEAD * (f % 2)
                    pe.wait_ge(proj_taken, l * PROJ_T + (QK_T + tk + 1))
                    pe.wait_ge(cum_ready, 2 * l + 2)
                else:
                    tq, tk, part = m // 2, DIFF_HEADS + m // 2, HEAD * (m % 2)
                    pe.wait_ge(roped, l * ROPED + (tk + 1))
                for q0, rows, c0, keys in reversed(QTILES):
                    out = bank[m % 3][0:rows, c0:c0 + keys]
                    mm = pe.matmul(out, qk[part:part + HEAD, tq, q0:q0 + rows], qk[part:part + HEAD, tk, 0:keys], start=True, stop=not fox)
                    if fox:
                        head = ident[0:FOX_HEADS, f:f + 1]
                        pe.matmul(out, ncum[:, q0:q0 + rows], head.to_broadcast([FOX_HEADS, keys]), start=False, stop=False)
                        mm = pe.matmul(out, head.to_broadcast([FOX_HEADS, rows]), cum[:, 0:keys], start=False, stop=True)
                mm.then_inc(s_done, 1)

            def turn_probs(l, p):
                if p < DIFF_HEADS:
                    pe.wait_ge(diff_p, l * DIFF_HEADS + (p + 1))
                else:
                    pe.wait_ge(fox_p, l * FOX_HEADS + (p - DIFF_HEADS + 1))
                if p >= 1:
                    pe.wait_ge(pt0_ready, l * HEADS + p)
                    pe.wait_ge(pt1_ready, l * HEADS + p)
                b = pr[:, p % 2, :]
                pe.transpose(bank[4][:, 0:P], b[:, 2 * META:2 * META + P], ident[:])
                pe.transpose(bank[4][:, P:2 * P], b[:, 3 * META + P:3 * META + 2 * P], ident[:])
                pe.transpose(bank[4][:, 2 * P:3 * P], b[:, 3 * META + 2 * P:MAPW], ident[:])
                pe.transpose(bank[5][0:META, 0:META], b[0:META, 0:META], ident[0:META, 0:META])
                pe.transpose(bank[5][0:META, META:META + P], b[:, META:2 * META], ident[:])
                pe.transpose(bank[5][0:META, META + P:LEN], b[:, 2 * META + P:3 * META + P], ident[:]).then_inc(t_done, 1)

            def meet_values(l, p):
                if p < DIFF_HEADS:
                    o, c, w, part = p, 0, P, 0
                else:
                    f = p - DIFF_HEADS
                    o, c, w, part = DIFF_HEADS + f // 2, HEAD * (f % 2), HEAD, HEAD * (f % 2)
                if p == 0:
                    pe.wait_ge(v_ready, l * VN + VN)
                if part == 0:
                    if 2 <= o < DIFF_HEADS + 2:
                        pe.wait_ge(diff_taken, l * DIFF_HEADS + (o - 1))
                    elif o >= DIFF_HEADS + 2:
                        pe.wait_ge(fox_mixed, l * (FOX_HEADS // 2) + (o - DIFF_HEADS - 1))
                pe.wait_ge(pt0_ready, l * HEADS + (p + 1))
                pe.wait_ge(pt1_ready, l * HEADS + (p + 1))
                b, i = bank[6 + o % 2][part:part + w, :], p % 2
                pe.matmul(b[:, 0:LEN], v0[:, o, c:c + w], pt0[:, i, :], start=True, stop=False, skip_group_check=True)
                pe.matmul(b[:, META:LEN], v12[:, o, 0, c:c + w], pt1[:, i, 0:KEYS1], start=False, stop=False, skip_group_check=True)
                pe.matmul(b[:, META + P:LEN], v12[:, o, 1, c:c + w], pt1[:, i, KEYS1:KEYS1 + P], start=False, stop=True,
                          skip_group_check=True).then_inc(pv_done, 1)

            def head_sums(l, h):
                pe.wait_ge(diff_taken, l * DIFF_HEADS + (h + 1))
                if h:
                    pe.wait_ge(msq_taken, l * DIFF_HEADS + h)
                pe.matmul(bank[3][:, 0:LEN], mean_h[:], sqo[:, h % 2, :], start=True, stop=True).then_inc(msq_done, 1)

            def first_out(l, j):
                hi, lo = unit_views(j, KD)
                pe.wait_ge(lo_ready, l * U1 + (j + 1))
                for s, d in enumerate(out_tiles(j)):
                    if d >= 4:
                        pe.wait_ge(x_ready, l * KD + (KD + d - 3))
                    for i, k in enumerate(MIX_ORDER):
                        if d == 0:
                            pe.wait_ge(mixlo_ready, l * KD + (i + 1))
                        mm = three_pass(pe, bank[d % 4][:, 0:LEN], hi[:, k, s * P:(s + 1) * P], lo[:, k, s * P:(s + 1) * P],
                                        uhi[:, k, :], ulo[:, k, :], i == 0, i == KD - 1)
                mm.then_inc(unit_done, 1)

            pe.wait_ge(const_ready, 1)
            pe.wait_ge(par_landed, 16 * N_PAR)
            with pe.Fori(0, LAYERS) as l:
                norm_sums(l, LEN)
                for i in range(PROJ_T):
                    project(l, i)
                    turn(l, i - TURN_LAG)
                for i in range(PROJ_T - TURN_LAG, PROJ_T):
                    turn(l, i)
                for s in range(MAPS + ATT_TAIL):
                    if s < MAPS:
                        scores(l, s)
                    if (p := head_at(s - 3)) is not None:
                        turn_probs(l, p)
                    if (p := head_at(s - 4)) is not None:
                        meet_values(l, p)
                    if (p := head_at(s - 5)) is not None and p < DIFF_HEADS:
                        head_sums(l, p)
                for j in range(PROJ_U, U1):
                    first_out(l, j)
            norm_sums(2, LEN)

            def mixer_tiles(L):
                n0 = UNIT_MIX[L]
                items = [(c, half * P, P) for c in range(CONV_T) for half in range(2)]
                items += [(CONV_T, half * P, P) for half in range(2)]
                items += [(CONV_T + 1 + h // 2, GM_DIM * (h % 2), GM_DIM) for h in range(GM_HEADS)]
                cv, at = CONV_T * L, ACT_TAKES * L
                taken = {4: (cv_taken, cv + 1), 5: (act_taken, at + 1), 6: (cv_taken, cv + 2), 7: (act_taken, at + 2),
                         8: (cv_taken, cv + 3), 9: (act_taken, at + 3), 10: (act_taken, at + 4), 11: (act_taken, at + 5)}
                for i, (u, c0, w) in enumerate(items):
                    hi, lo = unit_views(n0 + u, KD)
                    if c0 == 0:
                        pe.wait_ge(lo_ready, n0 + u + 1)
                    if i in taken:
                        pe.wait_ge(*taken[i])
                    for k in range(KD):
                        if i == 0:
                            pe.wait_ge(ulo_ready, SPLIT_OUTPUTS[3 + 2 * L] * KD + k + 1)
                        mm = three_pass(pe, bank[i % 4][0:w, 0:SEQ], hi[:, k, c0:c0 + w], lo[:, k, c0:c0 + w],
                                        uhi[:, k, 0:SEQ], ulo[:, k, 0:SEQ], k == 0, k == KD - 1)
                    if c0:
                        mm.then_inc(unit_done, 1)
                for s in range(2):
                    n = n0 + CONV_T + 3 + s
                    hi, lo = unit_views(n, KD)
                    w = unit_columns(n) // KD
                    pe.wait_ge(lo_ready, n + 1)
                    for tt in range(2):
                        out, t = bank[4 + tt][:, s * w:(s + 1) * w], slice(tt * P, (tt + 1) * P)
                        for k in range(KD):
                            mm = three_pass(pe, out, uhi[:, k, t], ulo[:, k, t], hi[:, k, :], lo[:, k, :], k == 0, k == KD - 1)
                    mm.then_inc(unit_done, 1)

            def mixer_parts(L):
                if L == 0:
                    pe.wait_ge(par2_landed, 16 * PAR2)
                    pe.wait_ge(const2_ready, CONST2)
                pe.wait_ge(pool_ready, POOL_T * (L + 1))
                for g in range(len(POOL_WINDOWS)):
                    part, c = slice(64 * (g % 2), 64 * (g % 2) + 64), g // 2
                    mm = pe.matmul(bank[6][part, c * SEQ:(c + 1) * SEQ], poolw[part, L, c, :], py[part, c, :], start=True, stop=True)
                mm.then_inc(pool_done, 1)
                pe.wait_ge(vn_ready, 2 * (L + 1))
                for h in range(GM_HEADS):
                    b = bank[7 if h < 2 else 4]
                    for blk in range(2):
                        c0 = (h % 2) * SEQ + blk * P
                        mm = pe.matmul(b[0:GM_DIM, c0:c0 + P], gv[:, blk, h * GM_DIM:(h + 1) * GM_DIM], wsT[:, L, h, :], start=True, stop=True)
                    if h % 2:
                        mm.then_inc(z_done, 1)
                for c in range(CONV_T):
                    pe.wait_ge(conv_ready, CONV_T * L + c + 1)
                    mm = pe.matmul(bank[5][:, 0:SEQ], mean_c[:], cacc[:, c, :], start=(c == 0), stop=(c == CONV_T - 1))
                mm.then_inc(mean_done, 1)
                pe.wait_ge(mlo_ready, MIX_SPLITS * L + POOL_T)
                for c in range(CONV_T):
                    pe.wait_ge(csq_ready, CONV_T * L + c + 1)
                    mm = pe.matmul(bank[6][:, 0:SEQ], mean_c[:], csq[:, c, :], start=(c == 0), stop=(c == CONV_T - 1))
                mm.then_inc(var_done, 1)
                n = UNIT_MIX[L] + PW_U
                hi, lo = unit_views(n, CONV_T)
                pe.wait_ge(lo_ready, n + 1)
                pe.wait_ge(act_taken, ACT_TAKES * (L + 1))
                for f in range(CONV_T):
                    for k in range(CONV_T):
                        if f == 0:
                            pe.wait_ge(clo_ready, CONV_T * L + k + 1)
                        mm = three_pass(pe, bank[f][:, 0:SEQ], hi[:, k, f * P:(f + 1) * P], lo[:, k, f * P:(f + 1) * P],
                                        chi[:, k, :], clo[:, k, :], k == 0, k == CONV_T - 1)
                mm.then_inc(unit_done, 1)

            def mixer_out(L):
                base = (1 if L == 0 else 3) * KD
                for d in range(KD):
                    n = UNIT_MIX[L] + PW_U + 1 + d
                    hi, lo = unit_views(n, MIX_T)
                    pe.wait_ge(lo_ready, n + 1)
                    if d == 0:
                        pe.wait_ge(mlo_ready, MIX_SPLITS * (L + 1))
                    if d >= 4:
                        pe.wait_ge(xs_ready, base + d - 3)
                    for i in range(MIX_T):
                        rows = slice(0, GM_DIM if POOL_T <= i < POOL_T + GM_HEADS else P)
                        mm = three_pass(pe, bank[d % 4][:, 0:SEQ], hi[rows, i, :], lo[rows, i, :], mhi[rows, i, :], mlo[rows, i, :],
                                        i == 0, i == MIX_T - 1)
                    mm.then_inc(unit_done, 1)

            def ffn_in(f, t=0):
                n = UNIT_FF + f
                hi, lo = unit_views(n, KD)
                pe.wait_ge(lo_ready, t * RAW + (n + 1))
                if f >= 2:
                    pe.wait_ge(fs_ready, t * RAW + (f - 1))
                    pe.wait_ge(fa_ready, t * RAW + (f - 1))
                for half in range(2):
                    cols = slice(half * P, (half + 1) * P)
                    for k in range(KD):
                        if f == 0 and half == 0:
                            pe.wait_ge(ulo_ready, SPLIT_OUTPUTS[4] * KD + k + 1)
                        mm = three_pass(pe, bank[2 * half + f % 2][:, 0:SEQ], hi[:, k, cols], lo[:, k, cols],
                                        uhi[:, k, 0:SEQ], ulo[:, k, 0:SEQ], k == 0, k == KD - 1)
                mm.then_inc(unit_done, 1)

            def ffn_out(d, t=0):
                if d >= 2:
                    pe.wait_ge(xs_ready, t * (RAW // 2) + (2 * KD + d - 2))
                for half in range(2):
                    n = UNIT_FF + FF_T + 2 * d + half
                    hi, lo = unit_views(n, FF_HALF)
                    pe.wait_ge(lo_ready, t * RAW + (n + 1))
                    for j in range(FF_HALF):
                        f = half * FF_HALF + j
                        if d == 0:
                            pe.wait_ge(flo_ready, f + 1)
                        mm = three_pass(pe, bank[4 + d % 3][:, 0:SEQ], hi[:, j, :], lo[:, j, :], fhi[:, f, :], flo[:, f, :],
                                        f == 0, f == FF_T - 1)
                    mm.then_inc(unit_done, 1)

            for L in range(LAYERS):
                norm_sums(3 + 2 * L, SEQ)
                mixer_tiles(L)
                mixer_parts(L)
                mixer_out(L)
                norm_sums(4 + 2 * L, SEQ)
                if L == 0:
                    for f in range(LEAD):
                        ffn_in(f)
                    with pe.Fori(0, (FF_T - LEAD) // RAW) as t:
                        for j in range(RAW):
                            ffn_in(LEAD + j, t)
                    for d in range(LEAD // 2):
                        ffn_out(d)
                    with pe.Fori(0, (2 * KD - LEAD) // RAW) as t:
                        for j in range(RAW // 2):
                            ffn_out(LEAD // 2 + j, t)

            for k in range(KD):
                pe.wait_ge(un_ready, k + 1)
                for tt in range(2):
                    mm = pe.matmul(bank[tt][:, 0:EXPERTS], un[:, k, tt * P:(tt + 1) * P], router[:, k, :], start=(k == 0), stop=(k == KD - 1))
            mm.then_inc(lg_done, 1)
            for tt in range(2):
                for half in range(2):
                    for i in range(4):
                        mm = pe.transpose(bank[2 + 2 * tt + half][:, i * P:(i + 1) * P], un[:, 4 * half + i, tt * P:(tt + 1) * P], ident[:])
                    mm.then_inc(nt_done, 1)
            pe.wait_ge(chosen_ready, 2)
            pe.matmul(bank[6][:, 0:EXPERTS], lt[:], chosen[:, 0, :], start=True, stop=True)
            pe.matmul(bank[6][:, EXPERTS:2 * EXPERTS], ones[:], chosen[:, 0, :], start=True, stop=False)
            pe.matmul(bank[6][:, EXPERTS:2 * EXPERTS], lt[:], chosen[:, 1, :], start=False, stop=True)
            pe.matmul(bank[6][:, 2 * EXPERTS:3 * EXPERTS], ones[:], chosen[:, 0, :], start=True, stop=False)
            pe.matmul(bank[6][:, 2 * EXPERTS:3 * EXPERTS], ones[:], chosen[:, 1, :], start=False, stop=True).then_inc(rank_done, 1)

            def gather(half, g):
                if half == 0:
                    pe.wait_ge(pick_ready, g + 1)
                else:
                    pe.wait_ge(htlo_ready, 2 * g + 1)
                for i in range(4):
                    d = 4 * half + i
                    for tt in range(2):
                        for part in (nhi, nlo):
                            mm = pe.matmul(bank[7][:, i * P:(i + 1) * P], part[:, tt, d * P:(d + 1) * P], pick[:, tt, :],
                                           start=(tt == 0 and part is nhi), stop=(tt == 1 and part is nlo))
                mm.then_inc(gather_done, 1)

            def scatter(r, done):
                for i in range(2):
                    d = 2 * r + i
                    mm = pe.matmul(bank[7][:, i * SEQ:(i + 1) * SEQ], yt[:, d * P:(d + 1) * P], gpickT[:].rearrange("p a t -> p (a t)"),
                                   start=True, stop=True)
                mm.then_inc(done, 1)

            def expert(it):
                def weights(pos):
                    n = UNIT_MOE + pos
                    pe.wait_ge(lo_ready, it * UM + (n + 1))
                    return unit_views(n, 2 if EXPERT_UNITS[pos][0] == "down" else 4)

                def rows(kind, c):
                    b = bank[(0 if kind == "gate" else 2) + c % 2]
                    if c >= 2:
                        pe.wait_ge(silu_ready if kind == "gate" else a_ready, it * CHUNKS + (c - 1))
                    for part in range(2):
                        hi, lo = weights(EXPERT_UNITS.index((kind, c, part)))
                        for i in range(4):
                            k = 4 * part + i
                            if c == 0 and kind == "gate" and i == 0:
                                pe.wait_ge(htlo_ready, 2 * it + (part + 1))
                            mm = three_pass(pe, b[:], hthi[:, k, :], htlo[:, k, :], hi[:, i, :], lo[:, i, :], k == 0, k == KD - 1)
                        mm.then_inc(unit_done, 1)

                def turn_rows(c):
                    pe.wait_ge(a_ready, it * CHUNKS + (c + 1))
                    if c:
                        pe.wait_ge(atlo_ready, it * CHUNKS + c)
                    for i in range(4):
                        mm = pe.transpose(bank[4][:, i * P:(i + 1) * P], ga[:, c % 2, i * P:(i + 1) * P], ident[:])
                    mm.then_inc(at_done, 1)

                def down(c):
                    pe.wait_ge(atlo_ready, it * CHUNKS + (c + 1))
                    if c == 0:
                        pe.wait_ge(yt_ready, it + 1)
                    for part in range(2):
                        hi, lo = weights(EXPERT_UNITS.index(("down", c, part)))
                        for i in range(2):
                            f = 2 * part + i
                            for half in range(2):
                                cols = slice(half * 512, (half + 1) * 512)
                                mm = three_pass(pe, bank[5 + half][:], athi[:, f, :], atlo[:, f, :], hi[:, i, cols], lo[:, i, cols],
                                                c == 0 and f == 0, c == CHUNKS - 1 and f == 3)
                        mm.then_inc(unit_done, 1)

                for c in range(CHUNKS):
                    if 1 <= c <= 4:
                        if c > 1:
                            pe.wait_ge(scat_taken, it * 4 + (c - 1))
                        scatter(c - 1, scat_done)
                    rows("gate", c)
                    if c:
                        turn_rows(c - 1)
                    rows("up", c)
                    if c == 5:
                        pe.wait_ge(gpick_ready, it + 1)
                        pe.wait_ge(scat_taken, it * 4 + 4)
                        pe.transpose(bank[7][:, 0:P], gpick[:, 0, :], ident[:])
                        pe.transpose(bank[7][:, P:2 * P], gpick[:, 1, :], ident[:]).then_inc(gpickT_done, 1)
                    if c == 6:
                        pe.wait_ge(gpickT_ready, it + 2)
                        gather(0, it + 1)
                    if c:
                        down(c - 1)
                turn_rows(CHUNKS - 1)
                gather(1, it + 1)
                down(CHUNKS - 1)

            pe.wait_ge(nlo_ready, 4)
            gather(0, 0)
            gather(1, 0)
            with pe.Fori(0, EXPERTS) as it:
                expert(it)
            pe.wait_ge(yt_ready, EXPERTS + 1)
            pe.wait_ge(htlo_ready, 2 * EXPERTS + 2)
            pe.wait_ge(count_ready, 1)
            fullest = pe.value_load(cnti[0:1, 0:1], min_val=0, max_val=SEQ)
            with pe.If(fullest > P):
                with pe.Fori(EXPERTS, 2 * EXPERTS) as it:
                    expert(it)
                pe.wait_ge(yt_ready, 2 * EXPERTS + 1)
                pe.wait_ge(htlo_ready, 4 * EXPERTS + 2)
            for r in range(4):
                if r:
                    pe.wait_ge(last_taken, r)
                scatter(r, last_done)
            pe.wait_ge(last_taken, 4)
            norm_sums(7, SEQ)
            for tt in range(2):
                for half in range(2):
                    for i in range(4):
                        if tt == 0:
                            pe.wait_ge(result_ready, 4 * half + i + 1)
                        mm = pe.transpose(bank[2 * tt + half][:, i * P:(i + 1) * P], un[:, 4 * half + i, tt * P:(tt + 1) * P], ident[:])
                    mm.then_inc(ot_done, 1)

        @block.scalar
        def _(act):
            def norm_squares(q, n, source, ready, per_tile=1, first_count=0):
                for k in range(KD):
                    act.wait_ge(ready, first_count + k // per_tile + 1)
                    if k >= 2:
                        act.wait_ge(ms_step, q * KD + (k - 1))
                    act.activation(sq[:, k % 2, 0:n], source[:, k, 0:n], ACT.Square).then_inc(sq_ready, 1)
                act.wait_ge(ms_step, q * KD + KD)
                act.activation(sd[:, 0:n], bank[7][:, 0:n], ACT.Sqrt, bias=eps[:]).then_inc(sd_ready, 1)

            def norm_hi(order, n):
                for k in range(KD):
                    act.wait_ge(u_ready, order * KD + (k + 1))
                    act.activation(uhi[:, k, 0:n], ut[:, k % 2, 0:n], ACT.Copy).then_inc(uhi_ready, 1)

            def take_tile(l, i):
                src = bank[i % 4][:, 0:LEN]
                if i < LOGIT_T:
                    act.activation(zs[:, i, :], src, ACT.Silu).then_inc(proj_taken, 1)
                elif i == LOGIT_T:
                    act.activation(xb, bank[i % 4][0:FOX_HEADS, 0:LEN], ACT.Identity,
                                   bias=bforget[:, bass.ds(l, 1)]).then_inc(proj_taken, 1)
                    act.wait_ge(proj_taken, l * PROJ_T + (i + 1))
                    act.activation(ab, xb, ACT.Abs).then_inc(logit_step, 1)
                    act.wait_ge(logit_step, 3 * l + 1)
                    act.activation(le, ab, ACT.Exp, scale=-1.0).then_inc(logit_step, 1)
                    act.wait_ge(logit_step, 3 * l + 2)
                    act.activation(ll, le, ACT.Ln, bias=one[0:FOX_HEADS, :]).then_inc(logit_step, 1)
                elif i < QK_T + ROPED:
                    r = i - QK_T
                    if r >= 2:
                        act.wait_ge(rot_done, l * ROPED + (r - 1))
                        act.wait_ge(rc_ready, l * ROPED + (r - 1))
                    act.activation(qraw[:, r % 2, :], src, ACT.Copy).then_inc(proj_taken, 1)
                elif i < V_T:
                    r = i - QK_T
                    scale = -SCALE if r < ROPED + QKN // 4 else 1.0
                    act.activation(qk[:, r, :], src, ACT.Copy, scale=scale).then_inc(proj_taken, 1)
                else:
                    v = i - V_T
                    if v >= 2:
                        act.wait_ge(vt_done, l * VN + (v - 1))
                    act.activation(vt[:, v % 2, :], src, ACT.Copy).then_inc(proj_taken, 1)

            def exp_map(l, m):
                act.wait_ge(masked, l * MAPS + (m + 1))
                if m >= 4:
                    if m - 4 < 2 * DIFF_HEADS:
                        act.wait_ge(diff_p, l * DIFF_HEADS + ((m - 4) // 2 + 1))
                    else:
                        act.wait_ge(fox_p, l * FOX_HEADS + (m - 4 - 2 * DIFF_HEADS + 1))
                for t, (q0, rows, c0, keys) in enumerate(QTILES):
                    op = act.activation(ex[0:rows, m % 4, c0:c0 + keys], sm[0:rows, m % 2, c0:c0 + keys], ACT.Exp,
                                        bias=nmax[0:rows, m % 4, t:t + 1], scale=-1.0, accum_out=sums[0:rows, m % 4, t:t + 1])
                op.then_inc(exp_done, 1)

            def mixed_hi(l, i):
                act.wait_ge(*((fox_mixed, l * 4 + (i + 1)) if i < 4 else (diff_mixed, l * 4 + (i - 3))))
                act.activation(uhi[:, MIX_ORDER[i], :], mx32[:, i % 2, :], ACT.Copy).then_inc(mixhi_ready, 1)

            act.wait_ge(const_ready, 1)
            split_hi(act, 0)
            split_hi(act, 1)
            act.wait_ge(lam_step, 2 * LAYERS)
            act.activation(lame[:], lamp[:], ACT.Exp).then_inc(lam_exp, 1)
            act.wait_ge(par_landed, 16 * N_PAR)
            with act.Fori(0, LAYERS) as l:
                norm_squares(l, LEN, hT, x_ready, 1, l * KD)
                norm_hi(l, LEN)
                i = 0
                for u in range(PROJ_U):
                    split_hi(act, u + 2, l, U1)
                    act.wait_ge(unit_done, l * U1 + (u + 1))
                    for _ in range(U1_TILES[u]):
                        take_tile(l, i)
                        i += 1
                for s in range(MAPS + ATT_TAIL):
                    if s < MAPS:
                        exp_map(l, s)
                    if (p := head_at(s - 3)) is not None:
                        act.wait_ge(t_done, l * HEADS + (p + 1))
                        if p >= 2:
                            act.wait_ge(pv_done, l * HEADS + (p - 1))
                        act.activation(pt0[:, p % 2, :], bank[5][0:META, 0:LEN], ACT.Copy).then_inc(pt0_ready, 1)
                    if (p := head_at(s - 4)) is not None and p < DIFF_HEADS:
                        act.wait_ge(pv_done, l * HEADS + (p + 1))
                        if p >= 2:
                            act.wait_ge(msq_done, l * DIFF_HEADS + (p - 1))
                        act.activation(osb[:, p, :], bank[6 + p % 2][:, 0:LEN], ACT.Copy)
                        act.activation(sqo[:, p % 2, :], bank[6 + p % 2][:, 0:LEN], ACT.Square).then_inc(diff_taken, 1)
                    if (p := head_at(s - 5)) is not None and p >= DIFF_HEADS and p % 2:
                        mixed_hi(l, (p - DIFF_HEADS) // 2)
                    if s == MAPS:
                        act.wait_ge(msq_taken, (l + 1) * DIFF_HEADS)
                        act.activation(msb, msb, ACT.Sqrt, bias=eps[:]).then_inc(subsd_ready, 1)
                for i in range(4, KD):
                    mixed_hi(l, i)
                for u in range(PROJ_U, U1):
                    split_hi(act, u + 2, l, U1, UNITC if u + 2 >= U1 else None)
            norm_squares(2, LEN, hT, x_ready, 1, LAYERS * KD)

            def mixer(L):
                n0 = UNIT_MIX[L]

                def unit(u):
                    split_hi(act, n0 + u + 2)
                    act.wait_ge(unit_done, n0 + u + 1)

                def part(done_sem, count, out, src, func, **how):
                    act.wait_ge(done_sem, count)
                    act.activation(out, src, func, **how).then_inc(mhi_ready, 1)

                for c in range(CONV_T):
                    unit(c)
                    if c >= 2:
                        act.wait_ge(cv_taken, CONV_T * L + c - 1)
                    act.activation(sig[:, c % 2, :], bank[(2 * c + 1) % 4][:, 0:SEQ], ACT.Sigmoid).then_inc(act_taken, 1)
                unit(3)
                for c in range(POOL_T):
                    act.activation(pa[:, c, :], bank[2 + c][:, 0:SEQ], ACT.Copy).then_inc(act_taken, 1)
                for u in (4, 5):
                    unit(u)
                    for h in (2 * u - 8, 2 * u - 7):
                        act.activation(gu[0:GM_DIM, h, :], bank[h][0:GM_DIM, 0:SEQ], ACT.Copy).then_inc(act_taken, 1)
                unit(6)
                unit(7)
                for tt in range(2):
                    op = act.activation(gvj[:, tt, :], bank[4 + tt][:, 0:GM_HEADS * GM_DIM], ACT.Square, accum_out=gss[:, 0, tt:tt + 1])
                op.then_inc(vsq_ready, 1)
                act.wait_ge(vsq_ready, L + 1)
                act.activation(gss[:, 1, :], gss[:, 0, :], ACT.Sqrt, bias=eps[:], scale=1.0 / (GM_HEADS * GM_DIM)).then_inc(vsd_ready, 1)
                split_hi(act, n0 + 10)
                for c in range(POOL_T):
                    part(pool_done, L + 1, mhi[:, c, :], bank[6][:, c * SEQ:(c + 1) * SEQ], ACT.Copy, scale=pools[:, L, c:c + 1])
                for pair in range(2):
                    hs = slice(2 * pair, 2 * pair + 2)
                    part(gm_ready, 2 * L + pair + 1, mhi[0:GM_DIM, POOL_T + 2 * pair:POOL_T + 2 * pair + 2, :], gz[0:GM_DIM, hs, :], ACT.Copy)
                for c in range(CONV_T):
                    act.wait_ge(centred, CONV_T * L + c + 1)
                    act.activation(csq[:, c, :], cacc[:, c, :], ACT.Square).then_inc(csq_ready, 1)
                act.wait_ge(var_done, L + 1)
                act.activation(crs[:, 0, :], bank[6][:, 0:SEQ], ACT.Sqrt, bias=eps[:]).then_inc(csd_ready, 1)
                for c in range(CONV_T):
                    act.wait_ge(cn_ready, CONV_T * L + c + 1)
                    act.activation(csq[:, c, :], cacc[:, c, :], ACT.Silu, bias=convp[:, L, 2, c:c + 1],
                                   scale=convp[:, L, 1, c:c + 1]).then_inc(cs_ready, 1)
                for c in range(CONV_T):
                    act.wait_ge(cs_ready, CONV_T * L + c + 1)
                    act.activation(chi[:, c, :], csq[:, c, :], ACT.Copy).then_inc(chi_ready, 1)
                for f in range(CONV_T):
                    part(unit_done, n0 + PW_U + 1, mhi[:, MIX_T - CONV_T + f, :], bank[f][:, 0:SEQ], ACT.Identity, bias=convp[:, L, 3, f:f + 1])
                for d in range(KD):
                    split_hi(act, n0 + PW_U + 3 + d)

            def ffn_hi(f, t=0):
                act.wait_ge(fa_ready, t * RAW + (f + 1))
                at = slice(f, f + 1) if isinstance(t, int) else bass.ds(t * RAW + f, 1)
                act.activation(fhi[:, at, :], fa[:, f % 2:f % 2 + 1, :], ACT.Copy).then_inc(fhi_ready, 1)

            def ffn_unit(f, t=0):
                n = UNIT_FF + f
                split_hi(act, n + 2, t, RAW, UNITC)
                act.wait_ge(unit_done, t * RAW + (n + 1))
                if f >= 2:
                    act.wait_ge(fa_ready, t * RAW + (f - 1))
                act.activation(fs[:, f % 2, :], bank[f % 2][:, 0:SEQ], ACT.Silu).then_inc(fs_ready, 1)
                if f:
                    ffn_hi(f - 1, t)

            for L in range(LAYERS):
                norm_squares(3 + 2 * L, SEQ, xT, xs_ready, 1, 2 * L * KD)
                norm_hi(SPLIT_OUTPUTS[3 + 2 * L], SEQ)
                mixer(L)
                norm_squares(4 + 2 * L, SEQ, xT, xs_ready, 1, (2 * L + 1) * KD)
                if L == 0:
                    norm_hi(SPLIT_OUTPUTS[4], SEQ)
                    for f in range(LEAD):
                        ffn_unit(f)
                    with act.Fori(0, (FF_T - LEAD) // RAW) as t:
                        for j in range(RAW):
                            ffn_unit(LEAD + j, t)
                    ffn_hi(FF_T - 1)
                    for j in range(LEAD):
                        split_hi(act, UNIT_FF + FF_T + j + 2)
                    with act.Fori(0, (2 * KD - LEAD) // RAW) as t:
                        for j in range(LEAD, LEAD + RAW):
                            split_hi(act, UNIT_FF + FF_T + j + 2, t, RAW, UNITC)

            act.wait_ge(un_ready, KD)
            act.activation(yt[:], one[:].to_broadcast([P, D]), ACT.Copy, scale=0.0).then_inc(yt_ready, 1)
            act.activation(gpickT[:].rearrange("p a t -> p (a t)"), one[:].to_broadcast([P, 2 * P]), ACT.Copy, scale=0.0).then_inc(gpickT_ready, 1)
            for i in range(4):
                act.wait_ge(nt_done, i + 1)
                act.activation(nhi[:, i // 2, (i % 2) * 512:(i % 2 + 1) * 512], bank[2 + i][:], ACT.Copy).then_inc(nhi_ready, 1)
            act.wait_ge(tw_diff, 1)
            act.activation(tw[:, 1, :], tw[:, 0, :], ACT.Exp).then_inc(tw_exp, 1)

            def gathered_hi(half, g):
                act.wait_ge(gather_done, g * 2 + (half + 1))
                act.activation(hthi[:, 4 * half:4 * half + 4, :], bank[7][:].rearrange("p (k t) -> p k t", k=4), ACT.Copy).then_inc(hthi_ready, 1)

            def expert(it):
                def rows_hi(c):
                    act.wait_ge(at_done, it * CHUNKS + (c + 1))
                    act.activation(athi[:], bank[4][:].rearrange("p (k t) -> p k t", k=4), ACT.Copy).then_inc(athi_ready, 1)

                for pos, (kind, c, part) in enumerate(EXPERT_UNITS):
                    split_hi(act, UNIT_MOE + pos + 2, it, UM)
                    if part == 0:
                        continue
                    if kind == "gate":
                        act.wait_ge(unit_done, it * UM + (UNIT_MOE + pos + 1))
                        if c >= 2:
                            act.wait_ge(a_ready, it * CHUNKS + (c - 1))
                        act.activation(gs[:, c % 2, :], bank[c % 2][:], ACT.Silu).then_inc(silu_ready, 1)
                        if c:
                            rows_hi(c - 1)
                    if kind == "up" and c == 5:
                        act.wait_ge(gpickT_done, it + 1)
                        act.activation(gpickT[:].rearrange("p a t -> p (a t)"), bank[7][:, 0:2 * P], ACT.Copy).then_inc(gpickT_ready, 1)
                    if kind == "up" and c == CHUNKS - 1:
                        gathered_hi(0, it + 1)
                    if kind == "down" and c == CHUNKS - 2:
                        rows_hi(CHUNKS - 1)
                        gathered_hi(1, it + 1)
                    if kind == "down" and c == CHUNKS - 1:
                        act.wait_ge(unit_done, it * UM + (UNIT_MOE + pos + 1))
                        act.activation(yt[:, 0:512], bank[5][:], ACT.Copy)
                        act.activation(yt[:, 512:D], bank[6][:], ACT.Copy).then_inc(yt_ready, 1)

            gathered_hi(0, 0)
            gathered_hi(1, 0)
            with act.Fori(0, EXPERTS) as it:
                expert(it)
            act.wait_ge(count_ready, 1)
            fullest = act.value_load(cnti[0:1, 0:1], min_val=0, max_val=SEQ)
            with act.If(fullest > P):
                with act.Fori(EXPERTS, 2 * EXPERTS) as it:
                    expert(it)
            norm_squares(7, SEQ, xT, last_taken, 2)
            for i in range(4):
                act.wait_ge(ot_done, i + 1)
                act.activation(outn[:, i // 2, (i % 2) * 512:(i % 2 + 1) * 512], bank[i][:], ACT.Copy).then_inc(ot_ready, 1)

        @block.vector
        def _(dve):
            def norm_scale(q):
                dve.wait_ge(sd_ready, q + 1)
                dve.reciprocal(rstd[:], sd[:]).then_inc(rstd_ready, 1)
                dve.wait_ge(rstd_ready, q + 1)

            def normed(q, out, source, k, n, ready):
                gain = gains[:, q:q + 1, k] if isinstance(q, int) else gains[:, bass.ds(q, 1), k]
                dve.scalar_tensor_tensor(out, source, gain, rstd[:, 0:n], ALU.mult, ALU.mult).then_inc(ready, 1)

            def norm_split(q, order, source, n):
                norm_scale(q)
                for k in range(KD + 1):
                    if 2 <= k < KD:
                        dve.wait_ge(ulo_ready, order * KD + (k - 1))
                    if k < KD:
                        normed(q, ut[:, k % 2, 0:n], source[:, k, 0:n], k, n, u_ready)
                    if k:
                        dve.wait_ge(uhi_ready, order * KD + k)
                        dve.tensor_tensor(ulo[:, k - 1, 0:n], ut[:, (k - 1) % 2, 0:n], uhi[:, k - 1, 0:n].bitcast(F32),
                                          ALU.subtract).then_inc(ulo_ready, 1)

            for tile, value in ((mean_d, 1.0 / D), (mean_h, 1.0 / P), (mean_c, 1.0 / (CONV_T * P)), (ones, 1.0), (eps, EPS),
                                (sd, 1.0), (sums, 1.0)):
                dve.memset(tile[:], value)
            dve.memset(one[:], 1.0).then_inc(const_ready, 1)
            dve.wait_ge(in_landed, 16)
            for k in range(KD):
                dve.tensor_copy(hT[:, k, :], h_in[:, k, :]).then_inc(x_ready, 1)
            split_lo(dve, 0)
            split_lo(dve, 1)
            dve.wait_ge(lam_landed, 16)
            for l in range(LAYERS):
                for i in range(2):
                    dve.tensor_tensor_reduce(rsn[:, 0:HEAD], lamv[:, l, 2 * i, :], lamv[:, l, 2 * i + 1, :], 1.0, 0.0,
                                             ALU.mult, ALU.add, lamp[:, l, i:i + 1]).then_inc(lam_step, 1)
                    dve.wait_ge(lam_step, 2 * l + i + 1)
            dve.wait_ge(lam_exp, 1)
            dve.tensor_tensor(lamd[:], lame[:, :, 0], lame[:, :, 1], ALU.subtract).then_inc(lam_ready, 1)
            dve.wait_ge(lam_ready, 1)
            dve.wait_ge(par_landed, 16 * N_PAR)
            for l in range(LAYERS):
                dve.tensor_scalar(lam[:, l:l + 1], lamd[:, l:l + 1], LAMBDA_INIT[l], None, ALU.add).then_inc(lam_ready, 1)
                dve.tensor_scalar(subg[:, l, :], subln[:, l, :], 1.0 - LAMBDA_INIT[l], None, ALU.mult).then_inc(lam_ready, 1)
            dve.wait_ge(lam_ready, 1 + 2 * LAYERS)

            def turned(l, i):
                if i == LOGIT_T:
                    dve.wait_ge(logit_step, 3 * l + 3)
                    dve.scalar_tensor_tensor(lf, xb, 0.0, ll, ALU.min, ALU.subtract).then_inc(lf_ready, 1)
                    dve.wait_ge(lf_ready, l + 1)
                    dve.tensor_tensor_scan(cum[:], one[0:FOX_HEADS, :].to_broadcast([FOX_HEADS, LEN]), lf, 0.0,
                                           ALU.mult, ALU.add).then_inc(cum_ready, 1)
                    dve.wait_ge(cum_ready, 2 * l + 1)
                    dve.tensor_scalar(ncum[:], cum[:], -1.0, None, ALU.mult).then_inc(cum_ready, 1)
                elif QK_T <= i < QK_T + ROPED:
                    r = i - QK_T
                    dve.wait_ge(rot_done, l * ROPED + (r + 1))
                    if r:
                        dve.wait_ge(roped, l * ROPED + r)
                    dve.tensor_tensor(rsn[:], bank[4 + r % 2][:, 0:LEN], rope[:, 2 * (r // 4) + 1, :], ALU.mult).then_inc(rot_taken, 1)
                    dve.wait_ge(rot_taken, l * ROPED + (r + 1))
                    dve.wait_ge(rc_ready, l * ROPED + (r + 1))
                    dve.tensor_tensor(qk[:, r, :], rc[:, r % 2, :], rsn[:], ALU.add).then_inc(roped, 1)
                elif i >= V_T:
                    v = i - V_T
                    dve.wait_ge(vt_done, l * VN + (v + 1))
                    b = bank[6 + v % 2]
                    dve.tensor_copy(v0[:, v, :], b[0:META, 0:P])
                    dve.tensor_copy(v12[:, v, :, :], b[:, P:3 * P].rearrange("p (t d) -> p t d", t=2)).then_inc(v_ready, 1)

            def mask_map(l, m):
                dve.wait_ge(s_done, l * MAPS + (m + 1))
                if m >= 2:
                    dve.wait_ge(exp_done, l * MAPS + (m - 1))
                dve.memset(held[:, m % 4:m % 4 + 1], 0.0)
                masks = mask[0:META, META + P:2 * META + P], mask[:, P:LEN], mask[:, :]
                for t, (q0, rows, c0, keys) in enumerate(QTILES):
                    op = dve.tensor_tensor_reduce(sm[0:rows, m % 2, c0:c0 + keys], bank[m % 3][0:rows, c0:c0 + keys], masks[t], 1.0, NEG,
                                                  ALU.add, ALU.min, nmax[0:rows, m % 4, t:t + 1])
                op.then_inc(masked, 1)

            def map_scales(l, m):
                dve.wait_ge(exp_done, l * MAPS + (m + 1))
                dve.reciprocal(rsum[:, m % 4, :], sums[:, m % 4, :]).then_inc(rsum_ready, 1)
                if m < 2 * DIFF_HEADS and m % 2:
                    dve.wait_ge(rsum_ready, l * MAPS + (m + 1))
                    dve.tensor_scalar(rlam[:, (m // 2) % 2, :], rsum[:, m % 4, :], lam[:, bass.ds(l, 1)], None, ALU.mult).then_inc(rlam_ready, 1)

            def difference(l, p):
                dve.wait_ge(pd_ready, l * DIFF_HEADS + (p + 1))
                if p >= 2:
                    dve.wait_ge(t_done, l * HEADS + (p - 1))
                m = 2 * p
                for t, (q0, rows, c0, keys) in enumerate(QTILES):
                    cols = slice(c0, c0 + keys)
                    op = dve.scalar_tensor_tensor(pr[0:rows, p % 2, cols], ex[0:rows, m % 4, cols], rsum[0:rows, m % 4, t:t + 1], pd[0:rows, cols],
                                                  ALU.mult, ALU.subtract)
                op.then_inc(diff_p, 1)

            def mixed_lo(l, i):
                dve.wait_ge(mixhi_ready, l * KD + (i + 1))
                dve.tensor_tensor(ulo[:, MIX_ORDER[i], :], mx32[:, i % 2, :], uhi[:, MIX_ORDER[i], :].bitcast(F32),
                                  ALU.subtract).then_inc(mixlo_ready, 1)

            with dve.Fori(0, LAYERS) as l:
                norm_split(l, l, hT, LEN)
                i = 0
                for u in range(PROJ_U):
                    split_lo(dve, u + 2, l, U1)
                    for _ in range(U1_TILES[u]):
                        turned(l, i - TURN_LAG)
                        i += 1
                for i in range(PROJ_T - TURN_LAG, PROJ_T):
                    turned(l, i)
                for s in range(MAPS + ATT_TAIL):
                    if s < MAPS:
                        mask_map(l, s)
                    if 1 <= s <= MAPS:
                        map_scales(l, s - 1)
                    if (p := head_at(s - 2)) is not None and p < DIFF_HEADS:
                        difference(l, p)
                    if (p := head_at(s - 3)) is not None:
                        dve.wait_ge(t_done, l * HEADS + (p + 1))
                        if p >= 2:
                            dve.wait_ge(pv_done, l * HEADS + (p - 1))
                        dve.tensor_copy(pt1[:, p % 2, :], bank[4][:, 0:KEYS1 + P]).then_inc(pt1_ready, 1)
                    if (p := head_at(s - 5)) is not None and p >= DIFF_HEADS and p % 2:
                        i = (p - DIFF_HEADS) // 2
                        o = DIFF_HEADS + i
                        dve.wait_ge(pv_done, l * HEADS + (p + 1))
                        if i >= 2:
                            dve.wait_ge(mixlo_ready, l * KD + (i - 1))
                        dve.tensor_tensor(mx32[:, i % 2, :], bank[6 + o % 2][:, 0:LEN], zs[:, o, :], ALU.mult).then_inc(fox_mixed, 1)
                    if (p := head_at(s - 6)) is not None:
                        if p < DIFF_HEADS:
                            dve.wait_ge(msq_done, l * DIFF_HEADS + (p + 1))
                            dve.tensor_copy(msb[:, p, :], bank[3][:, 0:LEN]).then_inc(msq_taken, 1)
                        elif p % 2:
                            mixed_lo(l, (p - DIFF_HEADS) // 2)
                    if s == MAPS + 1:
                        dve.wait_ge(subsd_ready, l + 1)
                        dve.reciprocal(msb, msb).then_inc(subrs_ready, 1)
                dve.wait_ge(subrs_ready, l + 1)
                for h in range(DIFF_HEADS + 1):
                    i = DIFF_HEADS + h
                    if h < DIFF_HEADS:
                        dve.scalar_tensor_tensor(ut[:, h % 2, :], osb[:, h, :], subg[:, bass.ds(l, 1), h], msb[:, h, :],
                                                 ALU.mult, ALU.mult).then_inc(sub_ready, 1)
                        dve.wait_ge(sub_ready, l * DIFF_HEADS + (h + 1))
                        dve.wait_ge(mixlo_ready, l * KD + (i - 1))
                        dve.tensor_tensor(mx32[:, i % 2, :], ut[:, h % 2, :], zs[:, h, :], ALU.mult).then_inc(diff_mixed, 1)
                    if h:
                        mixed_lo(l, i - 1)
                for u in range(PROJ_U, U1):
                    split_lo(dve, u + 2, l, U1, UNITC if u + 2 >= U1 else None)
                    dve.wait_ge(unit_done, l * U1 + (u + 1))
                    for d in out_tiles(u):
                        dve.tensor_tensor(hT[:, d, :], hT[:, d, :], bank[d % 4][:, 0:LEN], ALU.add).then_inc(x_ready, 1)
            norm_scale(2)
            for k in range(KD):
                dve.scalar_tensor_tensor(xT[:, k, :], hT[:, k, META:LEN], gains[:, 2, k:k + 1], rstd[:, META:LEN],
                                         ALU.mult, ALU.mult).then_inc(xs_ready, 1)

            def conv_taps(L, a, b):
                for i in range(a, min(b, CONV_T * TAPS)):
                    c, k = divmod(i, TAPS)
                    window, w = hpad[:, c, k:k + SEQ], convw[:, L, c, k:k + 1]
                    acc = csq if k % 2 else cacc
                    count = L * CONV_T * TAPS + i
                    if k == 0:
                        dve.wait_ge(cv_taken, CONV_T * L + c + 1)
                        op = dve.tensor_scalar(acc[:, c, :], window, w, convp[:, L, 0, c:c + 1], ALU.mult, ALU.add)
                    elif k == 1:
                        op = dve.tensor_scalar(acc[:, c, :], window, w, None, ALU.mult)
                    else:
                        dve.wait_ge(tap_done, count - 1)
                        op = dve.scalar_tensor_tensor(acc[:, c, :], window, w, acc[:, c, :], ALU.mult, ALU.add)
                    op.then_inc(tap_done, 1)
                    if k == TAPS - 1:
                        dve.wait_ge(tap_done, count + 1)
                        dve.tensor_tensor(cacc[:, c, :], cacc[:, c, :], csq[:, c, :], ALU.add).then_inc(conv_ready, 1)

            def mixer(L):
                n0 = UNIT_MIX[L]
                done = 0
                for u in range(8):
                    split_lo(dve, n0 + u + 2)
                    if u < CONV_T:
                        dve.wait_ge(act_taken, ACT_TAKES * L + u + 1)
                        dve.tensor_tensor(hpad[:, u, PADC:], bank[2 * u % 4][:, 0:SEQ], sig[:, u % 2, :], ALU.mult).then_inc(cv_taken, 1)
                    if u == 0:
                        dve.wait_ge(par2_landed, 16 * PAR2)
                        dve.wait_ge(const2_ready, CONST2 + 2 * L)
                    if u == 4:
                        for c in range(POOL_T):
                            dve.wait_ge(act_taken, ACT_TAKES * L + CONV_T + c + 1)
                            dve.tensor_tensor_scan(pc[:, c, PADP:], one[:].to_broadcast([P, SEQ]), pa[:, c, :], 0.0,
                                                   ALU.mult, ALU.add).then_inc(scan_ready, 1)
                    conv_taps(L, done, done + TAP_STEP)
                    done += TAP_STEP
                dve.wait_ge(vsd_ready, L + 1)
                dve.reciprocal(gss[:, 2, :], gss[:, 1, :]).then_inc(vrs_ready, 1)
                dve.wait_ge(vrs_ready, L + 1)
                for tt in range(2):
                    dve.scalar_tensor_tensor(gv[:, tt, :], bank[4 + tt][:, 0:GM_HEADS * GM_DIM], gss[:, 2, tt:tt + 1], gmg[:, L, :],
                                             ALU.mult, ALU.mult).then_inc(vn_ready, 1)
                split_lo(dve, n0 + 10)

                def hi_there(i):
                    dve.wait_ge(mhi_ready, MIX_SPLITS * L + i + 1)

                hi_there(POOL_T - 1)
                for c in range(POOL_T):
                    dve.scalar_tensor_tensor(mlo[:, c, :], bank[6][:, c * SEQ:(c + 1) * SEQ], pools[:, L, c:c + 1], mhi[:, c, :].bitcast(F32),
                                             ALU.mult, ALU.subtract).then_inc(mlo_ready, 1)
                for pair in range(2):
                    hs = slice(2 * pair, 2 * pair + 2)
                    z = bank[4 if pair else 7][0:GM_DIM, :].rearrange("p (h t) -> p h t", h=2)
                    dve.wait_ge(z_done, 2 * L + pair + 1)
                    dve.tensor_tensor(gz[0:GM_DIM, hs, :], z, gmb[0:GM_DIM, L, hs, :], ALU.add).then_inc(zb_ready, 1)
                for pair in range(2):
                    hs = slice(2 * pair, 2 * pair + 2)
                    dve.wait_ge(zb_ready, 2 * L + pair + 1)
                    dve.tensor_tensor(gz[0:GM_DIM, hs, :], gz[0:GM_DIM, hs, :], gu[0:GM_DIM, hs, :], ALU.mult).then_inc(gm_ready, 1)
                dve.wait_ge(mean_done, L + 1)
                for c in range(CONV_T):
                    dve.tensor_tensor(cacc[:, c, :], cacc[:, c, :], bank[5][:, 0:SEQ], ALU.subtract).then_inc(centred, 1)
                for pair in range(2):
                    hi_there(POOL_T + pair)
                    ms = slice(POOL_T + 2 * pair, POOL_T + 2 * pair + 2)
                    dve.tensor_tensor(mlo[0:GM_DIM, ms, :], gz[0:GM_DIM, 2 * pair:2 * pair + 2, :], mhi[0:GM_DIM, ms, :].bitcast(F32),
                                      ALU.subtract).then_inc(mlo_ready, 1)
                dve.wait_ge(csd_ready, L + 1)
                dve.reciprocal(crs[:, 1, :], crs[:, 0, :]).then_inc(crs_ready, 1)
                dve.wait_ge(crs_ready, L + 1)
                for c in range(CONV_T):
                    dve.tensor_tensor(cacc[:, c, :], cacc[:, c, :], crs[:, 1, :], ALU.mult).then_inc(cn_ready, 1)
                for c in range(CONV_T):
                    dve.wait_ge(chi_ready, CONV_T * L + c + 1)
                    dve.tensor_tensor(clo[:, c, :], csq[:, c, :], chi[:, c, :].bitcast(F32), ALU.subtract).then_inc(clo_ready, 1)
                for f in range(CONV_T):
                    hi_there(POOL_T + 2 + f)
                    dve.scalar_tensor_tensor(mlo[:, MIX_T - CONV_T + f, :], bank[f][:, 0:SEQ], convp[:, L, 3, f:f + 1],
                                             mhi[:, MIX_T - CONV_T + f, :].bitcast(F32), ALU.add, ALU.subtract).then_inc(mlo_ready, 1)
                for d in range(KD):
                    split_lo(dve, n0 + PW_U + 3 + d)
                    dve.wait_ge(unit_done, n0 + PW_U + 2 + d)
                    dve.tensor_tensor(xT[:, d, :], xT[:, d, :], bank[d % 4][:, 0:SEQ], ALU.add).then_inc(xs_ready, 1)

            def ffn_lo(f, t=0):
                dve.wait_ge(fhi_ready, t * RAW + (f + 1))
                at = slice(f, f + 1) if isinstance(t, int) else bass.ds(t * RAW + f, 1)
                dve.tensor_tensor(flo[:, at, :], fa[:, f % 2:f % 2 + 1, :], fhi[:, at, :].bitcast(F32), ALU.subtract).then_inc(flo_ready, 1)

            def ffn_unit(f, t=0):
                split_lo(dve, UNIT_FF + f + 2, t, RAW, UNITC)
                dve.wait_ge(fs_ready, t * RAW + (f + 1))
                if f >= 2:
                    dve.wait_ge(flo_ready, t * RAW + (f - 1))
                dve.tensor_tensor(fa[:, f % 2, :], fs[:, f % 2, :], bank[2 + f % 2][:, 0:SEQ], ALU.mult).then_inc(fa_ready, 1)
                if f:
                    ffn_lo(f - 1, t)

            def ffn_add(d, t=0):
                n = UNIT_FF + FF_T + 2 * d
                for half in range(2):
                    split_lo(dve, n + half + 2, t, RAW, UNITC if not isinstance(t, int) else None)
                dve.wait_ge(unit_done, t * RAW + (n + 2))
                at = slice(d, d + 1) if isinstance(t, int) else bass.ds(t * (RAW // 2) + d, 1)
                dve.tensor_tensor(xT[:, at, :], xT[:, at, :], bank[4 + d % 3][:, 0:SEQ].rearrange("p (a t) -> p a t", a=1), ALU.add).then_inc(xs_ready, 1)

            for L in range(LAYERS):
                norm_split(3 + 2 * L, SPLIT_OUTPUTS[3 + 2 * L], xT, SEQ)
                mixer(L)
                if L == 0:
                    norm_split(4, SPLIT_OUTPUTS[4], xT, SEQ)
                    for f in range(LEAD):
                        ffn_unit(f)
                    with dve.Fori(0, (FF_T - LEAD) // RAW) as t:
                        for j in range(RAW):
                            ffn_unit(LEAD + j, t)
                    ffn_lo(FF_T - 1)
                    for d in range(LEAD // 2):
                        ffn_add(d)
                    with dve.Fori(0, (2 * KD - LEAD) // RAW) as t:
                        for j in range(RAW // 2):
                            ffn_add(LEAD // 2 + j, t)

            norm_scale(6)
            for k in range(KD):
                normed(6, un[:, k, :], xT[:, k, :], k, SEQ, un_ready)
            dve.memset(rank[:], -1.0).then_inc(rank_zero, 1)
            steps = 0

            def step(op):
                nonlocal steps
                steps += 1
                op.then_inc(route_step, 1)
                dve.wait_ge(route_step, steps)

            dve.wait_ge(lg_done, 1)
            for tt in range(2):
                step(dve.tensor_copy(lg[:, tt, :], bank[tt][:, 0:EXPERTS]))
                step(dve.max(top[:, tt, :], lg[:, tt, :]))
                step(dve.max_index(topi[:, tt, :], top[:, tt, :], lg[:, tt, :]))
                step(dve.tensor_copy(topf[:, tt, :], topi[:, tt, :]))
            dve.tensor_tensor(tw[:, 0, :], top[:, :, 1], top[:, :, 0], ALU.subtract).then_inc(tw_diff, 1)
            for tt in range(2):
                for j in range(TOP_K):
                    step(dve.tensor_scalar(oh[:, tt, j, :], iota[:, 0:EXPERTS], topf[:, tt, j:j + 1], None, ALU.is_equal))
                dve.tensor_tensor(chosen[:, tt, :], oh[:, tt, 0, :], oh[:, tt, 1, :], ALU.add).then_inc(chosen_ready, 1)
            dve.wait_ge(tw_exp, 1)
            step(dve.tensor_scalar(tw[:, 2, :], tw[:, 1, :], 1.0, None, ALU.add))
            step(dve.reciprocal(tw[:, 2, :], tw[:, 2, :]))
            step(dve.tensor_tensor(tw[:, 3, :], tw[:, 1, :], tw[:, 2, :], ALU.mult))
            dve.wait_ge(chosen_ready, 2)
            for tt in range(2):
                step(dve.tensor_scalar(gate[:, tt, 0:EXPERTS], oh[:, tt, 0, :], tw[:, 2, tt:tt + 1], None, ALU.mult))
                step(dve.scalar_tensor_tensor(gate[:, tt, 0:EXPERTS], oh[:, tt, 1, :], tw[:, 3, tt:tt + 1], gate[:, tt, 0:EXPERTS], ALU.mult, ALU.add))
                step(dve.tensor_copy(gate[:, tt, EXPERTS:], gate[:, tt, 0:EXPERTS]))
            step(dve.tensor_scalar(big[:], chosen[:], FAR, -FAR, ALU.mult, ALU.add))
            dve.wait_ge(rank_done, 1)
            dve.wait_ge(rank_zero, 1)
            for tt in range(2):
                step(dve.tensor_tensor(rank[:, tt, 0:EXPERTS], bank[6][:, tt * EXPERTS:(tt + 1) * EXPERTS], big[:, tt, :], ALU.add))
                step(dve.tensor_scalar(rank[:, tt, EXPERTS:2 * EXPERTS], rank[:, tt, 0:EXPERTS], float(-P), None, ALU.add))
            step(dve.tensor_reduce(cnt[:], bank[6][:, 2 * EXPERTS:3 * EXPERTS], AXX, ALU.max))
            dve.tensor_copy(cnti[:], cnt[:]).then_inc(count_ready, 1)

            def select(g):
                for tt in range(2):
                    r = rank[:, tt, g:g + 1] if isinstance(g, int) else rank[:, tt, bass.ds(g, 1)]
                    op = dve.tensor_scalar(pick[:, tt, :], iota[:], r, None, ALU.is_equal)
                op.then_inc(pick_ready, 1)

            def gathered_lo(half, g):
                dve.wait_ge(hthi_ready, g * 2 + (half + 1))
                ks = slice(4 * half, 4 * half + 4)
                dve.tensor_tensor(htlo[:, ks, :], bank[7][:].rearrange("p (k t) -> p k t", k=4), hthi[:, ks, :].bitcast(F32),
                                  ALU.subtract).then_inc(htlo_ready, 1)

            def scatter_add(r, done, count, taken):
                dve.wait_ge(done, count)
                tiles = xT[:, 2 * r:2 * r + 2, :]
                dve.tensor_tensor(tiles, tiles, bank[7][:].rearrange("p (k t) -> p k t", k=2), ALU.add).then_inc(taken, 1)

            def expert(it):
                def rows_lo(c):
                    dve.wait_ge(athi_ready, it * CHUNKS + (c + 1))
                    dve.tensor_tensor(atlo[:], bank[4][:].rearrange("p (k t) -> p k t", k=4), athi[:].bitcast(F32),
                                      ALU.subtract).then_inc(atlo_ready, 1)

                for pos, (kind, c, part) in enumerate(EXPERT_UNITS):
                    split_lo(dve, UNIT_MOE + pos + 2, it, UM)
                    if kind == "gate" and part == 0 and 1 <= c <= 4:
                        scatter_add(c - 1, scat_done, it * 4 + c, scat_taken)
                        if c == 4:
                            for tt in range(2):
                                at = bass.ds(it, 1)
                                op = dve.tensor_scalar(gpick[:, tt, :], iota[:], rank[:, tt, at], gate[:, tt, at], ALU.is_equal, ALU.mult)
                            op.then_inc(gpick_ready, 1)
                    if part == 0:
                        continue
                    if kind == "gate" and c:
                        rows_lo(c - 1)
                    if kind == "up":
                        dve.wait_ge(silu_ready, it * CHUNKS + (c + 1))
                        dve.wait_ge(unit_done, it * UM + (UNIT_MOE + pos + 1))
                        if c >= 2:
                            dve.wait_ge(at_done, it * CHUNKS + (c - 1))
                        dve.tensor_tensor(ga[:, c % 2, :], gs[:, c % 2, :], bank[2 + c % 2][:], ALU.mult).then_inc(a_ready, 1)
                        if c == 5:
                            select(it + 1)
                        if c == CHUNKS - 1:
                            gathered_lo(0, it + 1)
                    if kind == "down" and c == CHUNKS - 2:
                        rows_lo(CHUNKS - 1)
                        gathered_lo(1, it + 1)

            for i in range(4):
                dve.wait_ge(nhi_ready, i + 1)
                cols = slice((i % 2) * 512, (i % 2 + 1) * 512)
                dve.tensor_tensor(nlo[:, i // 2, cols], bank[2 + i][:], nhi[:, i // 2, cols].bitcast(F32), ALU.subtract).then_inc(nlo_ready, 1)
            select(0)
            gathered_lo(0, 0)
            gathered_lo(1, 0)
            with dve.Fori(0, EXPERTS) as it:
                expert(it)
            dve.wait_ge(count_ready, 1)
            fullest = dve.value_load(cnti[0:1, 0:1], min_val=0, max_val=SEQ)
            with dve.If(fullest > P):
                with dve.Fori(EXPERTS, 2 * EXPERTS) as it:
                    expert(it)
            for r in range(4):
                scatter_add(r, last_done, r + 1, last_taken)
            norm_scale(7)
            for k in range(KD):
                normed(7, un[:, k, :], xT[:, k, :], k, SEQ, result_ready)

        @block.gpsimd
        def _(pool):
            def scaled(out, src, by):
                if out.shape[0] < P:
                    return pool.tensor_tensor(out, src, by.to_broadcast(out.shape), ALU.mult)
                return pool.tensor_scalar(out, src, by, None, ALU.mult)

            pool.wait_ge(par_landed, 16 * N_PAR)
            with pool.Fori(0, LAYERS) as l:
                for r in range(ROPED):
                    pool.wait_ge(proj_taken, l * PROJ_T + (QK_T + r + 1))
                    if r >= 2:
                        pool.wait_ge(roped, l * ROPED + (r - 1))
                    pool.tensor_tensor(rc[:, r % 2, :], qraw[:, r % 2, :], rope[:, 2 * (r // 4), :], ALU.mult).then_inc(rc_ready, 1)
                for p in range(DIFF_HEADS):
                    pool.wait_ge(rlam_ready, l * DIFF_HEADS + (p + 1))
                    if p:
                        pool.wait_ge(diff_p, l * DIFF_HEADS + p)
                    m = 2 * p + 1
                    for t, (q0, rows, c0, keys) in enumerate(QTILES):
                        op = scaled(pd[0:rows, c0:c0 + keys], ex[0:rows, m % 4, c0:c0 + keys], rlam[0:rows, p % 2, t:t + 1])
                    op.then_inc(pd_ready, 1)
                for f in range(FOX_HEADS):
                    m, p = 2 * DIFF_HEADS + f, DIFF_HEADS + f
                    pool.wait_ge(rsum_ready, l * MAPS + (m + 1))
                    pool.wait_ge(t_done, l * HEADS + (p - 1))
                    for t, (q0, rows, c0, keys) in enumerate(QTILES):
                        op = scaled(pr[0:rows, p % 2, c0:c0 + keys], ex[0:rows, m % 4, c0:c0 + keys], rsum[0:rows, m % 4, t:t + 1])
                    op.then_inc(fox_p, 1)

            pool.wait_ge(xs_ready, KD)
            params = ((convw, "convw"), (convp, "convp"), (pools, "pools"), (poolr, "poolr"), (poolw, "poolw"), (gmg, "gmg"), (gmb, "gmb"),
                      (wsT, "wsT"), (router, "router"), (lt, "lt"), (iota, "iota"))
            for dst, name in params:
                pool.dma_start(dst[:], io[name]).then_inc(par2_landed, 16)

            def zero_pads():
                pool.memset(hpad[:, :, 0:PADC], 0.0).then_inc(const2_ready, 1)
                pool.memset(pc[:, :, 0:PADP], 0.0).then_inc(const2_ready, 1)

            zero_pads()
            pool.wait_ge(par2_landed, 16 * PAR2)
            pool.wait_ge(const2_ready, 2)
            pool.memset(wsT[GM_CHUNK:P, :, :, 0:GM_CHUNK], 0.0).then_inc(const2_ready, 1)
            for L in range(LAYERS):
                if L:
                    pool.wait_ge(xs_ready, 3 * KD)
                    zero_pads()
                for c in range(POOL_T):
                    pool.wait_ge(scan_ready, POOL_T * L + c + 1)
                    if L:
                        pool.wait_ge(pool_done, L)
                    if c:
                        pool.wait_ge(pool_ready, POOL_T * L + c)
                    for g in (2 * c, 2 * c + 1):
                        part, win = slice(64 * (g % 2), 64 * (g % 2) + 64), POOL_WINDOWS[g]
                        pool.tensor_tensor(py[part, c, :], pc[part, c, PADP:PADP + SEQ], pc[part, c, PADP - win:PADP - win + SEQ],
                                           ALU.subtract).then_inc(pool_step, 1)
                    pool.wait_ge(pool_step, 3 * POOL_T * L + 3 * c + 2)
                    pool.tensor_tensor(py[:, c, :], py[:, c, :], poolr[:, c, :], ALU.mult).then_inc(pool_step, 1)
                    pool.wait_ge(pool_step, 3 * POOL_T * L + 3 * c + 3)
                    pool.tensor_tensor(py[:, c, :], py[:, c, :], pa[:, c, :], ALU.subtract).then_inc(pool_ready, 1)

    return nc


def columns(w, c0, c1):
    return w[:, c0:c1].reshape(-1, P, c1 - c0).transpose(1, 0, 2)


def lay_out(a):
    f32 = np.float32
    io = {"hT": np.concatenate([a["meta_tokens"], a["x"][0]]).T.reshape(KD, P, LEN).transpose(1, 0, 2)}

    w = np.zeros((UNIT_MOE, P, UNITC), f32)

    def put(n, part, at=0):
        flat = part.reshape(part.shape[0], -1)
        w[n, :part.shape[0], at:at + flat.shape[1]] = flat

    half = MIXW // 2
    dq, dk, dv, dz, fq, fk, fv, fz, fl = (half * i for i in range(9))
    order = [dz, fz, fl, dq, dk, fq, fk, dv, fv]
    tiles = [s + P * i for s in order for i in range(1 if s == fl else 4)]
    for l in range(LAYERS):
        w_in = np.pad(a["w_in"][l], ((0, 0), (0, fl + P - a["w_in"].shape[2])))
        i = 0
        for u in range(U1):
            if u < PROJ_U:
                starts = tiles[i:i + U1_TILES[u]]
                i += U1_TILES[u]
                put(l * U1 + u, np.concatenate([columns(w_in, s, s + P) for s in starts], axis=2))
        d = 0
        for u in range(PROJ_U, U1):
            put(l * U1 + u, columns(a["w_out"][l], d * P, (d + U1_TILES[u]) * P))
            d += U1_TILES[u]
        n = UNIT_MIX[l]
        win2, wout2 = a["w_in_2"][l], a["w_out_2"][l]
        pool_w, gm_w, conv_w = POOL_T * P, GM_HEADS * GM_DIM, CONV_T * P
        at_a, at_u, at_v = 0, pool_w, pool_w + gm_w
        at_cv, at_cg = at_v + gm_w, at_v + gm_w + conv_w
        for c in range(CONV_T):
            put(n + c, np.concatenate([columns(win2, s + c * P, s + (c + 1) * P) for s in (at_cv, at_cg)], axis=2))
        put(n + 3, columns(win2, at_a, at_a + pool_w))
        for s in range(2):
            put(n + 4 + s, columns(win2, at_u + s * gm_w // 2, at_u + (s + 1) * gm_w // 2))
            put(n + 6 + s, columns(win2, at_v + s * gm_w // 2, at_v + (s + 1) * gm_w // 2))
        put(n + PW_U, columns(a["conv_pw_w_2"][l], 0, conv_w))
        rows = [(i * P, P) for i in range(POOL_T)] + [(pool_w + i * GM_DIM, GM_DIM) for i in range(GM_HEADS)]
        rows += [(pool_w + gm_w + i * P, P) for i in range(CONV_T)]
        for dd in range(KD):
            for i, (r0, nr) in enumerate(rows):
                put(n + PW_U + 1 + dd, wout2[r0:r0 + nr, dd * P:(dd + 1) * P], i * P)
    for f in range(FF_T):
        put(UNIT_FF + f, np.concatenate([columns(a[name][0], f * P, (f + 1) * P) for name in ("ffn_wg_2", "ffn_wu_2")], axis=2))
    for i in range(2 * KD):
        d, h = divmod(i, 2)
        put(UNIT_FF + FF_T + i, columns(a["ffn_wd_2"][0][h * FF_HALF * P:(h + 1) * FF_HALF * P], d * P, (d + 1) * P))
    io["w"] = w

    wm = np.empty((EXPERTS, UM, P, UNITC), f32)
    for j, (kind, c, part) in enumerate(EXPERT_UNITS):
        if kind == "down":
            r0 = c * CHUNK + part * 2 * P
            block = a["moe_wd_2"][0][:, r0:r0 + 2 * P, :].reshape(EXPERTS, 2, P, D)
        else:
            m = a["moe_wg_2" if kind == "gate" else "moe_wu_2"][0]
            block = m[:, part * 512:(part + 1) * 512, c * CHUNK:(c + 1) * CHUNK].reshape(EXPERTS, 4, P, CHUNK)
        wm[:, j] = block.transpose(0, 2, 1, 3).reshape(EXPERTS, P, UNITC)
    io["wm"] = wm

    def per_feature(v):
        return np.moveaxis(v.reshape(v.shape[:-1] + (-1, P)), -1, 0)

    gains = [a["norm_g"][0], a["norm_g"][1], a["final_g"], a["norm1_g_2"][0], a["norm2_g_2"][0], a["norm1_g_2"][1], a["norm2_g_2"][1], a["final_g_2"]]
    io["gains"] = per_feature(np.stack(gains))

    inv = ROPE_THETA ** (-np.arange(HEAD // 2, dtype=f32) / f32(HEAD // 2))
    ang = np.arange(LEN, dtype=f32)[None, :] * inv.astype(f32)[:, None]
    cos, sin = np.cos(ang), np.sin(ang)
    cos, sin = np.tile(cos, (4, 1)), np.tile(np.concatenate([-sin, sin]), (2, 1))
    io["rope"] = np.stack([cos * -SCALE, sin * -SCALE, cos, sin], axis=1).astype(f32)
    partner = np.arange(P) ^ (HEAD // 2)
    io["rot"] = np.eye(P, dtype=f32)[partner]
    io["mask"] = np.where(np.arange(LEN)[None, :] <= META + P + np.arange(P)[:, None], 0.0, NEG).astype(f32)
    io["ident"] = np.eye(P, dtype=f32)
    io["bforget"] = a["b_forget"].T
    io["subln"] = per_feature(a["subln_g"])
    lams = np.stack([a["lam_q1"], a["lam_k1"], a["lam_q2"], a["lam_k2"]], axis=1)
    io["lamv"] = np.broadcast_to(lams, (P,) + lams.shape)

    io["wsT"] = a["gm_ws_2"].transpose(3, 0, 1, 2)
    gmb = np.tile(a["gm_b_2"], (1, 1, SEQ // P))
    io["gmb"] = np.broadcast_to(gmb, (P,) + gmb.shape)
    io["gmg"] = np.broadcast_to(a["gm_norm_g_2"], (P,) + a["gm_norm_g_2"].shape)
    io["poolw"] = a["pool_w_2"].reshape(LAYERS, POOL_T, 2, 64, 64).transpose(2, 3, 0, 1, 4).reshape(P, LAYERS, POOL_T, 64)
    io["pools"] = per_feature(a["pool_scale_2"])
    t = np.arange(1, SEQ + 1, dtype=f32)
    recip = np.stack([f32(1) / np.minimum(t, f32(win)) for win in POOL_WINDOWS])
    io["poolr"] = np.repeat(recip.reshape(POOL_T, 2, SEQ).transpose(1, 0, 2), 64, axis=0)
    io["convw"] = a["conv_dw_w_2"].reshape(LAYERS, TAPS, CONV_T, P).transpose(3, 0, 2, 1)
    convp = np.stack([a[name] for name in ("conv_dw_b_2", "conv_ln_g_2", "conv_ln_b_2", "conv_pw_b_2")], axis=1)
    io["convp"] = per_feature(convp)
    io["router"] = columns(a["moe_router_2"][0], 0, EXPERTS)
    io["lt"] = np.triu(np.ones((P, P), f32), 1)
    io["iota"] = np.broadcast_to(np.arange(P, dtype=f32), (P, P))
    return {"in_" + name: np.ascontiguousarray(v, dtype=f32) for name, v in io.items()}


def declare(nc, arrays):
    io = {name.removeprefix("in_"): nc.dram_tensor(name, v.shape, F32, kind="ExternalInput").ap() for name, v in arrays.items()}
    io["out"] = nc.dram_tensor("out", (1, SEQ, D), F32, kind="ExternalOutput").ap()
    return io


def kernel(**inputs):
    import concourse.bacc as bacc
    from concourse.bass_utils import run_bass_kernel_spmd

    arrays = lay_out({name: np.asarray(v) for name, v in inputs.items()})
    nc = bacc.Bacc("TRN2", target_bir_lowering=False, num_devices=1)
    build_program(nc, declare(nc, arrays))
    return run_bass_kernel_spmd(nc, [arrays], core_ids=[0]).results[0]["out"]
```

```python
from contextlib import ExitStack

import numpy as np

import concourse.bass as bass
from concourse import mybir

F32 = mybir.dt.float32
F32R = mybir.dt.float32r
U32 = mybir.dt.uint32
I32 = mybir.dt.int32
ACT = mybir.ActivationFunctionType
ALU = mybir.AluOpType
AXX = mybir.AxisListType.X

P = 128
D = 1024
KD = D // P
META, SEQ = 16, 256
LEN = META + SEQ
LAYERS = 2
EPS = 1e-6
LAMBDA_INIT = [0.8 - 0.6 * float(np.exp(-0.3 * layer)) for layer in range(LAYERS)]

DIFF_HEADS, FOX_HEADS, HEAD = 4, 8, 64
LOGIT_T, QK_T, V_T = 8, 9, 25
PROJ_T = 33
TURN_LAG = 2
MIX_ORDER = (4, 5, 0, 1, 6, 2, 3, 7)
MIX_STEP = {14: (0,), 16: (1, 2), 17: (3,), 18: (4, 5), 19: (6,), 20: (7,)}
SUB_STEP = 14
ATT_TAIL = 6
SCALE = HEAD ** -0.5
ROPE_THETA = 10000.0
MIXW = 1024
QKN, VN = 16, 8
ROPED = 8
MAPS = 2 * DIFF_HEADS + FOX_HEADS
HEADS = DIFF_HEADS + FOX_HEADS
QTILES = [(0, META, 0, META), (META, P, META, META + P), (META + P, P, 2 * META + P, LEN)]
MAPW = 2 * META + P + LEN
KEYS1 = LEN - META
NEG = 3.0e38

U1_TILES = [2] * 4 + [1] + [2] * 12 + [2] + [1] * 6
U1 = len(U1_TILES)
LOGIT_U, PROJ_U = 4, 17
UNITC = 2048
RAW, RING = 6, 3
POOL_T, GM_HEADS, GM_DIM, CONV_T, TAPS = 2, 4, 96, 3, 31
MIX_T = POOL_T + GM_HEADS + CONV_T
MIX_SPLITS = POOL_T + GM_HEADS // 2 + CONV_T
GM_CHUNK = 64
ACT_TAKES = CONV_T + POOL_T + GM_HEADS
POOL_TAP = 20
TAP_STEP, PROD_STEP = 7, 4
N_PAR, PAR2, CONST2 = 5, 11, 3
XS_FFN = KD + KD // 2
XS_MIX = XS_FFN + KD
LEAD = 4
TOP_K = 2
FAR = 1000.0
GM_T = POOL_T + GM_HEADS
U2 = [(KD, 256)] * 4 + [(KD // 2, GM_HEADS * GM_DIM)] * 2 + [(KD, 192)] * 2
U2 += [(2 * GM_T, P)] * (KD // 2) + [(CONV_T, CONV_T * P)] + [(4 * CONV_T, P)] * 2
POOL_U, V_U, GU_U, EARLY_U, PW_U, LATE_U = 3, 4, 6, 8, 12, 13
FF_T = 22
FF_HALF = FF_T // 2
UF = [(KD, 256)] * FF_T + [(FF_HALF, P)] * (2 * KD)
EXPERTS, CHUNKS, CHUNK = 8, 7, 512
UM = 6 * CHUNKS
UNIT_MIX = [LAYERS * U1, LAYERS * U1 + len(U2) + len(UF)]
UNIT_FF = UNIT_MIX[0] + len(U2)
UNIT_MOE = UNIT_MIX[1] + len(U2)
assert U1 % RAW == 0 and UM % RAW == 0 and RAW % RING == 0
POOL_WINDOWS = (2, 4, 8, 16)
PADC = TAPS - 1
PADP = max(POOL_WINDOWS)
SPLIT_OUTPUTS = {0: 0, 1: 1, 3: 2, 4: 3, 5: 4}


def expert_units():
    order = []
    for c in range(CHUNKS):
        order += [("gate", c, 0), ("gate", c, 1), ("up", c, 0), ("up", c, 1)]
        if c:
            order += [("down", c - 1, 0), ("down", c - 1, 1)]
    return order + [("down", CHUNKS - 1, 0), ("down", CHUNKS - 1, 1)]


EXPERT_UNITS = expert_units()


def unit_columns(n):
    if n < LAYERS * U1:
        return KD * P * U1_TILES[n % U1]
    for base in UNIT_MIX:
        if base <= n < base + len(U2):
            k, w = U2[n - base]
            return k * w
    if UNIT_FF <= n < UNIT_FF + len(UF):
        k, w = UF[n - UNIT_FF]
        return k * w
    return UNITC


def build_program(nc, io):
    ctx = ExitStack()
    with ctx:
        def sb(name, shape, dt=F32, scope=ctx):
            return scope.enter_context(nc.sbuf_tensor(name, shape, dt))

        semaphores = {}

        def sem(name):
            semaphores[name] = ctx.enter_context(nc.semaphore(name))
            return semaphores[name]

        bank = [ctx.enter_context(nc.psum_tensor(f"bank{i}", [P, 512], F32)) for i in range(8)]
        raw = sb("raw", [P, RAW, UNITC])
        whi = sb("whi", [P, RING, UNITC], F32R)
        wlo = sb("wlo", [P, RING, UNITC], F32R)
        uhi = sb("uhi", [P, KD, LEN], F32R)
        ulo = sb("ulo", [P, KD, LEN], F32R)
        sq = sb("sq", [P, 2, LEN])
        ut = sb("ut", [P, 2, LEN])
        sd = sb("sd", [P, LEN])
        rstd = sb("rstd", [P, LEN])
        zs = sb("zs", [P, KD, LEN])
        xT = zs[:, :, 0:SEQ]
        ident = sb("ident", [P, P])
        mean_d = sb("mean_d", [P, P])
        mean_h = sb("mean_h", [P, P])
        mean_c = sb("mean_c", [P, P])
        ones = sb("ones", [P, P])
        eps = sb("eps", [P, 1])
        one = sb("one", [P, 1])
        warm = sb("warm", [P, 8])
        gains = sb("gains", [P, 8, KD])

        first = ExitStack()
        hT = sb("hT", [P, KD, LEN], scope=first)
        qk = sb("qk", [P, QKN, LEN], scope=first)
        qraw = sb("qraw", [P, 2, LEN], scope=first)
        rc = sb("rc", [P, 2, LEN], scope=first)
        rsn = sb("rsn", [P, LEN], scope=first)
        vt = sb("vt", [P, 2, LEN], scope=first)
        v0 = sb("v0", [META, VN, P], scope=first)
        v12 = sb("v12", [P, VN, 2, P], scope=first)
        cum = sb("cum", [FOX_HEADS, LEN], scope=first)
        ncum = sb("ncum", [FOX_HEADS, LEN], scope=first)
        sm = sb("sm", [P, 2, MAPW], scope=first)
        ex = sb("ex", [P, 4, MAPW], scope=first)
        held = sb("held", [P, 4], scope=first)
        nmax = sb("nmax", [P, 4, 3], scope=first)
        sums = sb("sums", [P, 4, 3], scope=first)
        rsum = sb("rsum", [P, 4, 3], scope=first)
        rlam = sb("rlam", [P, 2, 3], scope=first)
        pd = sb("pd", [P, MAPW], scope=first)
        pr = sb("pr", [P, 2, MAPW], scope=first)
        pt0 = sb("pt0", [META, 2, LEN], scope=first)
        pt1 = sb("pt1", [P, 2, KEYS1 + P], scope=first)
        rope = sb("rope", [P, 4, LEN], scope=first)
        rot = sb("rot", [P, P], scope=first)
        mask = sb("mask", [P, LEN], scope=first)
        bforget = sb("bforget", [FOX_HEADS, LAYERS], scope=first)
        subln = sb("subln", [P, LAYERS, DIFF_HEADS], scope=first)
        subg = sb("subg", [P, LAYERS, DIFF_HEADS], scope=first)
        lamv = ex[:, 0:2, 0:256].rearrange("p l (v d) -> p l v d", v=4)
        lamp = sb("lamp", [P, LAYERS, 2], scope=first)
        lame = sb("lame", [P, LAYERS, 2], scope=first)
        lamd = sb("lamd", [P, LAYERS], scope=first)
        lam = sb("lam", [P, LAYERS], scope=first)
        h_in = qk[:, 0:KD, :]
        xb, ab, lf = (ex[0:FOX_HEADS, i, 0:LEN] for i in range(3))
        le, ll = sm[0:FOX_HEADS, 0, 0:LEN], sm[0:FOX_HEADS, 1, 0:LEN]
        osb = qk[:, 4:8, :]
        msb = qk[:, 0:4, :]
        sqo, mx32 = qraw, rc
        first.close()

        second = ExitStack()
        wsT = sb("wsT", [P, LAYERS, GM_HEADS, P], scope=second)
        gmb = sb("gmb", [P, LAYERS, GM_HEADS, SEQ], scope=second)
        gmg = sb("gmg", [P, LAYERS, GM_HEADS * GM_DIM], scope=second)
        poolw = sb("poolw", [P, LAYERS, POOL_T, 64], scope=second)
        pools = sb("pools", [P, LAYERS, POOL_T], scope=second)
        poolr = sb("poolr", [P, POOL_T, SEQ], scope=second)
        convw = sb("convw", [P, LAYERS, CONV_T, TAPS], scope=second)
        convp = sb("convp", [P, LAYERS, 4, CONV_T], scope=second)
        router = sb("router", [P, KD, EXPERTS], scope=second)
        lt = sb("lt", [P, P], scope=second)
        iota = sb("iota", [P, P], scope=second)
        mixer = ExitStack()
        sig = sb("sig", [P, 2, SEQ], scope=mixer)
        hpad = sb("hpad", [P, CONV_T, PADC + SEQ], scope=mixer)
        cacc = sb("cacc", [P, CONV_T, SEQ], scope=mixer)
        csq = sb("csq", [P, CONV_T, SEQ], scope=mixer)
        crs = sb("crs", [P, 2, SEQ], scope=mixer)
        prod = [csq[:, 0, :], crs[:, 0, :], crs[:, 1, :]]
        chi = sb("chi", [P, CONV_T, SEQ], F32R, scope=mixer)
        clo = sb("clo", [P, CONV_T, SEQ], F32R, scope=mixer)
        pa = sb("pa", [P, POOL_T, SEQ], scope=mixer)
        pc = sb("pc", [P, POOL_T, PADP + SEQ], scope=mixer)
        py = sb("py", [P, POOL_T, SEQ], scope=mixer)
        gu = sb("gu", [P, GM_HEADS, SEQ], scope=mixer)
        gv = sb("gv", [P, 2, GM_HEADS * GM_DIM], scope=mixer)
        gss = sb("gss", [P, 4, 2], scope=mixer)
        gz = sb("gz", [P, GM_HEADS, SEQ], scope=mixer)
        gvj = gz[:].rearrange("p h t -> p (h t)")[:, 0:2 * GM_HEADS * GM_DIM].rearrange("p (a c) -> p a c", a=2)
        mhi = sb("mhi", [P, MIX_T, SEQ], F32R, scope=mixer)
        mlo = sb("mlo", [P, MIX_T, SEQ], F32R, scope=mixer)
        mixer.close()
        ffn = ExitStack()
        fs = sb("fs", [P, 2, SEQ], scope=ffn)
        fa = sb("fa", [P, 2, SEQ], scope=ffn)
        fhi = sb("fhi", [P, FF_T, SEQ], F32R, scope=ffn)
        flo = sb("flo", [P, FF_T, SEQ], F32R, scope=ffn)
        ffn.close()
        moe = ExitStack()
        un = sb("un", [P, KD, SEQ], scope=moe)
        nhi = sb("nhi", [P, 2, D], F32R, scope=moe)
        nlo = sb("nlo", [P, 2, D], F32R, scope=moe)
        hthi = sb("hthi", [P, KD, P], F32R, scope=moe)
        htlo = sb("htlo", [P, KD, P], F32R, scope=moe)
        gsa = sb("gsa", [P, 4, CHUNK], scope=moe)
        gs, ga = gsa[:, 0:2, :], gsa[:, 2:4, :]
        outn = gsa[:].rearrange("p (t h) c -> p t (h c)", t=2)
        athi = sb("athi", [P, 4, P], F32R, scope=moe)
        atlo = sb("atlo", [P, 4, P], F32R, scope=moe)
        yt = sb("yt", [P, D], scope=moe)
        pick = sb("pick", [P, 2, P], F32R, scope=moe)
        gpick = sb("gpick", [P, 2, P], scope=moe)
        gpickT = sb("gpickT", [P, 2, P], scope=moe)
        lg = sb("lg", [P, 2, EXPERTS], scope=moe)
        top = sb("top", [P, 2, 8], scope=moe)
        topi = sb("topi", [P, 2, 8], U32, scope=moe)
        topf = sb("topf", [P, 2, 8], scope=moe)
        tw = sb("tw", [P, 4, 2], scope=moe)
        oh = sb("oh", [P, 2, 2, EXPERTS], scope=moe)
        chosen = sb("chosen", [P, 2, EXPERTS], scope=moe)
        big = sb("big", [P, 2, EXPERTS], scope=moe)
        rank = sb("rank", [P, 2, 2 * EXPERTS + 1], scope=moe)
        gate = sb("gate", [P, 2, 2 * EXPERTS], scope=moe)
        cnt = sb("cnt", [P, 1], scope=moe)
        cnti = sb("cnti", [P, 1], I32, scope=moe)
        moe.close()
        second.close()

        raw_landed = [sem(f"raw_landed{i}") for i in range(RAW)]
        hi_ready, lo_ready = sem("hi_ready"), sem("lo_ready")
        unit_done = sem("unit_done")
        in_landed, par_landed = sem("in_landed"), sem("par_landed")
        lam_landed, par2_landed = sem("lam_landed"), sem("par2_landed")
        const_ready, const2_ready = sem("const_ready"), sem("const2_ready")
        x_ready, xs_ready = sem("x_ready"), sem("xs_ready")
        sq_ready, ms_step, sd_ready, rstd_ready = sem("sq_ready"), sem("ms_step"), sem("sd_ready"), sem("rstd_ready")
        u_ready, uhi_ready, ulo_ready = sem("u_ready"), sem("uhi_ready"), sem("ulo_ready")
        lam_step, lam_exp, lam_ready = sem("lam_step"), sem("lam_exp"), sem("lam_ready")
        proj_taken = sem("proj_taken")
        rot_done, rot_taken, rc_ready, roped = sem("rot_done"), sem("rot_taken"), sem("rc_ready"), sem("roped")
        vt_done, v_ready = sem("vt_done"), sem("v_ready")
        logit_step, lf_ready, cum_ready = sem("logit_step"), sem("lf_ready"), sem("cum_ready")
        s_done, masked, exp_done = sem("s_done"), sem("masked"), sem("exp_done")
        rsum_ready, rlam_ready, pd_ready = sem("rsum_ready"), sem("rlam_ready"), sem("pd_ready")
        diff_p, fox_p = sem("diff_p"), sem("fox_p")
        t_done, pt0_ready, pt1_ready, pv_done = sem("t_done"), sem("pt0_ready"), sem("pt1_ready"), sem("pv_done")
        diff_taken, mixed = sem("diff_taken"), sem("mixed")
        msq_done, msq_taken = sem("msq_done"), sem("msq_taken")
        subsd_ready, subrs_ready, sub_ready = sem("subsd_ready"), sem("subrs_ready"), sem("sub_ready")
        mixhi_ready, mixlo_ready = sem("mixhi_ready"), sem("mixlo_ready")
        act_taken, cv_taken = sem("act_taken"), sem("cv_taken")
        vsq_ready, vsd_ready, vrs_ready, vn_ready = sem("vsq_ready"), sem("vsd_ready"), sem("vrs_ready"), sem("vn_ready")
        z_done, zb_ready, gm_ready = sem("z_done"), sem("zb_ready"), sem("gm_ready")
        scan_ready, pool_step, pool_ready, pool_done = sem("scan_ready"), sem("pool_step"), sem("pool_ready"), sem("pool_done")
        tap_done, conv_ready, mean_done, centred = sem("tap_done"), sem("conv_ready"), sem("mean_done"), sem("centred")
        out_done, prod_ready, sum0_done = sem("out_done"), sem("prod_ready"), sem("sum0_done")
        csq_ready, var_done, csd_ready, crs_ready = sem("csq_ready"), sem("var_done"), sem("csd_ready"), sem("crs_ready")
        cn_ready, cs_ready, chi_ready, clo_ready = sem("cn_ready"), sem("cs_ready"), sem("chi_ready"), sem("clo_ready")
        mhi_ready, mlo_ready = sem("mhi_ready"), sem("mlo_ready")
        fs_ready, fa_ready, fhi_ready, flo_ready = sem("fs_ready"), sem("fa_ready"), sem("fhi_ready"), sem("flo_ready")
        un_ready, lg_done, route_step = sem("un_ready"), sem("lg_done"), sem("route_step")
        tw_diff, tw_exp, chosen_ready = sem("tw_diff"), sem("tw_exp"), sem("chosen_ready")
        rank_done, count_ready = sem("rank_done"), sem("count_ready")
        nt_done, nhi_ready, nlo_ready = sem("nt_done"), sem("nhi_ready"), sem("nlo_ready")
        pick_ready, gpick_ready = sem("pick_ready"), sem("gpick_ready")
        gpickT_done, gpickT_ready = sem("gpickT_done"), sem("gpickT_ready")
        gather_done, hthi_ready, htlo_ready = sem("gather_done"), sem("hthi_ready"), sem("htlo_ready")
        silu_ready, a_ready = sem("silu_ready"), sem("a_ready")
        at_done, athi_ready, atlo_ready = sem("at_done"), sem("athi_ready"), sem("atlo_ready")
        rank_zero, yt_ready = sem("rank_zero"), sem("yt_ready")
        scat_done, scat_taken, last_done, last_taken = sem("scat_done"), sem("scat_taken"), sem("last_done"), sem("last_taken")
        result_ready, ot_done, ot_ready, stored = sem("result_ready"), sem("ot_done"), sem("ot_ready"), sem("stored")

        block = ctx.enter_context(nc.Block())

        def load_unit(sp, n, turn=0, per=0, source=None, columns=None):
            c = columns or unit_columns(n)
            if n >= RAW:
                sp.wait_ge(lo_ready, turn * per + (n - RAW + 1))
            if source is None:
                source = io["w"][n, :, 0:c]
            sp.dma_start(raw[:, n % RAW, 0:c], source).then_inc(raw_landed[n % RAW], 16)

        def split_hi(act, n, turn=0, per=0, columns=None):
            c = columns or unit_columns(n)
            act.wait_ge(raw_landed[n % RAW], turn * (16 * (per // RAW)) + 16 * (n // RAW + 1))
            if n >= RING:
                act.wait_ge(unit_done, turn * per + (n - RING + 1))
            act.activation(whi[:, n % RING, 0:c], raw[:, n % RAW, 0:c], ACT.Copy).then_inc(hi_ready, 1)

        def split_lo(dve, n, turn=0, per=0, columns=None):
            c = columns or unit_columns(n)
            dve.wait_ge(hi_ready, turn * per + (n + 1))
            dve.tensor_tensor(wlo[:, n % RING, 0:c], raw[:, n % RAW, 0:c], whi[:, n % RING, 0:c].bitcast(F32),
                              ALU.subtract).then_inc(lo_ready, 1)

        def unit_views(n, k):
            c = unit_columns(n)
            return [t[:, n % RING, 0:c].rearrange("p (k c) -> p k c", k=k) for t in (whi, wlo)]

        def three_pass(pe, out, s_hi, s_lo, m_hi, m_lo, start, stop, shared=False):
            pe.matmul(out, s_hi, m_hi, start=start, stop=False, skip_group_check=shared)
            pe.matmul(out, s_hi, m_lo, start=False, stop=False, skip_group_check=shared)
            return pe.matmul(out, s_lo, m_hi, start=False, stop=stop, skip_group_check=shared)

        def proj_place(i):
            if i < LOGIT_T:
                return i // 2, i % 2
            return (LOGIT_U, 0) if i == LOGIT_T else (LOGIT_U + 1 + (i - QK_T) // 2, (i - QK_T) % 2)

        def out_tiles(j):
            d = 0 if j == PROJ_U else 2 + (j - PROJ_U - 1)
            return range(d, d + U1_TILES[j])

        def pw_out(f):
            return bank[7 if f < 2 else 4][:, (f % 2) * SEQ:(f % 2 + 1) * SEQ]

        def head_at(m):
            if 0 <= m < 2 * DIFF_HEADS:
                return m // 2 if m % 2 else None
            return m - DIFF_HEADS if 2 * DIFF_HEADS <= m < MAPS else None

        @block.sync
        def _(sp):
            sp.dma_start(lamv, io["lamv"]).then_inc(lam_landed, 16)
            sp.dma_start(subln[:], io["subln"]).then_inc(lam_landed, 16)
            load_unit(sp, 0)
            load_unit(sp, 1)
            sp.dma_start(h_in, io["hT"]).then_inc(in_landed, 16)
            sp.dma_start(gains[:], io["gains"]).then_inc(in_landed, 16)
            load_unit(sp, 2)
            for dst, name in ((bforget, "bforget"), (rope, "rope"), (rot, "rot"), (ident, "ident"), (mask, "mask")):
                sp.dma_start(dst[:], io[name]).then_inc(par_landed, 16)
            for n in range(3, RAW):
                load_unit(sp, n)
            with sp.Fori(0, LAYERS) as l:
                for j in range(RAW, U1 + RAW):
                    c = unit_columns(j) if j < U1 else max(unit_columns(j), unit_columns(UNIT_MIX[0] + j - U1))
                    src = io["w"][bass.ds(l * U1 + j, 1), :, 0:c].rearrange("a p c -> (a p) c")
                    load_unit(sp, j, l, U1, src, c)
            for n in range(UNIT_MIX[0] + RAW, UNIT_FF):
                load_unit(sp, n)
            for first_n, count in ((UNIT_FF, FF_T), (UNIT_FF + FF_T, 2 * KD)):
                for n in range(first_n, first_n + LEAD):
                    load_unit(sp, n)
                n = first_n + LEAD
                with sp.Fori(0, (count - LEAD) // RAW) as t:
                    for j in range(RAW):
                        src = io["w"][bass.ds(t * RAW + (n + j), 1), :, 0:unit_columns(n + j)].rearrange("a p c -> (a p) c")
                        load_unit(sp, n + j, t, RAW, src)
            for n in range(UNIT_MIX[1], UNIT_MOE):
                load_unit(sp, n)
            for j in range(2):
                load_unit(sp, UNIT_MOE + j, source=io["wm"][0, j])

            def expert(it):
                for j in range(2, UM + 2):
                    e = it % EXPERTS if j < UM else (it + 1) % EXPERTS
                    src = io["wm"][bass.ds(e, 1), j % UM].rearrange("a p c -> (a p) c")
                    load_unit(sp, UNIT_MOE + j, it, UM, src)

            with sp.Fori(0, EXPERTS) as it:
                expert(it)
            sp.wait_ge(count_ready, 1)
            fullest = sp.value_load(cnti[0:1, 0:1], min_val=0, max_val=SEQ)
            with sp.If(fullest > P):
                with sp.Fori(EXPERTS, 2 * EXPERTS) as it:
                    expert(it)
            for tt in range(2):
                sp.wait_ge(ot_ready, 2 * tt + 2)
                sp.dma_start(io["out"][0, tt * P:(tt + 1) * P, :], outn[:, tt, :]).then_inc(stored, 16)
            sp.wait_ge(stored, 32)

        @block.tensor
        def _(pe):
            def norm_sums(q, n):
                for k in range(KD):
                    pe.wait_ge(sq_ready, q * KD + (k + 1))
                    pe.matmul(bank[7][:, 0:n], mean_d[:], sq[:, k % 2, 0:n], start=(k == 0), stop=(k == KD - 1)).then_inc(ms_step, 1)

            def project(l, i):
                u, s = proj_place(i)
                hi, lo = unit_views(u, KD)
                if i == 0:
                    pe.wait_ge(lo_ready, l * U1 + 1)
                    for k in range(KD):
                        pe.wait_ge(ulo_ready, l * KD + (k + 1))
                        for s in range(2):
                            cols = slice(s * P, (s + 1) * P)
                            mm = three_pass(pe, bank[s][:, 0:LEN], hi[:, k, cols], lo[:, k, cols], uhi[:, k, :], ulo[:, k, :], k == 0, k == KD - 1)
                    mm.then_inc(unit_done, 1)
                if i < 2:
                    return
                if s == 0:
                    pe.wait_ge(lo_ready, l * U1 + (u + 1))
                if i >= 4:
                    pe.wait_ge(proj_taken, l * PROJ_T + (i - 3))
                cols = slice(s * P, (s + 1) * P)
                for k in range(KD):
                    mm = three_pass(pe, bank[i % 4][:, 0:LEN], hi[:, k, cols], lo[:, k, cols],
                                    uhi[:, k, :], ulo[:, k, :], k == 0, k == KD - 1)
                if s == U1_TILES[u] - 1:
                    mm.then_inc(unit_done, 1)

            def turn(l, i):
                if QK_T <= i < QK_T + ROPED:
                    r = i - QK_T
                    if r == 0:
                        pe.wait_ge(par_landed, 16 * N_PAR)
                    pe.wait_ge(proj_taken, l * PROJ_T + (i + 1))
                    if r >= 2:
                        pe.wait_ge(rot_taken, l * ROPED + (r - 1))
                    pe.matmul(bank[4 + r % 2][:, 0:LEN], rot[:], qraw[:, r % 2, :], start=True, stop=True).then_inc(rot_done, 1)
                if i >= V_T:
                    v = i - V_T
                    pe.wait_ge(proj_taken, l * PROJ_T + (i + 1))
                    if v >= 2:
                        pe.wait_ge(v_ready, l * VN + (v - 1))
                    b = bank[6 + v % 2]
                    pe.transpose(b[0:META, 0:P], vt[:, v % 2, 0:META], ident[:])
                    pe.transpose(b[:, P:2 * P], vt[:, v % 2, META:META + P], ident[:])
                    pe.transpose(b[:, 2 * P:3 * P], vt[:, v % 2, META + P:LEN], ident[:]).then_inc(vt_done, 1)

            def scores(l, m):
                if m >= 3:
                    pe.wait_ge(masked, l * MAPS + (m - 2))
                fox = m >= 2 * DIFF_HEADS
                if fox:
                    f = m - 2 * DIFF_HEADS
                    tq, tk, part = 8 + f // 2, 12 + f // 2, HEAD * (f % 2)
                    pe.wait_ge(proj_taken, l * PROJ_T + (QK_T + tk + 1))
                    pe.wait_ge(cum_ready, 2 * l + 2)
                else:
                    tq, tk, part = m // 2, DIFF_HEADS + m // 2, HEAD * (m % 2)
                    pe.wait_ge(roped, l * ROPED + (tk + 1))
                for q0, rows, c0, keys in reversed(QTILES):
                    out = bank[m % 3][0:rows, c0:c0 + keys]
                    mm = pe.matmul(out, qk[part:part + HEAD, tq, q0:q0 + rows], qk[part:part + HEAD, tk, 0:keys], start=True, stop=not fox)
                    if fox:
                        head = ident[0:FOX_HEADS, f:f + 1]
                        pe.matmul(out, ncum[:, q0:q0 + rows], head.to_broadcast([FOX_HEADS, keys]), start=False, stop=False)
                        mm = pe.matmul(out, head.to_broadcast([FOX_HEADS, rows]), cum[:, 0:keys], start=False, stop=True)
                mm.then_inc(s_done, 1)

            def turn_probs(l, p):
                if p < DIFF_HEADS:
                    pe.wait_ge(diff_p, l * DIFF_HEADS + (p + 1))
                else:
                    pe.wait_ge(fox_p, l * FOX_HEADS + (p - DIFF_HEADS + 1))
                if p >= 1:
                    pe.wait_ge(pt0_ready, l * HEADS + p)
                    pe.wait_ge(pt1_ready, l * HEADS + p)
                b = pr[:, p % 2, :]
                pe.transpose(bank[4][:, 0:P], b[:, 2 * META:2 * META + P], ident[:])
                pe.transpose(bank[4][:, P:2 * P], b[:, 3 * META + P:3 * META + 2 * P], ident[:])
                pe.transpose(bank[4][:, 2 * P:3 * P], b[:, 3 * META + 2 * P:MAPW], ident[:])
                pe.transpose(bank[5][0:META, 0:META], b[0:META, 0:META], ident[0:META, 0:META])
                pe.transpose(bank[5][0:META, META:META + P], b[:, META:2 * META], ident[:])
                pe.transpose(bank[5][0:META, META + P:LEN], b[:, 2 * META + P:3 * META + P], ident[:]).then_inc(t_done, 1)

            def meet_values(l, p):
                if p < DIFF_HEADS:
                    o, c, w, part = p, 0, P, 0
                else:
                    f = p - DIFF_HEADS
                    o, c, w, part = DIFF_HEADS + f // 2, HEAD * (f % 2), HEAD, HEAD * (f % 2)
                if p == 0:
                    pe.wait_ge(v_ready, l * VN + VN)
                if part == 0:
                    if 2 <= o < DIFF_HEADS + 2:
                        pe.wait_ge(diff_taken, l * DIFF_HEADS + (o - 1))
                    elif o >= DIFF_HEADS + 2:
                        pe.wait_ge(mixed, l * KD + (MIX_ORDER.index(o - 2) + 1))
                pe.wait_ge(pt0_ready, l * HEADS + (p + 1))
                pe.wait_ge(pt1_ready, l * HEADS + (p + 1))
                b, i = bank[6 + o % 2][part:part + w, :], p % 2
                pe.matmul(b[:, 0:LEN], v0[:, o, c:c + w], pt0[:, i, :], start=True, stop=False, skip_group_check=True)
                pe.matmul(b[:, META:LEN], v12[:, o, 0, c:c + w], pt1[:, i, 0:KEYS1], start=False, stop=False, skip_group_check=True)
                pe.matmul(b[:, META + P:LEN], v12[:, o, 1, c:c + w], pt1[:, i, KEYS1:KEYS1 + P], start=False, stop=True,
                          skip_group_check=True).then_inc(pv_done, 1)

            def head_sums(l, h):
                pe.wait_ge(diff_taken, l * DIFF_HEADS + (h + 1))
                if h:
                    pe.wait_ge(msq_taken, l * DIFF_HEADS + h)
                pe.matmul(bank[3][:, 0:LEN], mean_h[:], sqo[:, h % 2, :], start=True, stop=True).then_inc(msq_done, 1)

            def first_out(l, j):
                hi, lo = unit_views(j, KD)
                pe.wait_ge(lo_ready, l * U1 + (j + 1))
                for s, d in enumerate(out_tiles(j)):
                    if d >= 4:
                        pe.wait_ge(x_ready, l * KD + (KD + d - 3))
                    for i, k in enumerate(MIX_ORDER):
                        if d == 0:
                            pe.wait_ge(mixlo_ready, l * KD + (i + 1))
                        mm = three_pass(pe, bank[d % 4][:, 0:LEN], hi[:, k, s * P:(s + 1) * P], lo[:, k, s * P:(s + 1) * P],
                                        uhi[:, k, :], ulo[:, k, :], i == 0, i == KD - 1)
                mm.then_inc(unit_done, 1)

            pe.wait_ge(const_ready, 1)
            with pe.Fori(0, LAYERS) as l:
                norm_sums(l, LEN)
                for i in range(PROJ_T):
                    project(l, i)
                    turn(l, i - TURN_LAG)
                for i in range(PROJ_T - TURN_LAG, PROJ_T):
                    turn(l, i)
                for s in range(MAPS + ATT_TAIL):
                    if s < MAPS:
                        scores(l, s)
                    if (p := head_at(s - 3)) is not None:
                        turn_probs(l, p)
                    if (p := head_at(s - 4)) is not None:
                        meet_values(l, p)
                    if (p := head_at(s - 5)) is not None and p < DIFF_HEADS:
                        head_sums(l, p)
                for j in range(PROJ_U, U1):
                    first_out(l, j)
            norm_sums(2, LEN)

            def mixer_tiles(L):
                n0 = UNIT_MIX[L]
                items = [(c, half * P, P) for c in range(CONV_T) for half in range(2)]
                items += [(POOL_U, half * P, P) for half in range(2)]
                items += [(GU_U + h // 2, GM_DIM * (h % 2), GM_DIM) for h in range(GM_HEADS)]
                cv, at = CONV_T * L, ACT_TAKES * L
                taken = {4: (cv_taken, cv + 1), 5: (act_taken, at + 1), 6: (cv_taken, cv + 2), 7: (act_taken, at + 2),
                         8: (cv_taken, cv + 3), 9: (act_taken, at + 3), 10: (act_taken, at + 4), 11: (act_taken, at + 5)}

                def tiles(a, b):
                    u = items[a][0]
                    hi, lo = unit_views(n0 + u, KD)
                    pe.wait_ge(lo_ready, n0 + u + 1)
                    for i in (a, b):
                        if i in taken:
                            pe.wait_ge(*taken[i])
                    for k in range(KD):
                        if a == 0:
                            pe.wait_ge(ulo_ready, SPLIT_OUTPUTS[3 + 2 * L] * KD + k + 1)
                        for i in (a, b):
                            _, c0, w = items[i]
                            mm = three_pass(pe, bank[i % 4][0:w, 0:SEQ], hi[:, k, c0:c0 + w], lo[:, k, c0:c0 + w],
                                            uhi[:, k, 0:SEQ], ulo[:, k, 0:SEQ], k == 0, k == KD - 1)
                    mm.then_inc(unit_done, 1)

                for c in range(CONV_T):
                    tiles(2 * c, 2 * c + 1)
                tiles(6, 7)
                for s in range(2):
                    n = n0 + V_U + s
                    hi, lo = unit_views(n, KD // 2)
                    pe.wait_ge(lo_ready, n + 1)
                    for tt in range(2):
                        out, t = bank[4 + tt][:, 0:GM_HEADS * GM_DIM], slice(tt * P, (tt + 1) * P)
                        for i in range(KD // 2):
                            k = s * (KD // 2) + i
                            mm = three_pass(pe, out, uhi[:, k, t], ulo[:, k, t], hi[:, i, :], lo[:, i, :], k == 0, k == KD - 1)
                    mm.then_inc(unit_done, 1)
                tiles(8, 9)
                tiles(10, 11)
                if L == 0:
                    pe.wait_ge(par2_landed, 16 * PAR2)
                    pe.wait_ge(const2_ready, CONST2)
                pe.wait_ge(vn_ready, 2 * (L + 1))
                for h in range(GM_HEADS):
                    b = bank[7 if h < 2 else 4]
                    for blk in range(2):
                        c0 = (h % 2) * SEQ + blk * P
                        mm = pe.matmul(b[0:GM_DIM, c0:c0 + P], gv[:, blk, h * GM_DIM:(h + 1) * GM_DIM], wsT[:, L, h, :], start=True, stop=True)
                    if h % 2:
                        mm.then_inc(z_done, 1)

            def mixer_parts(L):
                pe.wait_ge(pool_ready, POOL_T * (L + 1))
                for g in range(len(POOL_WINDOWS)):
                    part, c = slice(64 * (g % 2), 64 * (g % 2) + 64), g // 2
                    mm = pe.matmul(bank[6][part, c * SEQ:(c + 1) * SEQ], poolw[part, L, c, :], py[part, c, :], start=True, stop=True)
                mm.then_inc(pool_done, 1)

                def out_tile(n, d, first, count, place):
                    hi, lo = unit_views(n, U2[n - UNIT_MIX[L]][0])
                    for j in range(count):
                        i = first + j
                        rows = slice(0, GM_DIM if POOL_T <= i < GM_T else P)
                        out = bank[d // 2][:, (d % 2) * SEQ:(d % 2 + 1) * SEQ]
                        mm = three_pass(pe, out, hi[rows, place * count + j, :], lo[rows, place * count + j, :], mhi[rows, i, :], mlo[rows, i, :],
                                        i == 0 and d % 2 == 0, i == MIX_T - 1, shared=True)
                    return mm

                def early_out(a):
                    n = UNIT_MIX[L] + EARLY_U + a
                    pe.wait_ge(lo_ready, n + 1)
                    if a == 0:
                        pe.wait_ge(act_taken, ACT_TAKES * (L + 1))
                        pe.wait_ge(cv_taken, CONV_T * (L + 1))
                        pe.wait_ge(mlo_ready, MIX_SPLITS * L + POOL_T + 2)
                    for place in range(2):
                        mm = out_tile(n, 2 * a + place, 0, GM_T, place)
                    mm.then_inc(unit_done, 1)

                early_out(0)
                pe.wait_ge(sum0_done, (L + 1) * (TAPS - 1))
                pe.wait_ge(conv_ready, (CONV_T - 1) * (L + 1))
                for c in range(CONV_T):
                    mm = pe.matmul(bank[5][:, 0:SEQ], mean_c[:], cacc[:, c, :], start=(c == 0), stop=(c == CONV_T - 1))
                mm.then_inc(mean_done, 1)
                early_out(1)
                for c in range(CONV_T):
                    pe.wait_ge(csq_ready, CONV_T * L + c + 1)
                    mm = pe.matmul(bank[6][:, 0:SEQ], mean_c[:], csq[:, c, :], start=(c == 0), stop=(c == CONV_T - 1))
                mm.then_inc(var_done, 1)
                early_out(2)
                early_out(3)
                n = UNIT_MIX[L] + PW_U
                hi, lo = unit_views(n, CONV_T)
                pe.wait_ge(lo_ready, n + 1)
                for k in range(CONV_T):
                    pe.wait_ge(clo_ready, CONV_T * L + k + 1)
                for f in range(CONV_T):
                    for k in range(CONV_T):
                        mm = three_pass(pe, pw_out(f), hi[:, k, f * P:(f + 1) * P], lo[:, k, f * P:(f + 1) * P],
                                        chi[:, k, :], clo[:, k, :], k == 0, k == CONV_T - 1)
                mm.then_inc(unit_done, 1)
                for b in range(2):
                    n = UNIT_MIX[L] + LATE_U + b
                    pe.wait_ge(lo_ready, n + 1)
                    if b == 0:
                        pe.wait_ge(mlo_ready, MIX_SPLITS * (L + 1))
                    for place in range(4):
                        mm = out_tile(n, 4 * b + place, GM_T, CONV_T, place)
                        if place == 1:
                            mm.then_inc(out_done, 1)
                    mm.then_inc(unit_done, 1)

            def ffn_in(f, t=0):
                n = UNIT_FF + f
                hi, lo = unit_views(n, KD)
                pe.wait_ge(lo_ready, t * RAW + (n + 1))
                if f >= 2:
                    pe.wait_ge(fs_ready, t * RAW + (f - 1))
                    pe.wait_ge(fa_ready, t * RAW + (f - 1))
                for k in range(KD):
                    if f == 0:
                        pe.wait_ge(ulo_ready, SPLIT_OUTPUTS[4] * KD + k + 1)
                    for half in range(2):
                        cols = slice(half * P, (half + 1) * P)
                        mm = three_pass(pe, bank[2 * half + f % 2][:, 0:SEQ], hi[:, k, cols], lo[:, k, cols],
                                        uhi[:, k, 0:SEQ], ulo[:, k, 0:SEQ], k == 0, k == KD - 1)
                mm.then_inc(unit_done, 1)

            def ffn_out(d, t=0):
                if d >= 2:
                    pe.wait_ge(xs_ready, t * (RAW // 2) + (XS_FFN + d - 2))
                for half in range(2):
                    n = UNIT_FF + FF_T + 2 * d + half
                    hi, lo = unit_views(n, FF_HALF)
                    pe.wait_ge(lo_ready, t * RAW + (n + 1))
                    for j in range(FF_HALF):
                        f = half * FF_HALF + j
                        if d == 0:
                            pe.wait_ge(flo_ready, f + 1)
                        mm = three_pass(pe, bank[4 + d % 3][:, 0:SEQ], hi[:, j, :], lo[:, j, :], fhi[:, f, :], flo[:, f, :],
                                        f == 0, f == FF_T - 1)
                    mm.then_inc(unit_done, 1)

            for L in range(LAYERS):
                norm_sums(3 + 2 * L, SEQ)
                mixer_tiles(L)
                mixer_parts(L)
                norm_sums(4 + 2 * L, SEQ)
                if L == 0:
                    for f in range(LEAD):
                        ffn_in(f)
                    with pe.Fori(0, (FF_T - LEAD) // RAW) as t:
                        for j in range(RAW):
                            ffn_in(LEAD + j, t)
                    for d in range(LEAD // 2):
                        ffn_out(d)
                    with pe.Fori(0, (2 * KD - LEAD) // RAW) as t:
                        for j in range(RAW // 2):
                            ffn_out(LEAD // 2 + j, t)

            for k in range(KD):
                pe.wait_ge(un_ready, k + 1)
                for tt in range(2):
                    mm = pe.matmul(bank[tt][:, 0:EXPERTS], un[:, k, tt * P:(tt + 1) * P], router[:, k, :], start=(k == 0), stop=(k == KD - 1))
            mm.then_inc(lg_done, 1)
            for tt in range(2):
                for half in range(2):
                    for i in range(4):
                        mm = pe.transpose(bank[2 + 2 * tt + half][:, i * P:(i + 1) * P], un[:, 4 * half + i, tt * P:(tt + 1) * P], ident[:])
                    mm.then_inc(nt_done, 1)
            pe.wait_ge(chosen_ready, 2)
            pe.matmul(bank[6][:, 0:EXPERTS], lt[:], chosen[:, 0, :], start=True, stop=True)
            pe.matmul(bank[6][:, EXPERTS:2 * EXPERTS], ones[:], chosen[:, 0, :], start=True, stop=False)
            pe.matmul(bank[6][:, EXPERTS:2 * EXPERTS], lt[:], chosen[:, 1, :], start=False, stop=True)
            pe.matmul(bank[6][:, 2 * EXPERTS:3 * EXPERTS], ones[:], chosen[:, 0, :], start=True, stop=False)
            pe.matmul(bank[6][:, 2 * EXPERTS:3 * EXPERTS], ones[:], chosen[:, 1, :], start=False, stop=True).then_inc(rank_done, 1)

            def gather(half, g):
                if half == 0:
                    pe.wait_ge(pick_ready, g + 1)
                else:
                    pe.wait_ge(htlo_ready, 2 * g + 1)
                for i in range(4):
                    d = 4 * half + i
                    for tt in range(2):
                        for part in (nhi, nlo):
                            mm = pe.matmul(bank[7][:, i * P:(i + 1) * P], part[:, tt, d * P:(d + 1) * P], pick[:, tt, :],
                                           start=(tt == 0 and part is nhi), stop=(tt == 1 and part is nlo))
                mm.then_inc(gather_done, 1)

            def scatter(r, done, b=bank[7]):
                for i in range(2):
                    d = 2 * r + i
                    mm = pe.matmul(b[:, i * SEQ:(i + 1) * SEQ], yt[:, d * P:(d + 1) * P], gpickT[:].rearrange("p a t -> p (a t)"),
                                   start=True, stop=True)
                mm.then_inc(done, 1)

            def expert(it):
                def weights(pos):
                    n = UNIT_MOE + pos
                    pe.wait_ge(lo_ready, it * UM + (n + 1))
                    return unit_views(n, 2 if EXPERT_UNITS[pos][0] == "down" else 4)

                def rows(kind, c):
                    b = bank[(0 if kind == "gate" else 2) + c % 2]
                    if c >= 2:
                        pe.wait_ge(silu_ready if kind == "gate" else a_ready, it * CHUNKS + (c - 1))
                    for part in range(2):
                        hi, lo = weights(EXPERT_UNITS.index((kind, c, part)))
                        for i in range(4):
                            k = 4 * part + i
                            if c == 0 and kind == "gate" and i == 0:
                                pe.wait_ge(htlo_ready, 2 * it + (part + 1))
                            mm = three_pass(pe, b[:], hthi[:, k, :], htlo[:, k, :], hi[:, i, :], lo[:, i, :], k == 0, k == KD - 1)
                        mm.then_inc(unit_done, 1)

                def turn_rows(c):
                    pe.wait_ge(a_ready, it * CHUNKS + (c + 1))
                    if c:
                        pe.wait_ge(atlo_ready, it * CHUNKS + c)
                    for i in range(4):
                        mm = pe.transpose(bank[4][:, i * P:(i + 1) * P], ga[:, c % 2, i * P:(i + 1) * P], ident[:])
                    mm.then_inc(at_done, 1)

                def down(c):
                    pe.wait_ge(atlo_ready, it * CHUNKS + (c + 1))
                    if c == 0:
                        pe.wait_ge(yt_ready, it + 1)
                    for part in range(2):
                        hi, lo = weights(EXPERT_UNITS.index(("down", c, part)))
                        for i in range(2):
                            f = 2 * part + i
                            for half in range(2):
                                cols = slice(half * 512, (half + 1) * 512)
                                mm = three_pass(pe, bank[5 + half][:], athi[:, f, :], atlo[:, f, :], hi[:, i, cols], lo[:, i, cols],
                                                c == 0 and f == 0, c == CHUNKS - 1 and f == 3)
                        mm.then_inc(unit_done, 1)

                for c in range(CHUNKS):
                    if 1 <= c <= 4:
                        if c > 1:
                            pe.wait_ge(scat_taken, it * 4 + (c - 1))
                        scatter(c - 1, scat_done)
                    rows("gate", c)
                    if c:
                        turn_rows(c - 1)
                    rows("up", c)
                    if c == 5:
                        pe.wait_ge(gpick_ready, it + 1)
                        pe.wait_ge(scat_taken, it * 4 + 4)
                        pe.transpose(bank[7][:, 0:P], gpick[:, 0, :], ident[:])
                        pe.transpose(bank[7][:, P:2 * P], gpick[:, 1, :], ident[:]).then_inc(gpickT_done, 1)
                    if c == 6:
                        pe.wait_ge(gpickT_ready, it + 2)
                        gather(0, it + 1)
                    if c:
                        down(c - 1)
                turn_rows(CHUNKS - 1)
                gather(1, it + 1)
                down(CHUNKS - 1)

            pe.wait_ge(nlo_ready, 4)
            gather(0, 0)
            gather(1, 0)
            with pe.Fori(0, EXPERTS) as it:
                expert(it)
            pe.wait_ge(yt_ready, EXPERTS + 1)
            pe.wait_ge(htlo_ready, 2 * EXPERTS + 2)
            pe.wait_ge(count_ready, 1)
            fullest = pe.value_load(cnti[0:1, 0:1], min_val=0, max_val=SEQ)
            with pe.If(fullest > P):
                with pe.Fori(EXPERTS, 2 * EXPERTS) as it:
                    expert(it)
                pe.wait_ge(yt_ready, 2 * EXPERTS + 1)
                pe.wait_ge(htlo_ready, 4 * EXPERTS + 2)
            for r in range(4):
                scatter(r, last_done, bank[r])
            norm_sums(7, SEQ)
            for tt in range(2):
                for half in range(2):
                    for i in range(4):
                        if tt == 0:
                            pe.wait_ge(result_ready, 4 * half + i + 1)
                        mm = pe.transpose(bank[2 * tt + half][:, i * P:(i + 1) * P], un[:, 4 * half + i, tt * P:(tt + 1) * P], ident[:])
                    mm.then_inc(ot_done, 1)

        @block.scalar
        def _(act):
            def norm_squares(q, n, source, ready, per_tile=1, first_count=0):
                w = warm[:, q:q + 1] if isinstance(q, int) else warm[:, bass.ds(q, 1)]
                act.activation(w, eps[:], ACT.Sqrt)
                for k in range(KD):
                    act.wait_ge(ready, first_count + k // per_tile + 1)
                    if k >= 2:
                        act.wait_ge(ms_step, q * KD + (k - 1))
                    act.activation(sq[:, k % 2, 0:n], source[:, k, 0:n], ACT.Square).then_inc(sq_ready, 1)
                act.wait_ge(ms_step, q * KD + KD)
                act.activation(sd[:, 0:n], bank[7][:, 0:n], ACT.Sqrt, bias=eps[:]).then_inc(sd_ready, 1)

            def norm_hi(order, n):
                for k in range(KD):
                    act.wait_ge(u_ready, order * KD + (k + 1))
                    act.activation(uhi[:, k, 0:n], ut[:, k % 2, 0:n], ACT.Copy).then_inc(uhi_ready, 1)

            def take_tile(l, i):
                src = bank[i % 4][:, 0:LEN]
                if i < LOGIT_T:
                    act.activation(zs[:, i, :], src, ACT.Silu).then_inc(proj_taken, 1)
                elif i == LOGIT_T:
                    act.wait_ge(par_landed, 16 * N_PAR)
                    act.activation(xb, bank[i % 4][0:FOX_HEADS, 0:LEN], ACT.Identity,
                                   bias=bforget[:, bass.ds(l, 1)]).then_inc(proj_taken, 1)
                    act.wait_ge(proj_taken, l * PROJ_T + (i + 1))
                    act.activation(ab, xb, ACT.Abs).then_inc(logit_step, 1)
                    act.wait_ge(logit_step, 3 * l + 1)
                    act.activation(le, ab, ACT.Exp, scale=-1.0).then_inc(logit_step, 1)
                    act.wait_ge(logit_step, 3 * l + 2)
                    act.activation(ll, le, ACT.Ln, bias=one[0:FOX_HEADS, :]).then_inc(logit_step, 1)
                elif i < QK_T + ROPED:
                    r = i - QK_T
                    if r >= 2:
                        act.wait_ge(rot_done, l * ROPED + (r - 1))
                        act.wait_ge(rc_ready, l * ROPED + (r - 1))
                    act.activation(qraw[:, r % 2, :], src, ACT.Copy).then_inc(proj_taken, 1)
                elif i < V_T:
                    r = i - QK_T
                    scale = -SCALE if r < ROPED + QKN // 4 else 1.0
                    act.activation(qk[:, r, :], src, ACT.Copy, scale=scale).then_inc(proj_taken, 1)
                else:
                    v = i - V_T
                    if v >= 2:
                        act.wait_ge(vt_done, l * VN + (v - 1))
                    act.activation(vt[:, v % 2, :], src, ACT.Copy).then_inc(proj_taken, 1)

            def exp_map(l, m):
                act.wait_ge(masked, l * MAPS + (m + 1))
                if m >= 4:
                    if m - 4 < 2 * DIFF_HEADS:
                        act.wait_ge(diff_p, l * DIFF_HEADS + ((m - 4) // 2 + 1))
                    else:
                        act.wait_ge(fox_p, l * FOX_HEADS + (m - 4 - 2 * DIFF_HEADS + 1))
                for t, (q0, rows, c0, keys) in enumerate(QTILES):
                    op = act.activation(ex[0:rows, m % 4, c0:c0 + keys], sm[0:rows, m % 2, c0:c0 + keys], ACT.Exp,
                                        bias=nmax[0:rows, m % 4, t:t + 1], scale=-1.0, accum_out=sums[0:rows, m % 4, t:t + 1])
                op.then_inc(exp_done, 1)

            def mixed_hi(l, i):
                act.wait_ge(mixed, l * KD + (i + 1))
                act.activation(uhi[:, MIX_ORDER[i], :], mx32[:, i % 2, :], ACT.Copy).then_inc(mixhi_ready, 1)

            act.wait_ge(const_ready, 1)
            act.wait_ge(lam_step, 2 * LAYERS)
            act.activation(lame[:], lamp[:], ACT.Exp).then_inc(lam_exp, 1)
            split_hi(act, 0)
            split_hi(act, 1)
            with act.Fori(0, LAYERS) as l:
                norm_squares(l, LEN, hT, x_ready, 1, l * KD)
                norm_hi(l, LEN)
                i = 0
                for u in range(PROJ_U):
                    split_hi(act, u + 2, l, U1)
                    act.wait_ge(unit_done, l * U1 + (u + 1))
                    for _ in range(U1_TILES[u]):
                        take_tile(l, i)
                        i += 1
                for s in range(MAPS + ATT_TAIL):
                    if s < MAPS:
                        exp_map(l, s)
                    if (p := head_at(s - 3)) is not None:
                        act.wait_ge(t_done, l * HEADS + (p + 1))
                        if p >= 2:
                            act.wait_ge(pv_done, l * HEADS + (p - 1))
                        act.activation(pt1[:, p % 2, :], bank[4][:, 0:KEYS1 + P], ACT.Copy).then_inc(pt1_ready, 1)
                        act.activation(pt0[:, p % 2, :], bank[5][0:META, 0:LEN], ACT.Copy).then_inc(pt0_ready, 1)
                    if (p := head_at(s - 4)) is not None and p < DIFF_HEADS:
                        act.wait_ge(pv_done, l * HEADS + (p + 1))
                        if p >= 2:
                            act.wait_ge(msq_done, l * DIFF_HEADS + (p - 1))
                        act.activation(osb[:, p, :], bank[6 + p % 2][:, 0:LEN], ACT.Copy)
                        act.activation(sqo[:, p % 2, :], bank[6 + p % 2][:, 0:LEN], ACT.Square).then_inc(diff_taken, 1)
                    for i in MIX_STEP.get(s, ()):
                        mixed_hi(l, i)
                    if s == SUB_STEP:
                        act.wait_ge(msq_taken, (l + 1) * DIFF_HEADS)
                        act.activation(msb, msb, ACT.Sqrt, bias=eps[:]).then_inc(subsd_ready, 1)
                for u in range(PROJ_U, U1):
                    split_hi(act, u + 2, l, U1, UNITC if u + 2 >= U1 else None)
            norm_squares(2, LEN, hT, x_ready, 1, LAYERS * KD)

            def mixer(L):
                n0 = UNIT_MIX[L]

                def products(a):
                    for k in range(a, min(a + PROD_STEP, TAPS)):
                        if k == 0:
                            act.wait_ge(cv_taken, CONV_T * L + 1)
                            act.wait_ge(const2_ready, CONST2 + 2 * L)
                        if k > 3:
                            act.wait_ge(sum0_done, L * (TAPS - 1) + k - 3)
                        out, bias = (prod[k % 3], 0.0) if k else (cacc[:, 0, :], convp[:, L, 0, 0:1])
                        act.activation(out, hpad[:, 0, k:k + SEQ], ACT.Identity, bias=bias, scale=convw[:, L, 0, k:k + 1]).then_inc(prod_ready, 1)

                def unit(u):
                    split_hi(act, n0 + u + 2)
                    if u:
                        products((u - 1) * PROD_STEP)
                    act.wait_ge(unit_done, n0 + u + 1)

                def part(done_sem, count, out, src, func, **how):
                    act.wait_ge(done_sem, count)
                    act.activation(out, src, func, **how).then_inc(mhi_ready, 1)

                for c in range(CONV_T):
                    unit(c)
                    if c >= 2:
                        act.wait_ge(cv_taken, CONV_T * L + c - 1)
                    act.activation(sig[:, c % 2, :], bank[(2 * c + 1) % 4][:, 0:SEQ], ACT.Sigmoid).then_inc(act_taken, 1)
                unit(POOL_U)
                for c in range(POOL_T):
                    act.activation(pa[:, c, :], bank[2 + c][:, 0:SEQ], ACT.Copy).then_inc(act_taken, 1)
                unit(V_U)
                unit(V_U + 1)
                for tt in range(2):
                    op = act.activation(gvj[:, tt, :], bank[4 + tt][:, 0:GM_HEADS * GM_DIM], ACT.Square, accum_out=gss[:, 0, tt:tt + 1])
                op.then_inc(vsq_ready, 1)
                act.wait_ge(vsq_ready, L + 1)
                act.activation(gss[:, 1, :], gss[:, 0, :], ACT.Sqrt, bias=eps[:], scale=1.0 / (GM_HEADS * GM_DIM)).then_inc(vsd_ready, 1)
                for u in (GU_U, GU_U + 1):
                    unit(u)
                    for h in (2 * (u - GU_U), 2 * (u - GU_U) + 1):
                        act.activation(gu[0:GM_DIM, h, :], bank[h][0:GM_DIM, 0:SEQ], ACT.Copy).then_inc(act_taken, 1)
                products((EARLY_U - 1) * PROD_STEP)
                split_hi(act, n0 + EARLY_U + 2)
                for pair in range(2):
                    hs = slice(2 * pair, 2 * pair + 2)
                    part(gm_ready, 2 * L + pair + 1, mhi[0:GM_DIM, POOL_T + 2 * pair:POOL_T + 2 * pair + 2, :], gz[0:GM_DIM, hs, :], ACT.Copy)
                for c in range(POOL_T):
                    part(pool_done, L + 1, mhi[:, c, :], bank[6][:, c * SEQ:(c + 1) * SEQ], ACT.Copy, scale=pools[:, L, c:c + 1])
                for c in range(CONV_T):
                    act.wait_ge(centred, CONV_T * L + c + 1)
                    act.activation(csq[:, c, :], cacc[:, c, :], ACT.Square).then_inc(csq_ready, 1)
                split_hi(act, n0 + EARLY_U + 3)
                act.wait_ge(var_done, L + 1)
                act.activation(crs[:, 0, :], bank[6][:, 0:SEQ], ACT.Sqrt, bias=eps[:]).then_inc(csd_ready, 1)
                for c in range(CONV_T):
                    act.wait_ge(cn_ready, CONV_T * L + c + 1)
                    act.activation(csq[:, c, :], cacc[:, c, :], ACT.Silu, bias=convp[:, L, 2, c:c + 1],
                                   scale=convp[:, L, 1, c:c + 1]).then_inc(cs_ready, 1)
                for c in range(CONV_T):
                    act.wait_ge(cs_ready, CONV_T * L + c + 1)
                    act.activation(chi[:, c, :], csq[:, c, :], ACT.Copy).then_inc(chi_ready, 1)
                for n in range(n0 + PW_U, n0 + LATE_U + 2):
                    split_hi(act, n)
                for f in range(CONV_T):
                    part(unit_done, n0 + PW_U + 1, mhi[:, GM_T + f, :], pw_out(f), ACT.Identity, bias=convp[:, L, 3, f:f + 1])
                split_hi(act, n0 + LATE_U + 2)
                split_hi(act, n0 + LATE_U + 3)

            def ffn_hi(f, t=0):
                act.wait_ge(fa_ready, t * RAW + (f + 1))
                at = slice(f, f + 1) if isinstance(t, int) else bass.ds(t * RAW + f, 1)
                act.activation(fhi[:, at, :], fa[:, f % 2:f % 2 + 1, :], ACT.Copy).then_inc(fhi_ready, 1)

            def ffn_unit(f, t=0):
                n = UNIT_FF + f
                split_hi(act, n + 2, t, RAW, UNITC)
                act.wait_ge(unit_done, t * RAW + (n + 1))
                if f >= 2:
                    act.wait_ge(fa_ready, t * RAW + (f - 1))
                act.activation(fs[:, f % 2, :], bank[f % 2][:, 0:SEQ], ACT.Silu).then_inc(fs_ready, 1)
                if f:
                    ffn_hi(f - 1, t)

            for L in range(LAYERS):
                norm_squares(3 + 2 * L, SEQ, xT, xs_ready, 1, XS_MIX - KD if L else 0)
                norm_hi(SPLIT_OUTPUTS[3 + 2 * L], SEQ)
                mixer(L)
                norm_squares(4 + 2 * L, SEQ, xT, xs_ready, 2, XS_MIX if L else KD)
                if L == 0:
                    norm_hi(SPLIT_OUTPUTS[4], SEQ)
                    for f in range(LEAD):
                        ffn_unit(f)
                    with act.Fori(0, (FF_T - LEAD) // RAW) as t:
                        for j in range(RAW):
                            ffn_unit(LEAD + j, t)
                    ffn_hi(FF_T - 1)
                    for j in range(LEAD):
                        split_hi(act, UNIT_FF + FF_T + j + 2)
                    with act.Fori(0, (2 * KD - LEAD) // RAW) as t:
                        for j in range(LEAD, LEAD + RAW):
                            split_hi(act, UNIT_FF + FF_T + j + 2, t, RAW, UNITC)

            act.wait_ge(un_ready, KD)
            act.activation(yt[:], one[:].to_broadcast([P, D]), ACT.Copy, scale=0.0).then_inc(yt_ready, 1)
            act.activation(gpickT[:].rearrange("p a t -> p (a t)"), one[:].to_broadcast([P, 2 * P]), ACT.Copy, scale=0.0).then_inc(gpickT_ready, 1)
            for i in range(4):
                act.wait_ge(nt_done, i + 1)
                act.activation(nhi[:, i // 2, (i % 2) * 512:(i % 2 + 1) * 512], bank[2 + i][:], ACT.Copy).then_inc(nhi_ready, 1)
            act.wait_ge(tw_diff, 1)
            act.activation(tw[:, 1, :], tw[:, 0, :], ACT.Exp).then_inc(tw_exp, 1)

            def gathered_hi(half, g):
                act.wait_ge(gather_done, g * 2 + (half + 1))
                act.activation(hthi[:, 4 * half:4 * half + 4, :], bank[7][:].rearrange("p (k t) -> p k t", k=4), ACT.Copy).then_inc(hthi_ready, 1)

            def expert(it):
                def rows_hi(c):
                    act.wait_ge(at_done, it * CHUNKS + (c + 1))
                    act.activation(athi[:], bank[4][:].rearrange("p (k t) -> p k t", k=4), ACT.Copy).then_inc(athi_ready, 1)

                for pos, (kind, c, part) in enumerate(EXPERT_UNITS):
                    split_hi(act, UNIT_MOE + pos + 2, it, UM)
                    if part == 0:
                        continue
                    if kind == "gate":
                        act.wait_ge(unit_done, it * UM + (UNIT_MOE + pos + 1))
                        if c >= 2:
                            act.wait_ge(a_ready, it * CHUNKS + (c - 1))
                        act.activation(gs[:, c % 2, :], bank[c % 2][:], ACT.Silu).then_inc(silu_ready, 1)
                        if c:
                            rows_hi(c - 1)
                    if kind == "up" and c == 5:
                        act.wait_ge(gpickT_done, it + 1)
                        act.activation(gpickT[:].rearrange("p a t -> p (a t)"), bank[7][:, 0:2 * P], ACT.Copy).then_inc(gpickT_ready, 1)
                    if kind == "up" and c == CHUNKS - 1:
                        gathered_hi(0, it + 1)
                    if kind == "down" and c == CHUNKS - 2:
                        rows_hi(CHUNKS - 1)
                        gathered_hi(1, it + 1)
                    if kind == "down" and c == CHUNKS - 1:
                        act.wait_ge(unit_done, it * UM + (UNIT_MOE + pos + 1))
                        act.activation(yt[:, 0:512], bank[5][:], ACT.Copy)
                        act.activation(yt[:, 512:D], bank[6][:], ACT.Copy).then_inc(yt_ready, 1)

            gathered_hi(0, 0)
            gathered_hi(1, 0)
            with act.Fori(0, EXPERTS) as it:
                expert(it)
            act.wait_ge(count_ready, 1)
            fullest = act.value_load(cnti[0:1, 0:1], min_val=0, max_val=SEQ)
            with act.If(fullest > P):
                with act.Fori(EXPERTS, 2 * EXPERTS) as it:
                    expert(it)
            norm_squares(7, SEQ, xT, last_taken, 2)
            for i in range(4):
                act.wait_ge(ot_done, i + 1)
                act.activation(outn[:, i // 2, (i % 2) * 512:(i % 2 + 1) * 512], bank[i][:], ACT.Copy).then_inc(ot_ready, 1)

        @block.vector
        def _(dve):
            def norm_scale(q):
                dve.wait_ge(sd_ready, q + 1)
                dve.reciprocal(rstd[:], sd[:]).then_inc(rstd_ready, 1)
                dve.wait_ge(rstd_ready, q + 1)

            def normed(q, out, source, k, n, ready):
                gain = gains[:, q:q + 1, k] if isinstance(q, int) else gains[:, bass.ds(q, 1), k]
                dve.scalar_tensor_tensor(out, source, gain, rstd[:, 0:n], ALU.mult, ALU.mult).then_inc(ready, 1)

            def norm_split(q, order, source, n):
                norm_scale(q)
                for k in range(KD + 1):
                    if 2 <= k < KD:
                        dve.wait_ge(ulo_ready, order * KD + (k - 1))
                    if k < KD:
                        normed(q, ut[:, k % 2, 0:n], source[:, k, 0:n], k, n, u_ready)
                    if k:
                        dve.wait_ge(uhi_ready, order * KD + k)
                        dve.tensor_tensor(ulo[:, k - 1, 0:n], ut[:, (k - 1) % 2, 0:n], uhi[:, k - 1, 0:n].bitcast(F32),
                                          ALU.subtract).then_inc(ulo_ready, 1)

            for tile, value in ((mean_d, 1.0 / D), (mean_h, 1.0 / P), (mean_c, 1.0 / (CONV_T * P)), (ones, 1.0), (eps, EPS),
                                (sd, 1.0), (sums, 1.0)):
                dve.memset(tile[:], value)
            dve.memset(one[:], 1.0).then_inc(const_ready, 1)
            dve.wait_ge(lam_landed, 32)
            for l in range(LAYERS):
                for i in range(2):
                    dve.tensor_tensor_reduce(rsn[:, 0:HEAD], lamv[:, l, 2 * i, :], lamv[:, l, 2 * i + 1, :], 1.0, 0.0,
                                             ALU.mult, ALU.add, lamp[:, l, i:i + 1]).then_inc(lam_step, 1)
                    dve.wait_ge(lam_step, 2 * l + i + 1)
            dve.wait_ge(lam_exp, 1)
            dve.tensor_tensor(lamd[:], lame[:, :, 0], lame[:, :, 1], ALU.subtract).then_inc(lam_ready, 1)
            dve.wait_ge(lam_ready, 1)
            for l in range(LAYERS):
                dve.tensor_scalar(lam[:, l:l + 1], lamd[:, l:l + 1], LAMBDA_INIT[l], None, ALU.add).then_inc(lam_ready, 1)
                dve.tensor_scalar(subg[:, l, :], subln[:, l, :], 1.0 - LAMBDA_INIT[l], None, ALU.mult).then_inc(lam_ready, 1)
            dve.wait_ge(lam_ready, 1 + 2 * LAYERS)
            split_lo(dve, 0)
            split_lo(dve, 1)
            dve.wait_ge(in_landed, 32)
            for k in range(KD):
                dve.tensor_copy(hT[:, k, :], h_in[:, k, :]).then_inc(x_ready, 1)

            def turned(l, i):
                if i == LOGIT_T:
                    dve.wait_ge(logit_step, 3 * l + 3)
                    dve.scalar_tensor_tensor(lf, xb, 0.0, ll, ALU.min, ALU.subtract).then_inc(lf_ready, 1)
                    dve.wait_ge(lf_ready, l + 1)
                    dve.tensor_tensor_scan(cum[:], one[0:FOX_HEADS, :].to_broadcast([FOX_HEADS, LEN]), lf, 0.0,
                                           ALU.mult, ALU.add).then_inc(cum_ready, 1)
                    dve.wait_ge(cum_ready, 2 * l + 1)
                    dve.tensor_scalar(ncum[:], cum[:], -1.0, None, ALU.mult).then_inc(cum_ready, 1)
                elif QK_T <= i < QK_T + ROPED:
                    r = i - QK_T
                    if r == 0:
                        dve.wait_ge(par_landed, 16 * N_PAR)
                    dve.wait_ge(rot_done, l * ROPED + (r + 1))
                    if r:
                        dve.wait_ge(roped, l * ROPED + r)
                    dve.tensor_tensor(rsn[:], bank[4 + r % 2][:, 0:LEN], rope[:, 2 * (r // 4) + 1, :], ALU.mult).then_inc(rot_taken, 1)
                    dve.wait_ge(rot_taken, l * ROPED + (r + 1))
                    dve.wait_ge(rc_ready, l * ROPED + (r + 1))
                    dve.tensor_tensor(qk[:, r, :], rc[:, r % 2, :], rsn[:], ALU.add).then_inc(roped, 1)
                elif i >= V_T:
                    v = i - V_T
                    dve.wait_ge(vt_done, l * VN + (v + 1))
                    b = bank[6 + v % 2]
                    dve.tensor_copy(v0[:, v, :], b[0:META, 0:P])
                    dve.tensor_copy(v12[:, v, :, :], b[:, P:3 * P].rearrange("p (t d) -> p t d", t=2)).then_inc(v_ready, 1)

            def mask_map(l, m):
                dve.wait_ge(s_done, l * MAPS + (m + 1))
                if m >= 2:
                    dve.wait_ge(exp_done, l * MAPS + (m - 1))
                dve.memset(held[:, m % 4:m % 4 + 1], 0.0)
                masks = mask[0:META, META + P:2 * META + P], mask[:, P:LEN], mask[:, :]
                for t, (q0, rows, c0, keys) in enumerate(QTILES):
                    op = dve.tensor_tensor_reduce(sm[0:rows, m % 2, c0:c0 + keys], bank[m % 3][0:rows, c0:c0 + keys], masks[t], 1.0, NEG,
                                                  ALU.add, ALU.min, nmax[0:rows, m % 4, t:t + 1])
                op.then_inc(masked, 1)

            def map_scales(l, m):
                dve.wait_ge(exp_done, l * MAPS + (m + 1))
                dve.reciprocal(rsum[:, m % 4, :], sums[:, m % 4, :]).then_inc(rsum_ready, 1)
                if m < 2 * DIFF_HEADS and m % 2:
                    dve.wait_ge(rsum_ready, l * MAPS + (m + 1))
                    dve.tensor_scalar(rlam[:, (m // 2) % 2, :], rsum[:, m % 4, :], lam[:, bass.ds(l, 1)], None, ALU.mult).then_inc(rlam_ready, 1)

            def difference(l, p):
                dve.wait_ge(pd_ready, l * DIFF_HEADS + (p + 1))
                if p >= 2:
                    dve.wait_ge(t_done, l * HEADS + (p - 1))
                m = 2 * p
                for t, (q0, rows, c0, keys) in enumerate(QTILES):
                    cols = slice(c0, c0 + keys)
                    op = dve.scalar_tensor_tensor(pr[0:rows, p % 2, cols], ex[0:rows, m % 4, cols], rsum[0:rows, m % 4, t:t + 1], pd[0:rows, cols],
                                                  ALU.mult, ALU.subtract)
                op.then_inc(diff_p, 1)

            def mix(l, i):
                o = MIX_ORDER[i]
                if i >= 2:
                    dve.wait_ge(mixlo_ready, l * KD + (i - 1))
                if o >= DIFF_HEADS:
                    dve.wait_ge(pv_done, l * HEADS + (DIFF_HEADS + 2 * (o - DIFF_HEADS) + 2))
                    src = bank[6 + o % 2][:, 0:LEN]
                else:
                    src = ut[:, o % 2, :]
                    dve.wait_ge(subrs_ready, l * DIFF_HEADS + (o + 1))
                    dve.scalar_tensor_tensor(src, osb[:, o, :], subg[:, bass.ds(l, 1), o], msb[:, o, :], ALU.mult, ALU.mult).then_inc(sub_ready, 1)
                    dve.wait_ge(sub_ready, l * DIFF_HEADS + (o + 1))
                dve.tensor_tensor(mx32[:, i % 2, :], src, zs[:, o, :], ALU.mult).then_inc(mixed, 1)

            def mixed_lo(l, i):
                dve.wait_ge(mixhi_ready, l * KD + (i + 1))
                dve.tensor_tensor(ulo[:, MIX_ORDER[i], :], mx32[:, i % 2, :], uhi[:, MIX_ORDER[i], :].bitcast(F32),
                                  ALU.subtract).then_inc(mixlo_ready, 1)

            with dve.Fori(0, LAYERS) as l:
                norm_split(l, l, hT, LEN)
                i = 0
                for u in range(PROJ_U):
                    split_lo(dve, u + 2, l, U1)
                    for _ in range(U1_TILES[u]):
                        turned(l, i - TURN_LAG)
                        i += 1
                for i in range(PROJ_T - TURN_LAG, PROJ_T):
                    turned(l, i)
                for s in range(MAPS + ATT_TAIL):
                    if s < MAPS:
                        mask_map(l, s)
                    if 1 <= s <= MAPS:
                        map_scales(l, s - 1)
                    if (p := head_at(s - 2)) is not None and p < DIFF_HEADS:
                        difference(l, p)
                    for i in MIX_STEP.get(s - 1, ()):
                        mixed_lo(l, i)
                    for i in MIX_STEP.get(s, ()):
                        mix(l, i)
                    if (p := head_at(s - 6)) is not None and p < DIFF_HEADS:
                        dve.wait_ge(msq_done, l * DIFF_HEADS + (p + 1))
                        dve.tensor_copy(msb[:, p, :], bank[3][:, 0:LEN]).then_inc(msq_taken, 1)
                    if 0 <= (h := s - SUB_STEP - 1) < DIFF_HEADS:
                        dve.wait_ge(subsd_ready, l + 1)
                        dve.reciprocal(msb[:, h, :], msb[:, h, :]).then_inc(subrs_ready, 1)
                for u in range(PROJ_U, U1):
                    split_lo(dve, u + 2, l, U1, UNITC if u + 2 >= U1 else None)
                    dve.wait_ge(unit_done, l * U1 + (u + 1))
                    for d in out_tiles(u):
                        dve.tensor_tensor(hT[:, d, :], hT[:, d, :], bank[d % 4][:, 0:LEN], ALU.add).then_inc(x_ready, 1)
            norm_scale(2)
            for k in range(KD):
                dve.scalar_tensor_tensor(xT[:, k, :], hT[:, k, META:LEN], gains[:, 2, k:k + 1], rstd[:, META:LEN],
                                         ALU.mult, ALU.mult).then_inc(xs_ready, 1)

            taps = [(c, k) for c in range(1, CONV_T) for k in range(TAPS)]

            def conv_taps(L, a, b):
                for i in range(a, min(b, len(taps))):
                    c, k = taps[i]
                    window, w = hpad[:, c, k:k + SEQ], convw[:, L, c, k:k + 1]
                    acc = csq if k % 2 else cacc
                    count = L * len(taps) + i
                    if k == 0:
                        dve.wait_ge(cv_taken, CONV_T * L + c + 1)
                        op = dve.tensor_scalar(acc[:, c, :], window, w, convp[:, L, 0, c:c + 1], ALU.mult, ALU.add)
                    elif k == 1:
                        op = dve.tensor_scalar(acc[:, c, :], window, w, None, ALU.mult)
                    else:
                        dve.wait_ge(tap_done, count - 1)
                        op = dve.scalar_tensor_tensor(acc[:, c, :], window, w, acc[:, c, :], ALU.mult, ALU.add)
                    op.then_inc(tap_done, 1)

            def conv_sums(L):
                dve.wait_ge(tap_done, (L + 1) * len(taps))
                for c in range(1, CONV_T):
                    dve.tensor_tensor(cacc[:, c, :], cacc[:, c, :], csq[:, c, :], ALU.add).then_inc(conv_ready, 1)

            def mixer(L):
                n0 = UNIT_MIX[L]
                done = 0
                for u in range(8):
                    split_lo(dve, n0 + u + 2)
                    if u < CONV_T:
                        dve.wait_ge(act_taken, ACT_TAKES * L + u + 1)
                        dve.tensor_tensor(hpad[:, u, PADC:], bank[2 * u % 4][:, 0:SEQ], sig[:, u % 2, :], ALU.mult).then_inc(cv_taken, 1)
                    if u == 0:
                        dve.wait_ge(par2_landed, 16 * PAR2)
                        dve.wait_ge(const2_ready, CONST2 + 2 * L)
                    if u == V_U + 2:
                        dve.wait_ge(vsd_ready, L + 1)
                        dve.reciprocal(gss[:, 2, :], gss[:, 1, :]).then_inc(vrs_ready, 1)
                        dve.wait_ge(vrs_ready, L + 1)
                        for tt in range(2):
                            dve.scalar_tensor_tensor(gv[:, tt, :], bank[4 + tt][:, 0:GM_HEADS * GM_DIM], gss[:, 2, tt:tt + 1], gmg[:, L, :],
                                                     ALU.mult, ALU.mult).then_inc(vn_ready, 1)
                    if u == POOL_U + 1:
                        for c in range(POOL_T):
                            dve.wait_ge(act_taken, ACT_TAKES * L + CONV_T + c + 1)
                            dve.tensor_tensor_scan(pc[:, c, PADP:], one[:].to_broadcast([P, SEQ]), pa[:, c, :], 0.0,
                                                   ALU.mult, ALU.add).then_inc(scan_ready, 1)
                    if u:
                        conv_taps(L, done, done + TAP_STEP)
                        done += TAP_STEP
                    if u == GU_U + 1:
                        for pair in range(2):
                            hs = slice(2 * pair, 2 * pair + 2)
                            z = bank[4 if pair else 7][0:GM_DIM, :].rearrange("p (h t) -> p h t", h=2)
                            dve.wait_ge(z_done, 2 * L + pair + 1)
                            dve.tensor_tensor(gz[0:GM_DIM, hs, :], z, gmb[0:GM_DIM, L, hs, :], ALU.add).then_inc(zb_ready, 1)
                        dve.wait_ge(act_taken, ACT_TAKES * (L + 1))
                        for pair in range(2):
                            hs = slice(2 * pair, 2 * pair + 2)
                            dve.wait_ge(zb_ready, 2 * L + pair + 1)
                            dve.tensor_tensor(gz[0:GM_DIM, hs, :], gz[0:GM_DIM, hs, :], gu[0:GM_DIM, hs, :], ALU.mult).then_inc(gm_ready, 1)
                split_lo(dve, n0 + EARLY_U + 2)

                def hi_there(i):
                    dve.wait_ge(mhi_ready, MIX_SPLITS * L + i + 1)

                for pair in range(2):
                    hi_there(pair)
                    ms = slice(POOL_T + 2 * pair, POOL_T + 2 * pair + 2)
                    dve.tensor_tensor(mlo[0:GM_DIM, ms, :], gz[0:GM_DIM, 2 * pair:2 * pair + 2, :], mhi[0:GM_DIM, ms, :].bitcast(F32),
                                      ALU.subtract).then_inc(mlo_ready, 1)
                hi_there(2 + POOL_T - 1)
                for c in range(POOL_T):
                    dve.scalar_tensor_tensor(mlo[:, c, :], bank[6][:, c * SEQ:(c + 1) * SEQ], pools[:, L, c:c + 1], mhi[:, c, :].bitcast(F32),
                                             ALU.mult, ALU.subtract).then_inc(mlo_ready, 1)
                conv_taps(L, done, len(taps))
                conv_sums(L)
                dve.wait_ge(mean_done, L + 1)
                for c in range(CONV_T):
                    dve.tensor_tensor(cacc[:, c, :], cacc[:, c, :], bank[5][:, 0:SEQ], ALU.subtract).then_inc(centred, 1)
                split_lo(dve, n0 + EARLY_U + 3)
                dve.wait_ge(csd_ready, L + 1)
                dve.reciprocal(crs[:, 1, :], crs[:, 0, :]).then_inc(crs_ready, 1)
                dve.wait_ge(crs_ready, L + 1)
                for c in range(CONV_T):
                    dve.tensor_tensor(cacc[:, c, :], cacc[:, c, :], crs[:, 1, :], ALU.mult).then_inc(cn_ready, 1)
                for c in range(CONV_T):
                    dve.wait_ge(chi_ready, CONV_T * L + c + 1)
                    dve.tensor_tensor(clo[:, c, :], csq[:, c, :], chi[:, c, :].bitcast(F32), ALU.subtract).then_inc(clo_ready, 1)
                for n in range(n0 + PW_U, n0 + LATE_U + 2):
                    split_lo(dve, n)
                hi_there(POOL_T + 2 + 1)
                for f in range(CONV_T):
                    hi_there(POOL_T + 2 + f)
                    dve.scalar_tensor_tensor(mlo[:, GM_T + f, :], pw_out(f), convp[:, L, 3, f:f + 1],
                                             mhi[:, GM_T + f, :].bitcast(F32), ALU.add, ALU.subtract).then_inc(mlo_ready, 1)
                for b in range(2):
                    split_lo(dve, n0 + LATE_U + 2 + b)
                    dve.wait_ge(out_done, 2 * L + b + 1)
                    for j in (2 * b, 2 * b + 1):
                        if j % 2:
                            dve.wait_ge(unit_done, n0 + LATE_U + b + 1)
                        tiles = xT[:, 2 * j:2 * j + 2, :]
                        dve.tensor_tensor(tiles, tiles, bank[j][:].rearrange("p (k t) -> p k t", k=2), ALU.add).then_inc(xs_ready, 1)

            def ffn_lo(f, t=0):
                dve.wait_ge(fhi_ready, t * RAW + (f + 1))
                at = slice(f, f + 1) if isinstance(t, int) else bass.ds(t * RAW + f, 1)
                dve.tensor_tensor(flo[:, at, :], fa[:, f % 2:f % 2 + 1, :], fhi[:, at, :].bitcast(F32), ALU.subtract).then_inc(flo_ready, 1)

            def ffn_unit(f, t=0):
                split_lo(dve, UNIT_FF + f + 2, t, RAW, UNITC)
                dve.wait_ge(fs_ready, t * RAW + (f + 1))
                if f >= 2:
                    dve.wait_ge(flo_ready, t * RAW + (f - 1))
                dve.tensor_tensor(fa[:, f % 2, :], fs[:, f % 2, :], bank[2 + f % 2][:, 0:SEQ], ALU.mult).then_inc(fa_ready, 1)
                if f:
                    ffn_lo(f - 1, t)

            def ffn_add(d, t=0):
                n = UNIT_FF + FF_T + 2 * d
                for half in range(2):
                    split_lo(dve, n + half + 2, t, RAW, UNITC if not isinstance(t, int) else None)
                dve.wait_ge(unit_done, t * RAW + (n + 2))
                at = slice(d, d + 1) if isinstance(t, int) else bass.ds(t * (RAW // 2) + d, 1)
                dve.tensor_tensor(xT[:, at, :], xT[:, at, :], bank[4 + d % 3][:, 0:SEQ].rearrange("p (a t) -> p a t", a=1), ALU.add).then_inc(xs_ready, 1)

            for L in range(LAYERS):
                norm_split(3 + 2 * L, SPLIT_OUTPUTS[3 + 2 * L], xT, SEQ)
                mixer(L)
                if L == 0:
                    norm_split(4, SPLIT_OUTPUTS[4], xT, SEQ)
                    for f in range(LEAD):
                        ffn_unit(f)
                    with dve.Fori(0, (FF_T - LEAD) // RAW) as t:
                        for j in range(RAW):
                            ffn_unit(LEAD + j, t)
                    ffn_lo(FF_T - 1)
                    for d in range(LEAD // 2):
                        ffn_add(d)
                    with dve.Fori(0, (2 * KD - LEAD) // RAW) as t:
                        for j in range(RAW // 2):
                            ffn_add(LEAD // 2 + j, t)

            norm_scale(6)
            for k in range(KD):
                normed(6, un[:, k, :], xT[:, k, :], k, SEQ, un_ready)
            dve.memset(rank[:], -1.0).then_inc(rank_zero, 1)
            steps = 0

            def step(op):
                nonlocal steps
                steps += 1
                op.then_inc(route_step, 1)
                dve.wait_ge(route_step, steps)

            dve.wait_ge(lg_done, 1)
            for tt in range(2):
                step(dve.tensor_copy(lg[:, tt, :], bank[tt][:, 0:EXPERTS]))
                step(dve.max(top[:, tt, :], lg[:, tt, :]))
                step(dve.max_index(topi[:, tt, :], top[:, tt, :], lg[:, tt, :]))
                step(dve.tensor_copy(topf[:, tt, :], topi[:, tt, :]))
            dve.tensor_tensor(tw[:, 0, :], top[:, :, 1], top[:, :, 0], ALU.subtract).then_inc(tw_diff, 1)
            for tt in range(2):
                for j in range(TOP_K):
                    step(dve.tensor_scalar(oh[:, tt, j, :], iota[:, 0:EXPERTS], topf[:, tt, j:j + 1], None, ALU.is_equal))
                dve.tensor_tensor(chosen[:, tt, :], oh[:, tt, 0, :], oh[:, tt, 1, :], ALU.add).then_inc(chosen_ready, 1)
            dve.wait_ge(chosen_ready, 2)
            step(dve.tensor_scalar(big[:], chosen[:], FAR, -FAR, ALU.mult, ALU.add))
            for i in range(4):
                dve.wait_ge(nhi_ready, i + 1)
                cols = slice((i % 2) * 512, (i % 2 + 1) * 512)
                dve.tensor_tensor(nlo[:, i // 2, cols], bank[2 + i][:], nhi[:, i // 2, cols].bitcast(F32), ALU.subtract).then_inc(nlo_ready, 1)
            dve.wait_ge(rank_done, 1)
            dve.wait_ge(rank_zero, 1)
            for tt in range(2):
                step(dve.tensor_tensor(rank[:, tt, 0:EXPERTS], bank[6][:, tt * EXPERTS:(tt + 1) * EXPERTS], big[:, tt, :], ALU.add))
                step(dve.tensor_scalar(rank[:, tt, EXPERTS:2 * EXPERTS], rank[:, tt, 0:EXPERTS], float(-P), None, ALU.add))
            def select(g):
                for tt in range(2):
                    r = rank[:, tt, g:g + 1] if isinstance(g, int) else rank[:, tt, bass.ds(g, 1)]
                    op = dve.tensor_scalar(pick[:, tt, :], iota[:], r, None, ALU.is_equal)
                op.then_inc(pick_ready, 1)

            def gathered_lo(half, g):
                dve.wait_ge(hthi_ready, g * 2 + (half + 1))
                ks = slice(4 * half, 4 * half + 4)
                dve.tensor_tensor(htlo[:, ks, :], bank[7][:].rearrange("p (k t) -> p k t", k=4), hthi[:, ks, :].bitcast(F32),
                                  ALU.subtract).then_inc(htlo_ready, 1)

            def scatter_add(r, done, count, taken, b=bank[7]):
                dve.wait_ge(done, count)
                tiles = xT[:, 2 * r:2 * r + 2, :]
                dve.tensor_tensor(tiles, tiles, b[:].rearrange("p (k t) -> p k t", k=2), ALU.add).then_inc(taken, 1)

            def expert(it):
                def rows_lo(c):
                    dve.wait_ge(athi_ready, it * CHUNKS + (c + 1))
                    dve.tensor_tensor(atlo[:], bank[4][:].rearrange("p (k t) -> p k t", k=4), athi[:].bitcast(F32),
                                      ALU.subtract).then_inc(atlo_ready, 1)

                for pos, (kind, c, part) in enumerate(EXPERT_UNITS):
                    split_lo(dve, UNIT_MOE + pos + 2, it, UM)
                    if kind == "gate" and part == 0 and 1 <= c <= 4:
                        scatter_add(c - 1, scat_done, it * 4 + c, scat_taken)
                        if c == 4:
                            for tt in range(2):
                                at = bass.ds(it, 1)
                                op = dve.tensor_scalar(gpick[:, tt, :], iota[:], rank[:, tt, at], gate[:, tt, at], ALU.is_equal, ALU.mult)
                            op.then_inc(gpick_ready, 1)
                    if part == 0:
                        continue
                    if kind == "gate" and c:
                        rows_lo(c - 1)
                    if kind == "up":
                        dve.wait_ge(silu_ready, it * CHUNKS + (c + 1))
                        dve.wait_ge(unit_done, it * UM + (UNIT_MOE + pos + 1))
                        if c >= 2:
                            dve.wait_ge(at_done, it * CHUNKS + (c - 1))
                        dve.tensor_tensor(ga[:, c % 2, :], gs[:, c % 2, :], bank[2 + c % 2][:], ALU.mult).then_inc(a_ready, 1)
                        if c == 5:
                            select(it + 1)
                        if c == CHUNKS - 1:
                            gathered_lo(0, it + 1)
                    if kind == "down" and c == CHUNKS - 2:
                        rows_lo(CHUNKS - 1)
                        gathered_lo(1, it + 1)

            select(0)
            gathered_lo(0, 0)
            gathered_lo(1, 0)
            dve.wait_ge(tw_exp, 1)
            step(dve.tensor_scalar(tw[:, 2, :], tw[:, 1, :], 1.0, None, ALU.add))
            step(dve.reciprocal(tw[:, 2, :], tw[:, 2, :]))
            step(dve.tensor_tensor(tw[:, 3, :], tw[:, 1, :], tw[:, 2, :], ALU.mult))
            for tt in range(2):
                step(dve.tensor_scalar(gate[:, tt, 0:EXPERTS], oh[:, tt, 0, :], tw[:, 2, tt:tt + 1], None, ALU.mult))
                step(dve.scalar_tensor_tensor(gate[:, tt, 0:EXPERTS], oh[:, tt, 1, :], tw[:, 3, tt:tt + 1], gate[:, tt, 0:EXPERTS], ALU.mult, ALU.add))
                step(dve.tensor_copy(gate[:, tt, EXPERTS:], gate[:, tt, 0:EXPERTS]))
            step(dve.tensor_reduce(cnt[:], bank[6][:, 2 * EXPERTS:3 * EXPERTS], AXX, ALU.max))
            dve.tensor_copy(cnti[:], cnt[:]).then_inc(count_ready, 1)
            with dve.Fori(0, EXPERTS) as it:
                expert(it)
            dve.wait_ge(count_ready, 1)
            fullest = dve.value_load(cnti[0:1, 0:1], min_val=0, max_val=SEQ)
            with dve.If(fullest > P):
                with dve.Fori(EXPERTS, 2 * EXPERTS) as it:
                    expert(it)
            for r in range(4):
                scatter_add(r, last_done, r + 1, last_taken, bank[r])
            norm_scale(7)
            for k in range(KD):
                normed(7, un[:, k, :], xT[:, k, :], k, SEQ, result_ready)

        @block.gpsimd
        def _(pool):
            def scaled(out, src, by):
                if out.shape[0] < P:
                    return pool.tensor_tensor(out, src, by.to_broadcast(out.shape), ALU.mult)
                return pool.tensor_scalar(out, src, by, None, ALU.mult)

            pool.wait_ge(par_landed, 16 * N_PAR)
            with pool.Fori(0, LAYERS) as l:
                for r in range(ROPED):
                    pool.wait_ge(proj_taken, l * PROJ_T + (QK_T + r + 1))
                    if r >= 2:
                        pool.wait_ge(roped, l * ROPED + (r - 1))
                    pool.tensor_tensor(rc[:, r % 2, :], qraw[:, r % 2, :], rope[:, 2 * (r // 4), :], ALU.mult).then_inc(rc_ready, 1)
                for p in range(DIFF_HEADS):
                    pool.wait_ge(rlam_ready, l * DIFF_HEADS + (p + 1))
                    if p:
                        pool.wait_ge(diff_p, l * DIFF_HEADS + p)
                    m = 2 * p + 1
                    for t, (q0, rows, c0, keys) in enumerate(QTILES):
                        op = scaled(pd[0:rows, c0:c0 + keys], ex[0:rows, m % 4, c0:c0 + keys], rlam[0:rows, p % 2, t:t + 1])
                    op.then_inc(pd_ready, 1)
                for f in range(FOX_HEADS):
                    m, p = 2 * DIFF_HEADS + f, DIFF_HEADS + f
                    pool.wait_ge(rsum_ready, l * MAPS + (m + 1))
                    pool.wait_ge(t_done, l * HEADS + (p - 1))
                    for t, (q0, rows, c0, keys) in enumerate(QTILES):
                        op = scaled(pr[0:rows, p % 2, c0:c0 + keys], ex[0:rows, m % 4, c0:c0 + keys], rsum[0:rows, m % 4, t:t + 1])
                    op.then_inc(fox_p, 1)

            pool.wait_ge(xs_ready, KD)
            params = ((convw, "convw"), (convp, "convp"), (pools, "pools"), (poolr, "poolr"), (poolw, "poolw"), (gmg, "gmg"), (gmb, "gmb"),
                      (wsT, "wsT"), (router, "router"), (lt, "lt"), (iota, "iota"))
            for dst, name in params:
                pool.dma_start(dst[:], io[name]).then_inc(par2_landed, 16)

            def zero_pads():
                pool.memset(hpad[:, :, 0:PADC], 0.0).then_inc(const2_ready, 1)
                pool.memset(pc[:, :, 0:PADP], 0.0).then_inc(const2_ready, 1)

            zero_pads()
            pool.wait_ge(par2_landed, 16 * PAR2)
            pool.wait_ge(const2_ready, 2)
            pool.memset(wsT[GM_CHUNK:P, :, :, 0:GM_CHUNK], 0.0).then_inc(const2_ready, 1)
            def pooled(L):
                for c in range(POOL_T):
                    pool.wait_ge(scan_ready, POOL_T * L + c + 1)
                    if L:
                        pool.wait_ge(pool_done, L)
                    if c:
                        pool.wait_ge(pool_ready, POOL_T * L + c)
                    for g in (2 * c, 2 * c + 1):
                        part, win = slice(64 * (g % 2), 64 * (g % 2) + 64), POOL_WINDOWS[g]
                        pool.tensor_tensor(py[part, c, :], pc[part, c, PADP:PADP + SEQ], pc[part, c, PADP - win:PADP - win + SEQ],
                                           ALU.subtract).then_inc(pool_step, 1)
                    pool.wait_ge(pool_step, 3 * POOL_T * L + 3 * c + 2)
                    pool.tensor_tensor(py[:, c, :], py[:, c, :], poolr[:, c, :], ALU.mult).then_inc(pool_step, 1)
                    pool.wait_ge(pool_step, 3 * POOL_T * L + 3 * c + 3)
                    pool.tensor_tensor(py[:, c, :], py[:, c, :], pa[:, c, :], ALU.subtract).then_inc(pool_ready, 1)

            for L in range(LAYERS):
                if L:
                    pool.wait_ge(xs_ready, XS_MIX)
                    zero_pads()
                for k in range(1, TAPS):
                    if k > 1:
                        pool.wait_ge(sum0_done, L * (TAPS - 1) + k - 1)
                    pool.wait_ge(prod_ready, L * TAPS + k + 1)
                    pool.tensor_tensor(cacc[:, 0, :], cacc[:, 0, :], prod[k % 3], ALU.add).then_inc(sum0_done, 1)
                    if k == POOL_TAP:
                        pool.wait_ge(sum0_done, L * (TAPS - 1) + k)
                        pooled(L)

    return nc


def columns(w, c0, c1):
    return w[:, c0:c1].reshape(-1, P, c1 - c0).transpose(1, 0, 2)


def lay_out(a):
    f32 = np.float32
    io = {"hT": np.concatenate([a["meta_tokens"], a["x"][0]]).T.reshape(KD, P, LEN).transpose(1, 0, 2)}

    w = np.zeros((UNIT_MOE, P, UNITC), f32)

    def put(n, part, at=0):
        flat = part.reshape(part.shape[0], -1)
        w[n, :part.shape[0], at:at + flat.shape[1]] = flat

    half = MIXW // 2
    dq, dk, dv, dz, fq, fk, fv, fz, fl = (half * i for i in range(9))
    order = [dz, fz, fl, dq, dk, fq, fk, dv, fv]
    tiles = [s + P * i for s in order for i in range(1 if s == fl else 4)]
    for l in range(LAYERS):
        w_in = np.pad(a["w_in"][l], ((0, 0), (0, fl + P - a["w_in"].shape[2])))
        i = 0
        for u in range(U1):
            if u < PROJ_U:
                starts = tiles[i:i + U1_TILES[u]]
                i += U1_TILES[u]
                put(l * U1 + u, np.concatenate([columns(w_in, s, s + P) for s in starts], axis=2))
        d = 0
        for u in range(PROJ_U, U1):
            put(l * U1 + u, columns(a["w_out"][l], d * P, (d + U1_TILES[u]) * P))
            d += U1_TILES[u]
        n = UNIT_MIX[l]
        win2, wout2 = a["w_in_2"][l], a["w_out_2"][l]
        pool_w, gm_w, conv_w = POOL_T * P, GM_HEADS * GM_DIM, CONV_T * P
        at_a, at_u, at_v = 0, pool_w, pool_w + gm_w
        at_cv, at_cg = at_v + gm_w, at_v + gm_w + conv_w
        for c in range(CONV_T):
            put(n + c, np.concatenate([columns(win2, s + c * P, s + (c + 1) * P) for s in (at_cv, at_cg)], axis=2))
        put(n + POOL_U, columns(win2, at_a, at_a + pool_w))
        for s in range(2):
            put(n + GU_U + s, columns(win2, at_u + s * gm_w // 2, at_u + (s + 1) * gm_w // 2))
            put(n + V_U + s, columns(win2[s * D // 2:(s + 1) * D // 2], at_v, at_v + gm_w))
        put(n + PW_U, columns(a["conv_pw_w_2"][l], 0, conv_w))
        rows = [(i * P, P) for i in range(POOL_T)] + [(pool_w + i * GM_DIM, GM_DIM) for i in range(GM_HEADS)]
        rows += [(pool_w + gm_w + i * P, P) for i in range(CONV_T)]
        for dd in range(KD):
            for i, (r0, nr) in enumerate(rows):
                early = i < GM_T
                u, at = (EARLY_U + dd // 2, (dd % 2) * GM_T + i) if early else (LATE_U + dd // 4, (dd % 4) * CONV_T + i - GM_T)
                put(n + u, wout2[r0:r0 + nr, dd * P:(dd + 1) * P], at * P)
    for f in range(FF_T):
        put(UNIT_FF + f, np.concatenate([columns(a[name][0], f * P, (f + 1) * P) for name in ("ffn_wg_2", "ffn_wu_2")], axis=2))
    for i in range(2 * KD):
        d, h = divmod(i, 2)
        put(UNIT_FF + FF_T + i, columns(a["ffn_wd_2"][0][h * FF_HALF * P:(h + 1) * FF_HALF * P], d * P, (d + 1) * P))
    io["w"] = w

    wm = np.empty((EXPERTS, UM, P, UNITC), f32)
    for j, (kind, c, part) in enumerate(EXPERT_UNITS):
        if kind == "down":
            r0 = c * CHUNK + part * 2 * P
            block = a["moe_wd_2"][0][:, r0:r0 + 2 * P, :].reshape(EXPERTS, 2, P, D)
        else:
            m = a["moe_wg_2" if kind == "gate" else "moe_wu_2"][0]
            block = m[:, part * 512:(part + 1) * 512, c * CHUNK:(c + 1) * CHUNK].reshape(EXPERTS, 4, P, CHUNK)
        wm[:, j] = block.transpose(0, 2, 1, 3).reshape(EXPERTS, P, UNITC)
    io["wm"] = wm

    def per_feature(v):
        return np.moveaxis(v.reshape(v.shape[:-1] + (-1, P)), -1, 0)

    gains = [a["norm_g"][0], a["norm_g"][1], a["final_g"], a["norm1_g_2"][0], a["norm2_g_2"][0], a["norm1_g_2"][1], a["norm2_g_2"][1], a["final_g_2"]]
    io["gains"] = per_feature(np.stack(gains))

    inv = ROPE_THETA ** (-np.arange(HEAD // 2, dtype=f32) / f32(HEAD // 2))
    ang = np.arange(LEN, dtype=f32)[None, :] * inv.astype(f32)[:, None]
    cos, sin = np.cos(ang), np.sin(ang)
    cos, sin = np.tile(cos, (4, 1)), np.tile(np.concatenate([-sin, sin]), (2, 1))
    io["rope"] = np.stack([cos * -SCALE, sin * -SCALE, cos, sin], axis=1).astype(f32)
    partner = np.arange(P) ^ (HEAD // 2)
    io["rot"] = np.eye(P, dtype=f32)[partner]
    io["mask"] = np.where(np.arange(LEN)[None, :] <= META + P + np.arange(P)[:, None], 0.0, NEG).astype(f32)
    io["ident"] = np.eye(P, dtype=f32)
    io["bforget"] = a["b_forget"].T
    io["subln"] = per_feature(a["subln_g"])
    lams = np.stack([a["lam_q1"], a["lam_k1"], a["lam_q2"], a["lam_k2"]], axis=1)
    io["lamv"] = np.broadcast_to(lams, (P,) + lams.shape)

    io["wsT"] = a["gm_ws_2"].transpose(3, 0, 1, 2)
    gmb = np.tile(a["gm_b_2"], (1, 1, SEQ // P))
    io["gmb"] = np.broadcast_to(gmb, (P,) + gmb.shape)
    io["gmg"] = np.broadcast_to(a["gm_norm_g_2"], (P,) + a["gm_norm_g_2"].shape)
    io["poolw"] = a["pool_w_2"].reshape(LAYERS, POOL_T, 2, 64, 64).transpose(2, 3, 0, 1, 4).reshape(P, LAYERS, POOL_T, 64)
    io["pools"] = per_feature(a["pool_scale_2"])
    t = np.arange(1, SEQ + 1, dtype=f32)
    recip = np.stack([f32(1) / np.minimum(t, f32(win)) for win in POOL_WINDOWS])
    io["poolr"] = np.repeat(recip.reshape(POOL_T, 2, SEQ).transpose(1, 0, 2), 64, axis=0)
    io["convw"] = a["conv_dw_w_2"].reshape(LAYERS, TAPS, CONV_T, P).transpose(3, 0, 2, 1)
    convp = np.stack([a[name] for name in ("conv_dw_b_2", "conv_ln_g_2", "conv_ln_b_2", "conv_pw_b_2")], axis=1)
    io["convp"] = per_feature(convp)
    io["router"] = columns(a["moe_router_2"][0], 0, EXPERTS)
    io["lt"] = np.triu(np.ones((P, P), f32), 1)
    io["iota"] = np.broadcast_to(np.arange(P, dtype=f32), (P, P))
    return {"in_" + name: np.ascontiguousarray(v, dtype=f32) for name, v in io.items()}


def declare(nc, arrays):
    io = {name.removeprefix("in_"): nc.dram_tensor(name, v.shape, F32, kind="ExternalInput").ap() for name, v in arrays.items()}
    io["out"] = nc.dram_tensor("out", (1, SEQ, D), F32, kind="ExternalOutput").ap()
    return io


def kernel(**inputs):
    import concourse.bacc as bacc
    from concourse.bass_utils import run_bass_kernel_spmd

    arrays = lay_out({name: np.asarray(v) for name, v in inputs.items()})
    nc = bacc.Bacc("TRN2", target_bir_lowering=False, num_devices=1)
    build_program(nc, declare(nc, arrays))
    return run_bass_kernel_spmd(nc, [arrays], core_ids=[0]).results[0]["out"]
```
